# Optimizing a Trainium2 kernel written in Bass

```python
import jax, jax.numpy as jnp
from jax import lax
import numpy as np

D_MODEL = 1024
BATCH = 1
SEQ = 512
DEPTH = 2

CHUNK = 64
N_A_LAYERS = DEPTH // 2
N_B_LAYERS = DEPTH - N_A_LAYERS
EPS = 1e-6
SGU_BLOCK = 128
SGU_WIDTH = 2 * D_MODEL
SGU_GROUPS = 8
SGU_GROUP_DIM = SGU_WIDTH // SGU_GROUPS
N_HEADS = 16
HEAD_DIM = D_MODEL // N_HEADS
Q_BLOCK = 128
N_GROUPS = 4
EXPERTS_PER_GROUP = 8
N_EXPERTS = N_GROUPS * EXPERTS_PER_GROUP
TOP_K = 2
D_EXPERT = D_MODEL // 2
EXPERT_BLOCK = 128

kernel_name = "yoco_gmlp_fox_hmoe_trunk"

def rmsnorm(x, g):
    xf = x.astype(jnp.float32)
    y = xf * lax.rsqrt(jnp.mean(xf * xf, axis=-1, keepdims=True) + EPS)
    return (y * g.astype(jnp.float32)).astype(x.dtype)

def sgu_mixer(h, w_in, b_in, v_norm, w_s, b_s, w_out):
    B, S, _ = h.shape
    z = jax.nn.gelu(h @ w_in + b_in)
    u, v = jnp.split(z, 2, axis=-1)
    v = rmsnorm(v, v_norm)
    nb = S // SGU_BLOCK
    v = v.reshape(B, nb, SGU_BLOCK, SGU_GROUPS, SGU_GROUP_DIM)
    chunk_id = jnp.arange(SGU_BLOCK) // CHUNK
    mask = chunk_id[:, None] >= chunk_id[None, :]
    w_sm = jnp.where(mask[None], w_s, jnp.zeros_like(w_s))
    v = jnp.einsum('gts,bnsgc->bntgc', w_sm, v) + b_s.T[None, None, :, :, None]
    gated = u * v.reshape(B, S, SGU_WIDTH)
    return gated @ w_out

def shared_kv(x_kv, kv_norm, kv_w, kv_b_f, k_norm):
    B, S, _ = x_kv.shape
    h = rmsnorm(x_kv, kv_norm)
    kvf = h @ kv_w
    k, v, f = jnp.split(kvf, [D_MODEL, 2 * D_MODEL], axis=-1)
    k = rmsnorm(k.reshape(B, S, N_HEADS, HEAD_DIM), k_norm)
    v = v.reshape(B, S, N_HEADS, HEAD_DIM)
    log_f = jax.nn.log_sigmoid((f + kv_b_f).astype(jnp.float32))
    cum = jnp.cumsum(log_f, axis=1).transpose(0, 2, 1)
    return k, v, cum

def forgetting_attention(h, k, v, cum, w_qg, q_norm, w_out):
    B, S, _ = h.shape
    q, gate = jnp.split(h @ w_qg, 2, axis=-1)
    q = rmsnorm(q.reshape(B, S, N_HEADS, HEAD_DIM), q_norm)
    scale = HEAD_DIM ** -0.5
    outs = []
    for i in range(S // Q_BLOCK):
        q0, q1 = i * Q_BLOCK, (i + 1) * Q_BLOCK
        kb, vb = k[:, :q1], v[:, :q1]
        s = jnp.einsum('bqhd,bkhd->bhqk', q[:, q0:q1], kb).astype(jnp.float32) * scale
        decay = cum[:, :, q0:q1, None] - cum[:, :, None, :q1]
        mask = (q0 + jnp.arange(Q_BLOCK))[:, None] >= jnp.arange(q1)[None, :]
        s = jnp.where(mask, s + decay, -jnp.inf)
        p = jax.nn.softmax(s, axis=-1)
        outs.append(jnp.einsum('bhqk,bkhd->bqhd', p.astype(vb.dtype), vb))
    o = jnp.concatenate(outs, axis=1).reshape(B, S, D_MODEL)
    return (o * jax.nn.sigmoid(gate)) @ w_out

def hierarchical_moe(h, w_group, b_group, w_expert, b_expert, w1, w3, w2):
    B, S, D = h.shape
    T = B * S
    xf = h.reshape(T, D)
    tok = jnp.arange(T)
    g_logits = (xf @ w_group + b_group).astype(jnp.float32)
    g_prob = jax.nn.softmax(g_logits, axis=-1)
    g_sel = jnp.argmax(g_logits, axis=-1).astype(jnp.int32)
    g_w = g_prob[tok, g_sel][:, None]
    e_logits = (xf @ w_expert + b_expert).astype(jnp.float32)
    e_logits = e_logits.reshape(T, N_GROUPS, EXPERTS_PER_GROUP)[tok, g_sel]
    e_prob = jax.nn.softmax(e_logits, axis=-1)
    top_p, top_i = lax.top_k(e_prob, TOP_K)
    top_p = top_p / jnp.sum(top_p, axis=-1, keepdims=True)
    weights = g_w * top_p
    expert_id = g_sel[:, None] * EXPERTS_PER_GROUP + top_i.astype(jnp.int32)
    A = T * TOP_K
    flat_e = expert_id.reshape(A)
    flat_tok = jnp.arange(A, dtype=jnp.int32) // TOP_K
    flat_w = weights.reshape(A)
    order = jnp.argsort(flat_e)
    sorted_e = flat_e[order]
    counts = jnp.zeros((N_EXPERTS,), jnp.int32).at[flat_e].add(1)
    padded = (counts + EXPERT_BLOCK - 1) // EXPERT_BLOCK * EXPERT_BLOCK
    start = jnp.cumsum(counts) - counts
    pend = jnp.cumsum(padded)
    pstart = pend - padded
    dest = pstart[sorted_e] + (jnp.arange(A, dtype=jnp.int32) - start[sorted_e])
    n_blocks = -(-A // EXPERT_BLOCK) + N_EXPERTS
    n_rows = n_blocks * EXPERT_BLOCK
    tok_buf = jnp.full((n_rows,), T, jnp.int32).at[dest].set(flat_tok[order])
    w_buf = jnp.zeros((n_rows,), jnp.float32).at[dest].set(flat_w[order])
    block_start = jnp.arange(n_blocks, dtype=jnp.int32) * EXPERT_BLOCK
    block_e = jnp.minimum(jnp.searchsorted(pend, block_start, side='right'),
                          N_EXPERTS - 1).astype(jnp.int32)
    x_pad = jnp.concatenate([xf, jnp.zeros((1, D), xf.dtype)], axis=0)
    xs = x_pad[tok_buf].reshape(n_blocks, EXPERT_BLOCK, D)

    def expert_block(args):
        xb, e = args
        hid = jax.nn.silu(xb @ w1[e]) * (xb @ w3[e])
        return hid @ w2[e]

    ys = lax.map(expert_block, (xs, block_e)).reshape(n_rows, D)
    ys = ys * w_buf[:, None].astype(ys.dtype)
    out = jnp.zeros((T + 1, D), ys.dtype).at[tok_buf].add(ys)[:T]
    return out.reshape(B, S, D)

def setup_inputs(seed: int = 0) -> dict:
    key = jax.random.key(seed)
    ks = jax.random.split(key, 32)

    def nrm(k, shape, scale):
        return jax.random.normal(k, shape, jnp.float32) * scale

    def gain(k, shape):
        return 1.0 + 0.02 * jax.random.normal(k, shape, jnp.float32)

    NA, NB, L = N_A_LAYERS, N_B_LAYERS, DEPTH
    return {
        "x": nrm(ks[0], (BATCH, SEQ, D_MODEL), 1.0),
        "a_norm": gain(ks[1], (NA, D_MODEL)),
        "a_w_in": nrm(ks[2], (NA, D_MODEL, 2 * SGU_WIDTH), D_MODEL ** -0.5),
        "a_b_in": nrm(ks[3], (NA, 2 * SGU_WIDTH), 0.01),
        "a_v_norm": gain(ks[4], (NA, SGU_WIDTH)),
        "a_w_s": nrm(ks[5], (NA, SGU_GROUPS, SGU_BLOCK, SGU_BLOCK), SGU_BLOCK ** -0.5),
        "a_b_s": gain(ks[6], (NA, SGU_GROUPS, SGU_BLOCK)),
        "a_w_out": nrm(ks[7], (NA, SGU_WIDTH, D_MODEL), SGU_WIDTH ** -0.5),
        "kv_norm": gain(ks[8], (D_MODEL,)),
        "kv_w": nrm(ks[9], (D_MODEL, 2 * D_MODEL + N_HEADS), D_MODEL ** -0.5),
        "kv_b_f": nrm(ks[10], (N_HEADS,), 0.01),
        "k_norm": gain(ks[11], (HEAD_DIM,)),
        "b_norm": gain(ks[12], (NB, D_MODEL)),
        "b_w_qg": nrm(ks[13], (NB, D_MODEL, 2 * D_MODEL), D_MODEL ** -0.5),
        "q_norm": gain(ks[14], (NB, HEAD_DIM)),
        "b_w_out": nrm(ks[15], (NB, D_MODEL, D_MODEL), D_MODEL ** -0.5),
        "m_norm": gain(ks[16], (L, D_MODEL)),
        "m_w_group": nrm(ks[17], (L, D_MODEL, N_GROUPS), D_MODEL ** -0.5),
        "m_b_group": nrm(ks[18], (L, N_GROUPS), 0.01),
        "m_w_expert": nrm(ks[19], (L, D_MODEL, N_EXPERTS), D_MODEL ** -0.5),
        "m_b_expert": nrm(ks[20], (L, N_EXPERTS), 0.01),
        "m_w1": nrm(ks[21], (L, N_EXPERTS, D_MODEL, D_EXPERT), D_MODEL ** -0.5),
        "m_w3": nrm(ks[22], (L, N_EXPERTS, D_MODEL, D_EXPERT), D_MODEL ** -0.5),
        "m_w2": nrm(ks[23], (L, N_EXPERTS, D_EXPERT, D_MODEL), D_EXPERT ** -0.5),
    }

def reference(x, a_norm, a_w_in, a_b_in, a_v_norm, a_w_s, a_b_s, a_w_out,
              kv_norm, kv_w, kv_b_f, k_norm,
              b_norm, b_w_qg, q_norm, b_w_out,
              m_norm, m_w_group, m_b_group, m_w_expert, m_b_expert, m_w1, m_w3, m_w2):
    k = v = cum = None
    for layer in range(DEPTH):
        if layer < N_A_LAYERS:
            i = layer
            x = x + sgu_mixer(rmsnorm(x, a_norm[i]), a_w_in[i], a_b_in[i], a_v_norm[i],
                              a_w_s[i], a_b_s[i], a_w_out[i])
        else:
            if layer == N_A_LAYERS:
                k, v, cum = shared_kv(x, kv_norm, kv_w, kv_b_f, k_norm)
            j = layer - N_A_LAYERS
            x = x + forgetting_attention(rmsnorm(x, b_norm[j]), k, v, cum,
                                         b_w_qg[j], q_norm[j], b_w_out[j])
        x = x + hierarchical_moe(rmsnorm(x, m_norm[layer]), m_w_group[layer], m_b_group[layer],
                                 m_w_expert[layer], m_b_expert[layer],
                                 m_w1[layer], m_w3[layer], m_w2[layer])
    return x


_drawn_inputs = setup_inputs


def setup_inputs(seed=0):
    import zlib

    import numpy as np

    out = dict(_drawn_inputs(seed))
    spreads = {}
    factors = {'a_b_in': 2.969,
     'kv_norm': 3.213,
     'kv_b_f': 8.0,
     'k_norm': 8.0,
     'b_norm': 4.08,
     'q_norm': 5.244,
     'm_b_group': 3.181,
     'm_b_expert': 3.165}
    for name, (base, spread) in spreads.items():
        noise = np.random.default_rng([zlib.crc32(name.encode()), seed]).standard_normal(out[name].shape)
        drawn = base * np.exp(spread * noise) if base else spread * noise
        out[name] = __import__('jax').numpy.asarray(drawn.astype(out[name].dtype))
    for name, factor in factors.items():
        out[name] = (out[name] * factor).astype(out[name].dtype)
    return out
```

```python
from contextlib import ExitStack

import concourse.bass as bass
from concourse import mybir

F32 = mybir.dt.float32
I32 = mybir.dt.int32
BF16 = mybir.dt.bfloat16
ALU = mybir.AluOpType
ACT = mybir.ActivationFunctionType
AX = mybir.AxisListType.X

P = 128
D = 1024
T = 512
NT = T // P
KD = D // P
EPS = 1e-6
WIDTH = 2 * D
NC = WIDTH // P
SG = 8
HEADS = 16
PAIRS = HEADS // 2
DH = D // HEADS
NG = 4
EPG = 8
NE = NG * EPG
DE = D // 2
KE = DE // P
NR = NG + NE
CAP = 64
SLOTS = 2 * T
MAX_ITEMS = SLOTS // CAP + NE
NBASE = MAX_ITEMS + 2
NBUF = 3
COL = 512
BIG = 1e30


def trunk(nc, x_in, a_norm, a_w_in, a_b_in, a_v_norm, a_w_s, a_b_s, a_w_out, kv_norm, kv_w, kv_b_f, k_norm,
          b_norm, b_w_qg, q_norm, b_w_out, m_norm, m_w_group, m_b_group, m_w_expert, m_b_expert,
          m_w1, m_w3, m_w2, out):
    with ExitStack() as ctx:
        def sb(name, shape, dt=F32):
            return ctx.enter_context(nc.sbuf_tensor(name, shape, dt))

        def sem(name):
            return ctx.enter_context(nc.semaphore(name))

        def sems(name, n):
            return [sem(f"{name}{i}") for i in range(n)]

        y_rows = [nc.dram_tensor(f"y_rows{l}", (SLOTS + CAP, D), F32, kind="Internal").ap() for l in range(2)]
        ncum_rows = nc.dram_tensor("ncum_rows", (HEADS, T), F32, kind="Internal").ap()

        X = sb("X", [P, NT, D])
        H = sb("H", [P, NT * D])
        EB = [sb(f"EB{s}", [P, 3 * KD * COL]) for s in range(NBUF)]
        SCR = sb("SCR", [P, 5 * D])
        gain = sb("gain", [P, D])

        h_tok = H[:, :].rearrange("p (t k q) -> p t k q", t=NT, k=KD)
        hT = H[:, :].rearrange("p (k n) -> p k n", k=KD)
        TILE = KD * COL
        w1_sb = [EB[s][:, 0:TILE].rearrange("p (k n) -> p k n", k=KD) for s in range(NBUF)]
        w3_sb = [EB[s][:, TILE:2 * TILE].rearrange("p (k n) -> p k n", k=KD) for s in range(NBUF)]
        w2_sb = [EB[s][:, 2 * TILE:3 * TILE].rearrange("p (k n) -> p k n", k=KE) for s in range(NBUF)]
        ring = [EB[1][:, s * TILE:(s + 1) * TILE].rearrange("p (k n) -> p k n", k=KD) for s in range(2)]
        spare = EB[1][:, 2 * TILE:3 * TILE]
        ws_raw = spare[:, 0:D].rearrange("p (g s) -> p g s", g=SG)
        wsT = spare[:, D:2 * D].rearrange("p (g s) -> p g s", g=SG)
        bs_bc = spare[:, 2 * D:3 * D].rearrange("p (g s) -> p g s", g=SG)
        vg = EB[2][:, 0:2 * TILE].rearrange("p (t n) -> p t n", t=NT)
        wsTs = EB[2][:, 2 * TILE:3 * TILE].rearrange("p (t g s) -> p t g s", t=NT, g=SG)
        KT = EB[2][:, 0:TILE].rearrange("p (c n) -> p c n", c=PAIRS)
        QT = EB[2][:, TILE:2 * TILE].rearrange("p (c n) -> p c n", c=PAIRS)
        V = EB[2][:, 2 * TILE:3 * TILE].rearrange("p (t n) -> p t n", t=NT)
        GT = spare.rearrange("p (c n) -> p c n", c=PAIRS)
        y_got = EB[2][:, 0:2 * TILE].rearrange("p (i n) -> p i n", i=2 * NT)

        PT = EB[0][:, 2 * TILE:3 * TILE].rearrange("p (h b n) -> p h b n", h=2, b=NT)

        def scr(a, b):
            return SCR[:, a:b]

        hrow = [scr(s * D, (s + 1) * D).rearrange("p (k q) -> p k q", k=KD) for s in range(2)]
        junk = scr(4 * D, 5 * D)
        b_v = [scr(2 * D + s * COL, 2 * D + (s + 1) * COL) for s in range(2)]
        u_tmp = [scr(3 * D + s * COL, 3 * D + (s + 1) * COL) for s in range(2)]
        kn = [scr(2 * D + s * COL, 2 * D + (s + 1) * COL) for s in range(2)]
        sq = [scr(3 * D + s * COL, 3 * D + (s + 1) * COL) for s in range(2)]
        Pr = scr(0, 6 * COL).rearrange("p (b h n) -> p b h n", b=3, h=2)
        nck = scr(6 * COL, 10 * COL).rearrange("p (b h n) -> p b h n", b=2, h=2)
        hTc = [scr(s * D, (s + 1) * D).rearrange("p (k q) -> p k q", k=KD) for s in range(2)]
        xg = scr(0, COL)
        xT = scr(COL, 2 * COL).rearrange("p (k c) -> p k c", k=KD)
        hid = scr(2 * COL, 3 * COL)
        silu = scr(3 * COL, 4 * COL)
        ysb = scr(4 * COL, 5 * COL)
        eqs = scr(5 * COL, 6 * COL).rearrange("p (k c j) -> p k c j", k=2, c=NT)
        hidT = scr(6 * COL, 6 * COL + 256).rearrange("p (k c) -> p k c", k=KE)
        S = scr(6 * COL + 256, 7 * COL).rearrange("p (c j) -> p c j", c=NT)
        at = [7 * COL]

        def route(n):
            at[0] += n
            assert at[0] <= 5 * D
            return scr(at[0] - n, at[0])

        lg = route(NT * NR).rearrange("p (t n) -> p t n", t=NT)
        el = route(NT * NE).rearrange("p (t n) -> p t n", t=NT)
        oh = [route(NT * NE).rearrange("p (t n) -> p t n", t=NT) for _ in range(2)]
        cand = route(NT * NE).rearrange("p (t n) -> p t n", t=NT)
        msum = route(NT * NE).rearrange("p (t n) -> p t n", t=NT)
        ohg = route(NT * NG).rearrange("p (t n) -> p t n", t=NT)
        pen = route(NT * NG).rearrange("p (t n) -> p t n", t=NT)
        cntb = route(P)
        item_tmp = route(3 * NBASE).rearrange("p (a n) -> p a n", a=3)
        cmp7 = route(8)

        col = sb("col", [P, 64])
        gmax, gmin, gsum, m1, m2, mmin, dexp = (col[:, 4 * i:4 * i + 4] for i in range(7))
        cn = col[:, 28:30]
        s0n0 = col[:, 30:32]
        pb = col[:, 32:40]
        gw = col[:, 40:44]
        w12 = sb("w12", [P, 8])
        pos = sb("pos", [P, 8])
        pos_i = sb("pos_i", [P, 8], I32)
        base_f = sb("base_f", [P, NBASE])
        base_i = sb("base_i", [1, NBASE + 2], I32)
        n0_i = sb("n0_i", [1, NE + 2], I32)
        ss = sb("ss", [P, NT])
        rms = sb("rms", [P, NT])
        rinv = sb("rinv", [P, NT])
        vss = sb("vss", [P, NT, 4])
        hss = sb("hss", [P, 2, 8])
        hr = sb("hr", [P, 2, 8])
        nmx = sb("nmx", [P, 3, 2])
        rsum = sb("rsum", [P, 3, 2])
        rrec = sb("rrec", [P, 3, 2])
        eps = sb("eps", [P, 1])
        cols_raw = sb("cols_raw", [2 * NC + 2, P])
        cols = sb("cols", [P, 2 * NC + 2])
        b_u, v_gain, kq_gain = cols[:, 0:NC], cols[:, NC:2 * NC], cols[:, 2 * NC:2 * NC + 2]
        wf = sb("wf", [P, KD, HEADS])
        bf_bc = sb("bf_bc", [P, HEADS])
        lf = sb("lf", [P, 3, NT * HEADS])
        wr = sb("wr", [P, KD, NR])
        br = sb("br", [P, NR])
        ident = sb("ident", [P, P])
        tri = sb("tri", [P, P])
        tri_in = sb("tri_in", [P, P])
        ones = sb("ones", [P, P])
        ident_b = sb("ident_b", [P, P], BF16)
        mask_b = sb("mask_b", [P, P], BF16)
        iota_m = sb("iota_m", [P, NE])
        iota_c = sb("iota_c", [P, CAP])
        thr7 = sb("thr7", [P, 8])

        ps = [ctx.enter_context(nc.psum_tensor(f"ps{i}", [P, COL], F32)) for i in range(8)]

        const_made = sem("const_made")
        const_ready = sem("const_ready")
        x_loaded = sems("x_loaded", NT)
        small_loaded = sem("small_loaded")
        col_loaded = sem("col_loaded")
        bv_loaded = sems("bv_loaded", 2)
        tile_loaded = sems("tile_loaded", 2)
        acc_ready = sem("acc_ready")
        dve_step = sem("dve_step")
        act_step = sem("act_step")
        norm = {}
        for n in ("a", "m0", "kv", "b", "m1"):
            norm[n] = {k: sem(f"{n}_{k}") for k in ("gain", "rms", "hrow", "tr", "ht")}
        z_ready = sem("z_ready")
        v_ready = sem("v_ready")
        vr_ready = sem("vr_ready")
        wst_done = sem("wst_done")
        wst_ready = sem("wst_ready")
        wsts_ready = sem("wsts_ready")
        mix_done = sems("mix_done", 2)
        mix_free = sems("mix_free", 2)
        u_ready = sem("u_ready")
        gated = sem("gated")
        out_done = sem("out_done")
        x_mixed = sem("x_mixed")
        moe = []
        for l in range(2):
            moe.append({k: sem(f"moe{l}_{k}") for k in (
                "router_loaded", "logits", "route_exp_in", "route_exp", "lists_in", "lists_out", "tables", "sel", "up", "silu", "hid", "gath", "xg", "hidT_tr", "hidT",
                "xT_tr", "xT", "down", "y_out", "y_stored", "y_complete", "combined", "step")})
            moe[l]["w13"] = sems(f"moe{l}_w13_", NBUF)
            moe[l]["w2"] = sems(f"moe{l}_w2_", NBUF)
            moe[l]["y_got"] = sems(f"moe{l}_y_got", NT)
        v_out = sem("v_out")
        g_done = sem("g_done")
        g_out = sem("g_out")
        sq_ready = sem("sq_ready")
        hss_ready = sem("hss_ready")
        hrms_ready = sem("hrms_ready")
        kn_ready = sem("kn_ready")
        kn_tr = sem("kn_tr")
        kn_out = sem("kn_out")
        f_done = sem("f_done")
        f_ready = sem("f_ready")
        f_ln = sem("f_ln")
        lf_ready = sem("lf_ready")
        cum_done = sem("cum_done")
        cum_ready = sem("cum_ready")
        cumT_done = sem("cumT_done")
        ncum_ready = sem("ncum_ready")
        ncum_stored = sem("ncum_stored")
        nck_loaded = sems("nck_loaded", 2)
        s_done = sem("s_done")
        s_max = sem("s_max")
        p_exp = sem("p_exp")
        p_ready = sem("p_ready")
        pt_tr = sem("pt_tr")
        pt_out = sems("pt_out", 2)
        o_done = sem("o_done")
        o_gated = sem("o_gated")
        x_attn = sem("x_attn")
        stored = sem("stored")

        def rows_pk(w, c0):
            return w.rearrange("(p k) n -> p k n", k=KD)[:, :, c0:c0 + COL]

        def rows_cp(w, c, c0):
            return w[c * KD * P:(c + 1) * KD * P, c0:c0 + COL].rearrange("(k p) n -> p k n", p=P)

        tiles = [rows_pk(a_w_in[0], WIDTH + COL * i) for i in range(4)]
        tiles += [rows_pk(a_w_in[0], COL * i) for i in range(4)]
        tiles += [rows_cp(a_w_out[0], c, COL * n) for n in range(2) for c in range(2)]
        tiles += [rows_pk(kv_w, COL * i) for i in range(4)]
        tiles += [rows_pk(b_w_qg[0], COL * i) for i in range(4)]
        tiles += [rows_cp(b_w_out[0], 0, COL * n) for n in range(2)]
        T_V, T_U, T_O, T_K, T_VV, T_Q, T_G, T_WO = 0, 4, 8, 12, 14, 16, 18, 20
        G_V, G_U, G_K, G_VV, G_Q, G_WO = 0, 16, 32, 40, 48, 56

        block = ctx.enter_context(nc.Block())

        @block.sync
        def _(sp):
            def load_tile(i):
                if i >= 2:
                    j = i - 2
                    if T_O <= j < T_K:
                        sp.wait_ge(out_done, 4 * (j - T_O + 1))
                    elif j >= T_G:
                        sp.wait_ge(g_done, 4 * (j - T_G + 1))
                    else:
                        groups = 4 * (j + 1 if j < T_O else j + 1 - (T_K - T_O))
                        sp.wait_ge(acc_ready, groups)
                sp.dma_start(ring[i % 2], tiles[i]).then_inc(tile_loaded[i % 2], 16)

            def load_expert(l, e, s, w13=True, w2=True):
                m = moe[l]
                if not w13:
                    sp.dma_start(w2_sb[s], m_w2[l, e].rearrange("(p k) n -> p k n", k=KE)).then_inc(m["w2"][s], 16)
                    return
                sp.dma_start(w1_sb[s], m_w1[l, e].rearrange("(p k) n -> p k n", k=KD)).then_inc(m["w13"][s], 16)
                sp.dma_start(w3_sb[s], m_w3[l, e].rearrange("(p k) n -> p k n", k=KD)).then_inc(m["w13"][s], 16)
                if w2:
                    sp.dma_start(w2_sb[s], m_w2[l, e].rearrange("(p k) n -> p k n", k=KE)).then_inc(m["w2"][s], 16)

            def load_later_expert(l, e, s):
                m = moe[l]
                ended = sp.value_load(n0_i[0:1, bass.ds(e - (NBUF - 1), 1)], min_val=1, max_val=MAX_ITEMS)
                sp.wait_ge(m["up"], ended)
                w1e = m_w1[l][bass.ds(e, 1), :, :].rearrange("a (p k) n -> p (a k) n", k=KD)
                w3e = m_w3[l][bass.ds(e, 1), :, :].rearrange("a (p k) n -> p (a k) n", k=KD)
                w2e = m_w2[l][bass.ds(e, 1), :, :].rearrange("a (p k) n -> p (a k) n", k=KE)
                sp.dma_start(w1_sb[s], w1e).then_inc(m["w13"][s], 16)
                sp.dma_start(w3_sb[s], w3e).then_inc(m["w13"][s], 16)
                sp.wait_ge(m["down"], ended)
                sp.dma_start(w2_sb[s], w2e).then_inc(m["w2"][s], 16)

            def moe_loads(l):
                m = moe[l]
                load_expert(l, 1, 1)
                load_expert(l, 2, 2)
                sp.wait_ge(m["tables"], 2)
                with sp.Fori(1, NE // NBUF) as r:
                    for s in range(NBUF):
                        load_later_expert(l, r * NBUF + s, s)
                for e in range(NE // NBUF * NBUF, NE):
                    load_later_expert(l, e, e % NBUF)

            for t in range(NT):
                sp.dma_start(X[:, t, :], x_in[0, t * P:(t + 1) * P, :]).then_inc(x_loaded[t], 16)
            load_tile(0)
            load_tile(1)
            load_expert(0, 0, 0)
            for i in range(2, T_K):
                load_tile(i)
            sp.wait_ge(out_done, 16)
            moe_loads(0)
            total = sp.value_load(n0_i[0:1, NE:NE + 1], min_val=1, max_val=MAX_ITEMS)
            sp.wait_ge(moe[0]["down"], total)
            for i in range(T_K, T_K + 2):
                sp.dma_start(ring[i % 2], tiles[i]).then_inc(tile_loaded[i % 2], 16)
            load_expert(1, 0, 0, w2=False)
            for i in range(T_K + 2, len(tiles)):
                load_tile(i)
            sp.wait_ge(acc_ready, G_WO + 8)
            load_expert(1, 0, 0, w13=False)
            moe_loads(1)
            for t in range(NT):
                sp.wait_ge(moe[1]["combined"], 2 * t + 2)
                sp.dma_start(out[0, t * P:(t + 1) * P, :], X[:, t, :]).then_inc(stored, 16)
            sp.wait_ge(stored, 16 * NT)

        @block.gpsimd
        def _(pool):
            g = nc.gpsimd
            made = [0]

            def make(ins):
                made[0] += 1
                ins.then_inc(const_made, 1)

            make(g.memset(ident[:, :], 0.0))
            make(g.memset(tri[:, :], 1.0))
            make(g.memset(tri_in[:, :], 1.0))
            make(g.memset(ones[:, :], 1.0))
            make(g.memset(ident_b[:, :], 0.0))
            make(g.memset(mask_b[:, :], 0.0))
            make(g.memset(eps[:, :], EPS))
            make(g.iota(iota_m[:, :], pattern=[[1, NE]], base=-64, channel_multiplier=0,
                        allow_small_or_imprecise_dtypes=True))
            make(g.iota(iota_c[:, :], pattern=[[1, CAP]], base=0, channel_multiplier=0,
                        allow_small_or_imprecise_dtypes=True))
            make(g.iota(thr7[:, :], pattern=[[CAP, 8]], base=CAP, channel_multiplier=0,
                        allow_small_or_imprecise_dtypes=True))
            pool.wait_ge(const_made, made[0])
            for m in (ident, ident_b):
                g.affine_select(out=m[:, :], in_=m[:, :], compare_op=ALU.not_equal, fill=1.0, base=0,
                                pattern=[[-1, P]], channel_multiplier=1).then_inc(const_ready, 1)
            g.affine_select(out=tri[:, :], in_=tri[:, :], compare_op=ALU.is_ge, fill=0.0, base=-1,
                            pattern=[[1, P]], channel_multiplier=-1).then_inc(const_ready, 1)
            g.affine_select(out=tri_in[:, :], in_=tri_in[:, :], compare_op=ALU.is_ge, fill=0.0, base=0,
                            pattern=[[1, P]], channel_multiplier=-1).then_inc(const_ready, 1)
            g.affine_select(out=mask_b[:, :], in_=mask_b[:, :], compare_op=ALU.is_ge, fill=-BIG, base=0,
                            pattern=[[-1, P]], channel_multiplier=1).then_inc(const_ready, 1)

            def load_gain(n, src):
                pool.dma_start(gain[:, :], src.partition_broadcast(P)).then_inc(norm[n]["gain"], 16)

            def load_router(l):
                m = moe[l]
                pool.dma_start(wr[:, :, 0:NG], m_w_group[l].rearrange("(p k) n -> p k n", k=KD))\
                    .then_inc(m["router_loaded"], 16)
                pool.dma_start(wr[:, :, NG:NR], m_w_expert[l].rearrange("(p k) n -> p k n", k=KD))\
                    .then_inc(m["router_loaded"], 16)
                pool.dma_start(br[:, 0:NG], m_b_group[l].partition_broadcast(P)).then_inc(m["router_loaded"], 16)
                pool.dma_start(br[:, NG:NR], m_b_expert[l].partition_broadcast(P)).then_inc(m["router_loaded"], 16)

            def gather_outputs(l):
                m = moe[l]
                pool.wait_ge(m["y_complete"], 1)
                for t in range(NT):
                    for k in range(2):
                        g.indirect_dma_start(
                            out=y_got[:, 2 * t + k, :], out_offset=None, in_=y_rows[l][0:SLOTS, :],
                            in_offset=bass.IndirectOffsetOnAxis(ap=pos_i[:, 4 * k + t:4 * k + t + 1], axis=0),
                        ).then_inc(m["y_got"][t], 16)

            pool.dma_start(ws_raw, a_w_s[0].rearrange("g t s -> t g s")).then_inc(small_loaded, 16)
            pool.dma_start(spare[:, 2 * D:3 * D], a_b_s[0].rearrange("g t -> (g t)").partition_broadcast(P))\
                .then_inc(small_loaded, 16)
            for c, src in enumerate((a_b_in[0, 0:WIDTH], a_v_norm[0])):
                pool.dma_start(cols_raw[c * NC:(c + 1) * NC, :], src.rearrange("(c p) -> c p", p=P))\
                    .then_inc(col_loaded, 16)
            for i, src in enumerate((k_norm, q_norm[0])):
                for h in range(2):
                    pool.dma_start(cols_raw[2 * NC + i:2 * NC + i + 1, h * DH:(h + 1) * DH],
                                   src.rearrange("(a p) -> a p", a=1)).then_inc(col_loaded, 16)
            pool.dma_start(wf[:, :, :], kv_w.rearrange("(p k) n -> p k n", k=KD)[:, :, 2 * D:2 * D + HEADS])\
                .then_inc(col_loaded, 16)
            pool.dma_start(bf_bc[:, :], kv_b_f.partition_broadcast(P)).then_inc(col_loaded, 16)
            for i in range(4):
                if i >= 2:
                    pool.wait_ge(z_ready, 4 * (i - 1) + 1)
                pool.dma_start(b_v[i % 2], a_b_in[0, WIDTH + COL * i:WIDTH + COL * (i + 1)].partition_broadcast(P))\
                    .then_inc(bv_loaded[i % 2], 16)
            load_router(0)
            pool.wait_ge(norm["a"]["hrow"], NT)
            load_gain("m0", m_norm[0])
            pool.wait_ge(norm["m0"]["hrow"], NT)
            load_gain("kv", kv_norm)
            pool.wait_ge(moe[0]["lists_in"], 1)
            load_router(1)
            gather_outputs(0)
            pool.wait_ge(norm["kv"]["hrow"], NT)
            load_gain("b", b_norm[0])
            pool.wait_ge(norm["b"]["hrow"], NT)
            load_gain("m1", m_norm[1])

            gather_outputs(1)

        @block.scalar
        def _(act):
            a = nc.scalar
            done = [0]

            def then(ins):
                done[0] += 1
                ins.then_inc(act_step, 1)
                act.wait_ge(act_step, done[0])

            def stats(n, ready):
                for t in range(NT):
                    act.wait_ge(*ready(t))
                    then(a.activation(junk, X[:, t, :], ACT.Square, accum_out=ss[:, t:t + 1]))
                    a.activation(rms[:, t:t + 1], ss[:, t:t + 1], ACT.Sqrt, bias=eps[:, :], scale=1.0 / D)\
                        .then_inc(norm[n]["rms"], 1)

            def transposed_rows(n):
                for t in range(NT):
                    for h in range(2):
                        act.wait_ge(norm[n]["tr"], 2 * t + h + 1)
                        a.activation(hT[:, 4 * h:4 * h + 4, t * P:(t + 1) * P],
                                     ps[2 + h][:, :].rearrange("p (k n) -> p k n", k=4), ACT.Copy)\
                            .then_inc(norm[n]["ht"], 1)

            def moe_act(l, ready):
                m = moe[l]
                stats(f"m{l}", ready)
                for t in range(NT):
                    if t >= 2:
                        act.wait_ge(m["logits"], t - 1)
                    for h in range(2):
                        act.wait_ge(norm[f"m{l}"]["tr"], 2 * t + h + 1)
                        a.activation(hTc[t % 2][:, 4 * h:4 * h + 4, :],
                                     ps[2 + h][:, :].rearrange("p (k n) -> p k n", k=4), ACT.Copy)\
                            .then_inc(norm[f"m{l}"]["ht"], 1)
                act.wait_ge(m["route_exp_in"], 1)
                a.activation(ohg, ohg, ACT.Exp).then_inc(m["route_exp"], 1)
                act.wait_ge(m["route_exp_in"], 2)
                a.activation(dexp, dexp, ACT.Exp).then_inc(m["route_exp"], 1)
                act.wait_ge(m["tables"], 3)
                total = act.value_load(n0_i[0:1, NE:NE + 1], min_val=1, max_val=MAX_ITEMS)
                a.activation(junk[:, 0:1], eps[:, :], ACT.Copy).then_inc(m["y_out"], 1)
                a.activation(junk[:, 1:2], eps[:, :], ACT.Copy).then_inc(m["y_stored"], 1)
                with act.Fori(0, total) as n:
                    act.wait_ge(m["up"], n + 1)
                    a.activation(silu[CAP:P, :], ps[0][0:CAP, :], ACT.Silu).then_inc(m["silu"], 1)
                    base = act.value_load(base_i[0:1, bass.ds(n, 1)], min_val=0, max_val=SLOTS)
                    act.wait_ge(m["down"], n + 1)
                    act.wait_ge(m["y_stored"], 32 * n + 1)
                    a.activation(ysb, ps[4][:, :], ACT.Copy).then_inc(m["y_out"], 1)
                    act.wait_ge(m["y_out"], n + 2)
                    for h in range(2):
                        act.dma_start(y_rows[l][bass.ds(base, CAP), h * COL:(h + 1) * COL],
                                      ysb[h * CAP:(h + 1) * CAP, :]).then_inc(m["y_stored"], 16)
                act.wait_ge(m["y_stored"], 32 * total + 1)
                a.activation(junk[:, 0:1], eps[:, :], ACT.Copy).then_inc(m["y_complete"], 1)

            act.dma_start(gain[:, :], a_norm[0].partition_broadcast(P)).then_inc(norm["a"]["gain"], 16)
            act.wait_ge(const_ready, 5)
            stats("a", lambda t: (x_loaded[t], 16))
            transposed_rows("a")
            with act.Fori(0, 4) as i:
                for t in range(NT):
                    act.wait_ge(z_ready, 4 * i + t + 2)
                    v_t = vg[:, t, bass.ds(i * COL, COL)]
                    a.activation(v_t, v_t, ACT.Gelu_apprx_tanh).then_inc(v_ready, 1)
                    act.wait_ge(v_ready, 4 * i + t + 1)
                    a.activation(junk[:, 0:COL], v_t, ACT.Square,
                                 accum_out=vss[:, t, bass.ds(i, 1)]).then_inc(vr_ready, 1)
            act.wait_ge(wsts_ready, 1)
            then(a.activation(rms[:, :], ss[:, :], ACT.Sqrt, bias=eps[:, :], scale=1.0 / WIDTH))
            a.activation(junk[:, 0:1], rms[:, 0:1], ACT.Copy).then_inc(vr_ready, 1)
            act.wait_ge(wst_ready, 2)
            for c in range(NC):
                g = G_U + c
                act.wait_ge(acc_ready, g + 1)
                if c >= 2:
                    act.wait_ge(gated, c - 1)
                a.activation(u_tmp[c % 2], ps[g % 2][:, :], ACT.Gelu_apprx_tanh, bias=b_u[:, c:c + 1])\
                    .then_inc(u_ready, 1)
            moe_act(0, lambda t: (x_mixed, 4 + t + 1))

            stats("kv", lambda t: (moe[0]["combined"], 2 * t + 2))
            transposed_rows("kv")

            def head_norms(r, g0, gain_col, dst):
                for j in range(8):
                    g, q = g0 + j, 8 * r + j
                    act.wait_ge(acc_ready, g + 1)
                    if q >= 2:
                        act.wait_ge(hss_ready, q - 1)
                    a.activation(sq[q % 2], ps[g % 2][:, :], ACT.Square).then_inc(sq_ready, 1)
                    act.wait_ge(hss_ready, q + 1)
                    a.activation(hr[:, q % 2, :], hss[:, q % 2, :], ACT.Sqrt, bias=eps[:, :], scale=1.0 / DH)\
                        .then_inc(hrms_ready, 1)
                    if j >= 1:
                        put_heads(r, j - 1, gain_col, dst)
                put_heads(r, 7, gain_col, dst)

            def put_heads(r, j, gain_col, dst):
                q = 8 * r + j
                t, c = j % NT, 4 * (j // NT)
                act.wait_ge(kn_tr, q + 1)
                a.activation(dst[:, c:c + 4, t * P:(t + 1) * P],
                             ps[4 + q % 2][:, :].rearrange("p (c n) -> p c n", c=4), ACT.Copy,
                             scale=kq_gain[:, gain_col:gain_col + 1]).then_inc(kn_out, 1)

            head_norms(0, G_K, 0, KT)
            act.wait_ge(f_ready, 1)
            then(a.activation(lf[:, 1, :], lf[:, 0, :], ACT.Abs))
            then(a.activation(lf[:, 1, :], lf[:, 1, :], ACT.Exp, scale=-1.0))
            a.activation(lf[:, 1, :], lf[:, 1, :], ACT.Ln, bias=1.0).then_inc(f_ln, 1)
            transposed_rows("b")
            act.wait_ge(cumT_done, 1)
            a.activation(junk[0:HEADS, 0:T], ps[6][0:HEADS, :], ACT.Copy, scale=-1.0).then_inc(ncum_ready, 1)
            act.wait_ge(ncum_ready, 1)
            act.dma_start(ncum_rows, junk[0:HEADS, 0:T]).then_inc(ncum_stored, 16)
            head_norms(1, G_Q, 1, QT)
            def load_nck(c):
                for h in range(2):
                    act.dma_start(nck[:, c % 2, h, :], ncum_rows[2 * c + h].partition_broadcast(P))\
                        .then_inc(nck_loaded[c % 2], 16)

            act.wait_ge(ncum_stored, 16)
            act.wait_ge(kn_out, 16)
            load_nck(0)
            load_nck(1)
            for u in range(PAIRS * NT + 2):
                if u >= NT and u % NT == 0:
                    c = u // NT - 1
                    act.wait_ge(g_done, c + 1)
                    a.activation(GT[:, c, :], ps[7][:, :], ACT.Tanh, scale=0.5).then_inc(g_out, 1)
                if u < PAIRS * NT:
                    w = (u % NT + 1) * P
                    for h in range(2):
                        act.wait_ge(s_max, 2 * u + h + 1)
                        a.activation(Pr[:, u % 3, h, 0:w], Pr[:, u % 3, h, 0:w], ACT.Exp, scale=-1.0,
                                     bias=nmx[:, u % 3, h:h + 1],
                                     accum_out=rsum[:, u % 3, h:h + 1]).then_inc(p_exp, 1)
                    if u % NT == NT - 1 and u // NT + 2 < PAIRS:
                        load_nck(u // NT + 2)
                if u >= 2:
                    v = u - 2
                    i = v % NT
                    act.wait_ge(pt_tr, 2 * v + 2)
                    a.activation(PT[:, 1, 0:i + 1, i * P:(i + 1) * P],
                                 ps[5][:, 0:(i + 1) * P].rearrange("p (b n) -> p b n", n=P), ACT.Copy)\
                        .then_inc(pt_out[1], 1)
            moe_act(1, lambda t: (x_attn, 4 + t + 1))

        @block.vector
        def _(dve):
            v = nc.vector
            done = [0]

            def then(ins):
                done[0] += 1
                ins.then_inc(dve_step, 1)
                dve.wait_ge(dve_step, done[0])

            def scaled_rows(n, dst, stats=True, combine=None):
                m = norm[n]
                dve.wait_ge(m["gain"], 16)
                for t in range(NT):
                    if combine is not None:
                        combine(t)
                    if stats:
                        dve.wait_ge(m["rms"], t + 1)
                        then(v.reciprocal(rinv[:, t:t + 1], rms[:, t:t + 1]))
                    if dst is hrow and t >= 2:
                        dve.wait_ge(m["tr"], 2 * t - 2)
                    to = hrow[t % 2] if dst is hrow else h_tok[:, t]
                    v.scalar_tensor_tensor(to, X[:, t, :].rearrange("p (q k) -> p k q", k=KD), rinv[:, t:t + 1],
                                           gain[:, :].rearrange("p (q k) -> p k q", k=KD), ALU.mult, ALU.mult)\
                        .then_inc(m["hrow"], 1)

            def bc(ap, n):
                return ap.unsqueeze(2).to_broadcast([P, NT, n])

            def over_t(ap, n):
                return ap.unsqueeze(1).to_broadcast([P, NT, n])

            def first_of_max(vals, top, n, onehot):
                then(v.tensor_reduce(top, vals, AX, ALU.max))
                then(v.tensor_tensor(cand[:, :, 0:n], vals, bc(top, n), ALU.is_equal))
                then(v.tensor_tensor(cand[:, :, 0:n], cand[:, :, 0:n], over_t(iota_m[:, 0:n], n), ALU.mult))
                then(v.tensor_reduce(mmin, cand[:, :, 0:n], AX, ALU.min))
                then(v.tensor_tensor(onehot, over_t(iota_m[:, 0:n], n), bc(mmin, n), ALU.is_equal))

            def select(n, m, k, link):
                link(v.tensor_scalar(pb, pos[:, :], base_f[:, bass.ds(n, 1)], None, ALU.subtract), 1)
                link(v.tensor_tensor(eqs.rearrange("p k c j -> p (k c) j"),
                                     pb.unsqueeze(2).to_broadcast([P, 8, CAP]),
                                     iota_c[:, :].unsqueeze(1).to_broadcast([P, 8, CAP]), ALU.is_equal), 2)
                v.tensor_tensor(S, eqs[:, 0], eqs[:, 1], ALU.add).then_inc(m["sel"], 1)

            def moe_dve(l):
                m = moe[l]
                scaled_rows(f"m{l}", h_tok)
                dve.wait_ge(m["router_loaded"], 64)
                dve.wait_ge(m["logits"], NT)
                then(v.tensor_tensor(lg, ps[4][:, 0:NT * NR].rearrange("p (t n) -> p t n", t=NT),
                                     over_t(br[:, :], NR), ALU.add))
                glog = lg[:, :, 0:NG]
                first_of_max(glog, gmax, NG, pen)
                then(v.tensor_scalar(pen, pen, BIG, -BIG, ALU.mult, ALU.add))
                v.tensor_tensor(ohg, glog, bc(gmax, NG), ALU.subtract).then_inc(m["route_exp_in"], 1)
                then(v.tensor_tensor(el.rearrange("p t (g e) -> p t g e", g=NG),
                                     lg[:, :, NG:NR].rearrange("p t (g e) -> p t g e", g=NG),
                                     pen.unsqueeze(3).to_broadcast([P, NT, NG, EPG]), ALU.add))
                first_of_max(el, m1, NE, oh[0])
                then(v.scalar_tensor_tensor(el, oh[0], -2.0 * BIG, el, ALU.mult, ALU.add))
                first_of_max(el, m2, NE, oh[1])
                v.tensor_tensor(dexp, m2, m1, ALU.subtract).then_inc(m["route_exp_in"], 1)
                v.tensor_tensor(msum, oh[0], oh[1], ALU.add).then_inc(m["lists_in"], 1)
                dve.wait_ge(m["route_exp"], 2)
                then(v.tensor_reduce(gsum, ohg, AX, ALU.add))
                then(v.tensor_scalar(m1, dexp, 1.0, None, ALU.add))
                then(v.tensor_tensor(m1, m1, gsum, ALU.mult))
                then(v.reciprocal(w12[:, 0:4], m1))
                v.tensor_tensor(w12[:, 4:8], w12[:, 0:4], dexp, ALU.mult).then_inc(m["step"], 1)
                dve.wait_ge(m["step"], 1)
                dve.wait_ge(m["lists_out"], 1)
                then(v.tensor_copy(cn[0:NE, 0:1], ps[6][0:NE, 0:1]))
                then(v.tensor_tensor(cmp7[0:NE, 0:7], thr7[0:NE, 0:7], cn[0:NE, 0:1].to_broadcast([NE, 7]), ALU.is_lt))
                then(v.tensor_reduce(cn[0:NE, 1:2], cmp7[0:NE, 0:7], AX, ALU.add))
                then(v.tensor_scalar(cn[0:NE, 1:2], cn[0:NE, 1:2], 1.0, None, ALU.add))
                v.tensor_scalar(cntb[0:NE, :], ones[0:NE, :], cn[0:NE, 0:1], None, ALU.mult).then_inc(m["lists_in"], 1)
                dve.wait_ge(m["lists_out"], 2)
                then(v.tensor_copy(s0n0[0:NE, :], ps[6][0:NE, 4:6]))
                it = item_tmp[0:NE]
                then(v.tensor_scalar(it[:, 0, :], iota_c[0:NE, 0:NBASE], s0n0[0:NE, 1:2], None, ALU.subtract))
                then(v.tensor_scalar(it[:, 1, :], it[:, 0, :], float(CAP), s0n0[0:NE, 0:1], ALU.mult, ALU.add))
                then(v.tensor_scalar(it[:, 2, :], it[:, 0, :], cn[0:NE, 1:2], None, ALU.is_lt))
                then(v.tensor_tensor(it[:, 1, :], it[:, 1, :], it[:, 2, :], ALU.mult))
                then(v.tensor_scalar(it[:, 2, :], it[:, 0, :], 0.0, None, ALU.is_ge))
                v.tensor_tensor(it[:, 1, :], it[:, 1, :], it[:, 2, :], ALU.mult).then_inc(m["lists_in"], 1)
                for k in range(2):
                    then(v.tensor_tensor(cand, oh[k], ps[5][:, 0:NT * NE].rearrange("p (t n) -> p t n", t=NT),
                                         ALU.mult))
                    then(v.tensor_reduce(pos[:, 4 * k:4 * k + 4], cand, AX, ALU.add))
                v.tensor_copy(pos_i[:, :], pos[:, :]).then_inc(m["tables"], 1)
                v.tensor_copy(n0_i[0:1, 0:NE + 1], ps[6][0:1, 8:8 + NE + 1]).then_inc(m["tables"], 1)
                dve.wait_ge(m["lists_out"], 3)
                then(v.tensor_copy(base_f[:, :], ps[7][:, 0:NBASE]))
                v.tensor_copy(base_i[0:1, 0:NBASE], base_f[0:1, :]).then_inc(m["tables"], 1)
                dve.wait_ge(m["tables"], 3)
                total = dve.value_load(n0_i[0:1, NE:NE + 1], min_val=1, max_val=MAX_ITEMS)
                v.memset(hid[CAP:P, :], 0.0)
                select(0, m, 0, lambda ins, k: then(ins))
                dve.wait_ge(m["gath"], 1)
                v.tensor_copy(xg, ps[1][:, :]).then_inc(m["xg"], 1)
                dve.wait_ge(m["xT_tr"], 1)
                v.tensor_copy(xT.rearrange("p (h j) c -> p j h c", h=2),
                              ps[3][:, :].rearrange("p (j h c) -> p j h c", j=4, h=2)).then_inc(m["xT"], 1)
                select(1, m, 0, lambda ins, k: then(ins))
                with dve.Fori(0, total) as n:
                    dve.wait_ge(m["silu"], n + 1)
                    v.tensor_tensor(hid[0:CAP, :], silu[CAP:P, :], ps[0][CAP:P, :], ALU.mult).then_inc(m["hid"], 1)
                    dve.wait_ge(m["gath"], n + 2)
                    v.tensor_copy(xg, ps[1][:, :]).then_inc(m["xg"], 1)
                    dve.wait_ge(m["hidT_tr"], n + 1)
                    v.tensor_copy(hidT, ps[2][:, :].rearrange("p (k c) -> p k c", k=KE)[:, :, 0:CAP])\
                        .then_inc(m["hidT"], 1)
                    dve.wait_ge(m["xT_tr"], n + 2)
                    v.tensor_copy(xT.rearrange("p (h j) c -> p j h c", h=2),
                                  ps[3][:, :].rearrange("p (j h c) -> p j h c", j=4, h=2)).then_inc(m["xT"], 1)

                    def link(ins, k):
                        ins.then_inc(m["step"], 1)
                        dve.wait_ge(m["step"], 2 * n + k + 1)

                    select(n + 2, m, 0, link)

            def combine(l, t):
                m = moe[l]
                dve.wait_ge(m["y_got"][t], 32)
                for k in range(2):
                    v.scalar_tensor_tensor(X[:, t, :], y_got[:, 2 * t + k, :], w12[:, 4 * k + t:4 * k + t + 1],
                                           X[:, t, :], ALU.mult, ALU.add).then_inc(m["combined"], 1)
                    dve.wait_ge(m["combined"], 2 * t + k + 1)

            dve.wait_ge(const_ready, 5)
            scaled_rows("a", hrow)
            v.memset(vss[:, :, :], 0.0).then_inc(z_ready, 1)
            with dve.Fori(0, 2) as r:
                for j in range(2):
                    dve.wait_ge(bv_loaded[j], 16 * (r + 1))
                    for t in range(NT):
                        b = t % 2
                        dve.wait_ge(acc_ready, 8 * r + 4 * j + t + 1)
                        v.tensor_tensor(vg[:, t, bass.ds(r * 2 * COL + j * COL, COL)], ps[b][:, :], b_v[j], ALU.add)\
                            .then_inc(z_ready, 1)
            dve.wait_ge(wst_done, 3)
            for h in range(2):
                then(v.tensor_copy(wsT[:, 4 * h:4 * h + 4, :], ps[4 + h][:, :].rearrange("p (g s) -> p g s", g=4)))
            v.memset(wsT[P // 2:P, :, 0:P // 2], 0.0).then_inc(wst_ready, 1)
            v.tensor_copy(cols[:, :], ps[6][:, 0:2 * NC + 2]).then_inc(wst_ready, 1)
            dve.wait_ge(vr_ready, 16)
            v.tensor_reduce(ss[:, :], vss[:, :, :], AX, ALU.add).then_inc(wsts_ready, 1)
            dve.wait_ge(vr_ready, 17)
            then(v.reciprocal(rinv[:, :], rms[:, :]))
            dve.wait_ge(wst_ready, 2)
            for t in range(NT):
                v.tensor_scalar(wsTs[:, t], wsT, rinv[:, t:t + 1], None, ALU.mult).then_inc(wsts_ready, 1)
            dve.wait_ge(small_loaded, 32)
            for c in range(NC):
                dve.wait_ge(mix_done[c % 2], c // 2 + 1)
                v.scalar_tensor_tensor(vg[:, :, c * P:(c + 1) * P], ps[4 + c % 2][:, :].rearrange("p (t n) -> p t n", t=NT),
                                       v_gain[:, c:c + 1], over_t(bs_bc[:, c // 2, :], P), ALU.mult, ALU.add)\
                    .then_inc(mix_free[c % 2], 1)
            for c in range(NC):
                dve.wait_ge(u_ready, c + 1)
                dve.wait_ge(mix_free[c % 2], c // 2 + 1)
                v.tensor_tensor(vg[:, :, c * P:(c + 1) * P], vg[:, :, c * P:(c + 1) * P],
                                u_tmp[c % 2].rearrange("p (t n) -> p t n", t=NT), ALU.mult).then_inc(gated, 1)
            for n in range(2):
                for t in range(NT):
                    dve.wait_ge(out_done, 8 * n + 4 + t + 1)
                    v.tensor_tensor(X[:, t, n * COL:(n + 1) * COL], X[:, t, n * COL:(n + 1) * COL], ps[4 + t][:, :],
                                    ALU.add).then_inc(x_mixed, 1)
            moe_dve(0)

            combine(0, 0)
            scaled_rows("kv", hrow, combine=lambda t: combine(0, t + 1) if t + 1 < NT else None)

            def head_norms(r, g0):
                for j in range(8):
                    g, q = g0 + j, 8 * r + j
                    dve.wait_ge(sq_ready, q + 1)
                    v.tensor_reduce(hss[:, q % 2, :], sq[q % 2].rearrange("p (h d) -> p h d", h=8), AX, ALU.add)\
                        .then_inc(hss_ready, 1)
                    dve.wait_ge(hrms_ready, q + 1)
                    then(v.reciprocal(hr[:, q % 2, :], hr[:, q % 2, :]))
                    if q >= 2:
                        dve.wait_ge(kn_tr, q - 1)
                    v.tensor_tensor(kn[q % 2].rearrange("p (h d) -> p h d", h=8),
                                    ps[g % 2][:, :].rearrange("p (h d) -> p h d", h=8),
                                    hr[:, q % 2, :].unsqueeze(2).to_broadcast([P, 8, DH]), ALU.mult)\
                        .then_inc(kn_ready, 1)

            head_norms(0, G_K)
            for j in range(8):
                g = G_VV + j
                dve.wait_ge(acc_ready, g + 1)
                v.tensor_copy(V[:, j % NT, (j // NT) * COL:(j // NT + 1) * COL], ps[g % 2][:, :])\
                    .then_inc(v_out, 1)
            dve.wait_ge(f_done, 1)
            f3 = lf[:, 0, :].rearrange("p (t n) -> p t n", t=NT)
            v.tensor_tensor(f3, ps[6][:, 0:NT * HEADS].rearrange("p (t n) -> p t n", t=NT),
                            over_t(bf_bc[:, :], HEADS), ALU.add).then_inc(f_ready, 1)
            dve.wait_ge(f_ready, 1)
            then(v.tensor_scalar(lf[:, 2, :], lf[:, 0, :], 0.0, None, ALU.min))
            scaled_rows("b", hrow, stats=False)
            dve.wait_ge(f_ln, 1)
            v.tensor_tensor(lf[:, 0, :], lf[:, 2, :], lf[:, 1, :], ALU.subtract).then_inc(lf_ready, 1)
            dve.wait_ge(cum_done, 1)
            v.tensor_copy(lf[:, 1, :], ps[7][:, 0:NT * HEADS]).then_inc(cum_ready, 1)
            then(v.tensor_scalar(kq_gain[:, 1:2], kq_gain[:, 1:2], DH ** -0.5, None, ALU.mult))
            head_norms(1, G_Q)
            n_units = PAIRS * NT
            for u in range(n_units + 3):
                if u < n_units:
                    i, c = u % NT, u // NT
                    w = (i + 1) * P
                    if i == 0:
                        dve.wait_ge(nck_loaded[c % 2], 32 * (c // 2 + 1))
                    for h in range(2):
                        dve.wait_ge(s_done, 2 * u + h + 1)
                        if u >= 3:
                            dve.wait_ge(pt_tr, 2 * (u - 3) + h + 1)
                        v.tensor_tensor_reduce(out=Pr[:, u % 3, h, 0:w], in0=ps[2 * (u % 2) + h][:, 0:w],
                                               in1=nck[:, c % 2, h, 0:w], scale=-1.0, scalar=BIG, op0=ALU.add,
                                               op1=ALU.min, accum_out=nmx[:, u % 3, h:h + 1]).then_inc(s_max, 1)
                if 1 <= u <= n_units:
                    q = u - 1
                    dve.wait_ge(p_exp, 2 * q + 2)
                    then(v.reciprocal(rrec[:, q % 3, :], rsum[:, q % 3, :]))
                    w = (q % NT + 1) * P
                    for h in range(2):
                        v.tensor_scalar(Pr[:, q % 3, h, 0:w], Pr[:, q % 3, h, 0:w], rrec[:, q % 3, h:h + 1], 0.5,
                                        ALU.mult, ALU.mult).then_inc(p_ready, 1)
                if 2 <= u <= n_units + 1:
                    q = u - 2
                    i = q % NT
                    dve.wait_ge(pt_tr, 2 * q + 1)
                    v.tensor_copy(PT[:, 0, 0:i + 1, i * P:(i + 1) * P],
                                  ps[4][:, 0:(i + 1) * P].rearrange("p (b n) -> p b n", n=P)).then_inc(pt_out[0], 1)
                if u >= 3 and (u - 3) % NT == NT - 1:
                    c = (u - 3) // NT
                    dve.wait_ge(o_done, c + 1)
                    dve.wait_ge(g_out, c + 1)
                    v.scalar_tensor_tensor(GT[:, c, :], GT[:, c, :], 1.0, ps[6][:, :], ALU.add, ALU.mult)\
                        .then_inc(o_gated, 1)
            for j in range(8):
                g, t, n = G_WO + j, j % NT, j // NT
                dve.wait_ge(acc_ready, g + 1)
                v.tensor_tensor(X[:, t, n * COL:(n + 1) * COL], X[:, t, n * COL:(n + 1) * COL], ps[g % 2][:, :],
                                ALU.add).then_inc(x_attn, 1)
            moe_dve(1)
            for t in range(NT):
                combine(1, t)

        @block.tensor
        def _(pe):
            mm = nc.tensor.matmul

            def transpose_rows(n, t, rows):
                m = norm[n]
                pe.wait_ge(m["hrow"], t + 1)
                for h in range(2):
                    if t >= 1:
                        pe.wait_ge(m["ht"], 2 * (t - 1) + h + 1)
                    for j in range(4):
                        last = nc.tensor.transpose(ps[2 + h][:, j * P:(j + 1) * P], rows[:, 4 * h + j, :], ident[:, :])
                    last.then_inc(m["tr"], 1)

            def project(i, g0, bank_free):
                pe.wait_ge(tile_loaded[i % 2], 16 * (i // 2 + 1))
                for t in range(NT):
                    g = g0 + t
                    bank_free(g)
                    for k in range(KD):
                        last = mm(ps[g % 2][:, :], hT[:, k, t * P:(t + 1) * P], ring[i % 2][:, k, :],
                                  start=k == 0, stop=k == KD - 1)
                    last.then_inc(acc_ready, 1)

            def project_transposed(i, g0, bank_free):
                pe.wait_ge(tile_loaded[i % 2], 16 * (i // 2 + 1))
                for j in range(4):
                    g = g0 + j
                    bank_free(g)
                    for k in range(KD):
                        last = mm(ps[g % 2][:, :], ring[i % 2][:, k, j * P:(j + 1) * P], hT[:, k, :],
                                  start=k == 0, stop=k == KD - 1)
                    last.then_inc(acc_ready, 1)

            def moe_pe(l):
                m = moe[l]

                def logits(t):
                    pe.wait_ge(norm[f"m{l}"]["ht"], 2 * t + 2)
                    for k in range(KD):
                        last = mm(ps[4][:, t * NR:(t + 1) * NR], hTc[t % 2][:, k, :], wr[:, k, :],
                                  start=k == 0, stop=k == KD - 1)
                    last.then_inc(m["logits"], 1)

                pe.wait_ge(m["router_loaded"], 64)
                for t in range(NT):
                    transpose_rows(f"m{l}", t, h_tok[:, t])
                    if t >= 1:
                        logits(t - 1)
                logits(NT - 1)
                pe.wait_ge(m["lists_in"], 1)
                for c in range(NT):
                    last = mm(ps[6][0:NE, 0:1], msum[:, c, :], ones[:, 0:1], start=c == 0, stop=c == NT - 1)
                last.then_inc(m["lists_out"], 1)
                pe.wait_ge(m["lists_in"], 2)
                mm(ps[6][0:NE, 4:6], tri[0:NE, 0:NE], cn[0:NE, :], start=True, stop=True)
                mm(ps[6][0:1, 8:8 + NE + 1], cn[0:NE, 1:2], tri[0:NE, 0:NE + 1], start=True, stop=True)
                for c in range(NT):
                    rk = ps[5][:, c * NE:(c + 1) * NE]
                    mm(rk, tri[:, :], msum[:, c, :], start=True, stop=False)
                    for b in range(c):
                        mm(rk, ones[:, :], msum[:, b, :], start=False, stop=False)
                    last = mm(rk, cntb[0:NE, :], tri[0:NE, 0:NE], start=False, stop=True)
                last.then_inc(m["lists_out"], 1)
                pe.wait_ge(m["lists_in"], 3)
                mm(ps[7][:, 0:NBASE], ones[0:NE, :], item_tmp[0:NE, 1, :], start=True, stop=True)\
                    .then_inc(m["lists_out"], 1)

                def gather(n):
                    pe.wait_ge(m["sel"], n + 1)
                    for c in range(NT):
                        for h in range(2):
                            last = mm(ps[1][h * CAP:(h + 1) * CAP, :], S[:, c, :],
                                      H[:, c * D + h * COL:c * D + (h + 1) * COL], start=c == 0, stop=c == NT - 1)
                    last.then_inc(m["gath"], 1)

                def transpose_item(n):
                    pe.wait_ge(m["xg"], n + 1)
                    for j in range(4):
                        last = nc.tensor.transpose(ps[3][:, j * P:(j + 1) * P], xg[:, j * P:(j + 1) * P], ident[:, :])
                    last.then_inc(m["xT_tr"], 1)

                def expert(s, loads, r0, r1):
                    with pe.Fori(r0, r1) as n:
                        pe.wait_ge(m["w13"][s], 32 * loads)
                        pe.wait_ge(m["xT"], n + 1)
                        for k in range(KD):
                            for h, w in enumerate((w1_sb[s], w3_sb[s])):
                                last = mm(ps[0][h * CAP:(h + 1) * CAP, :], xT[:, k, :], w[:, k, :],
                                          start=k == 0, stop=k == KD - 1)
                        last.then_inc(m["up"], 1)
                        gather(n + 1)
                        pe.wait_ge(m["hid"], n + 1)
                        for k in range(KE):
                            last = nc.tensor.transpose(ps[2][:, k * P:(k + 1) * P], hid[:, k:DE:KE], ident[:, :])
                        last.then_inc(m["hidT_tr"], 1)
                        transpose_item(n + 1)
                        pe.wait_ge(m["hidT"], n + 1)
                        pe.wait_ge(m["w2"][s], 16 * loads)
                        pe.wait_ge(m["y_out"], n + 1)
                        for k in range(KE):
                            for h in range(2):
                                last = mm(ps[4][h * CAP:(h + 1) * CAP, :], hidT[:, k, :],
                                          w2_sb[s][:, k, h * COL:(h + 1) * COL], start=k == 0, stop=k == KE - 1)
                        last.then_inc(m["down"], 1)

                def items_of(e):
                    return (pe.value_load(n0_i[0:1, bass.ds(e, 1)], min_val=0, max_val=MAX_ITEMS - 1),
                            pe.value_load(n0_i[0:1, bass.ds(e + 1, 1)], min_val=1, max_val=MAX_ITEMS))

                pe.wait_ge(m["tables"], 3)
                gather(0)
                transpose_item(0)
                with pe.Fori(0, NE // NBUF) as r:
                    for s in range(NBUF):
                        expert(s, r + 1, *items_of(r * NBUF + s))
                for e in range(NE // NBUF * NBUF, NE):
                    expert(e % NBUF, e // NBUF + 1, *items_of(e))

            pe.wait_ge(const_ready, 5)
            for t in range(NT):
                transpose_rows("a", t, hrow[t % 2])
            pe.wait_ge(norm["a"]["ht"], 8)
            with pe.Fori(0, 2) as r:
                for j in range(2):
                    pe.wait_ge(tile_loaded[j], 16 * (r + 1))
                    for t in range(NT):
                        b = t % 2
                        pe.wait_ge(z_ready, 8 * r + max(4 * j + t - 1, 0) + 1)
                        for k in range(KD):
                            last = mm(ps[b][:, :], hT[:, k, t * P:(t + 1) * P], ring[j][:, k, :],
                                      start=k == 0, stop=k == KD - 1)
                        last.then_inc(acc_ready, 1)
            pe.wait_ge(small_loaded, 32)
            for h in range(2):
                for j in range(4):
                    last = nc.tensor.transpose(ps[4 + h][:, j * P:(j + 1) * P], ws_raw[:, 4 * h + j, :], ident[:, :])
                last.then_inc(wst_done, 1)
            pe.wait_ge(col_loaded, 16 * 8)
            nc.tensor.transpose(ps[6][:, 0:2 * NC + 2], cols_raw[:, :], ident[0:2 * NC + 2, 0:2 * NC + 2])\
                .then_inc(wst_done, 1)
            def free_u(g):
                c = g - G_U
                pe.wait_ge(*((z_ready, 16 + c) if c < 2 else (u_ready, c - 1)))

            for i in range(4):
                project_transposed(T_U + i, G_U + 4 * i, free_u)
                if i == 0:
                    pe.wait_ge(wsts_ready, 5)
                    for c in range(NC):
                        pe.wait_ge(mix_free[c % 2], c // 2)
                        for t in range(NT):
                            last = mm(ps[4 + c % 2][:, t * P:(t + 1) * P], vg[:, t, c * P:(c + 1) * P],
                                      wsTs[:, t, c // 2, :], start=True, stop=True)
                        last.then_inc(mix_done[c % 2], 1)
            for n in range(2):
                for c in range(2):
                    i = T_O + 2 * n + c
                    pe.wait_ge(tile_loaded[i % 2], 16 * (i // 2 + 1))
                    pe.wait_ge(gated, 8 * (c + 1))
                    for t in range(NT):
                        if n == 1 and c == 0:
                            pe.wait_ge(x_mixed, t + 1)
                        for k in range(KD):
                            last = mm(ps[4 + t][:, :], vg[:, t, (8 * c + k) * P:(8 * c + k + 1) * P],
                                      ring[i % 2][:, k, :], start=c == 0 and k == 0, stop=c == 1 and k == KD - 1)
                        last.then_inc(out_done, 1)
            moe_pe(0)

            for t in range(NT):
                transpose_rows("kv", t, hrow[t % 2])

            def turn_heads(q):
                pe.wait_ge(kn_ready, q + 1)
                if q >= 2:
                    pe.wait_ge(kn_out, q - 1)
                for c in range(4):
                    last = nc.tensor.transpose(ps[4 + q % 2][:, c * P:(c + 1) * P], kn[q % 2][:, c * P:(c + 1) * P],
                                               ident[:, :])
                last.then_inc(kn_tr, 1)

            def project_heads(i0, g0, r, bank_free):
                for i in range(2):
                    pe.wait_ge(tile_loaded[(i0 + i) % 2], 16 * ((i0 + i) // 2 + 1))
                    for t in range(NT):
                        g = g0 + 4 * i + t
                        bank_free(g)
                        for k in range(KD):
                            last = mm(ps[g % 2][:, :], hT[:, k, t * P:(t + 1) * P], ring[(i0 + i) % 2][:, k, :],
                                      start=k == 0, stop=k == KD - 1)
                        last.then_inc(acc_ready, 1)
                        if 4 * i + t >= 1:
                            turn_heads(8 * r + 4 * i + t - 1)

            pe.wait_ge(norm["kv"]["ht"], 8)

            def free_k(g):
                if g - G_K >= 2:
                    pe.wait_ge(kn_ready, g - G_K - 1)

            def free_vv(g):
                j = g - G_VV
                pe.wait_ge(*((kn_ready, 7 + j) if j < 2 else (v_out, j - 1)))

            def free_q(g):
                j = g - G_Q
                pe.wait_ge(*((v_out, 7 + j) if j < 2 else (kn_ready, 8 + j - 1)))

            project_heads(T_K, G_K, 0, free_k)
            for t in range(NT):
                for k in range(KD):
                    last = mm(ps[6][:, t * HEADS:(t + 1) * HEADS], hT[:, k, t * P:(t + 1) * P], wf[:, k, :],
                              start=k == 0, stop=k == KD - 1)
            last.then_inc(f_done, 1)
            turn_heads(7)
            project(T_VV, G_VV, free_vv)
            project(T_VV + 1, G_VV + 4, free_vv)
            for t in range(NT):
                transpose_rows("b", t, hrow[t % 2])
            pe.wait_ge(lf_ready, 1)
            for c in range(NT):
                o = ps[7][:, c * HEADS:(c + 1) * HEADS]
                for b in range(c):
                    mm(o, ones[:, :], lf[:, 0, b * HEADS:(b + 1) * HEADS], start=b == 0, stop=False)
                last = mm(o, tri_in[:, :], lf[:, 0, c * HEADS:(c + 1) * HEADS], start=c == 0, stop=True)
            last.then_inc(cum_done, 1)
            pe.wait_ge(cum_ready, 1)
            for c in range(NT):
                last = nc.tensor.transpose(ps[6][0:HEADS, c * P:(c + 1) * P], lf[:, 1, c * HEADS:(c + 1) * HEADS],
                                           ident[:, :])
            last.then_inc(cumT_done, 1)
            pe.wait_ge(norm["b"]["ht"], 8)
            project_heads(T_Q, G_Q, 1, free_q)
            turn_heads(15)

            pe.wait_ge(kn_out, 16)
            n_units = PAIRS * NT
            for u in range(n_units + 2):
                if u < n_units:
                    i, c = u % NT, u // NT
                    w = (i + 1) * P
                    if u >= 2:
                        pe.wait_ge(s_max, 2 * (u - 2) + 2)
                    for h in range(2):
                        mm(ps[2 * (u % 2) + h][:, 0:w], QT[h * DH:(h + 1) * DH, c, i * P:(i + 1) * P],
                           KT[h * DH:(h + 1) * DH, c, 0:w], start=True, stop=False)
                    for h in range(2):
                        mm(ps[2 * (u % 2) + h][:, i * P:w], ident_b[:, :], mask_b[:, :], start=False, stop=True)\
                            .then_inc(s_done, 1)
                    j = T_G + c // 4
                    if i == 0:
                        pe.wait_ge(tile_loaded[j % 2], 16 * (j // 2 + 1))
                        if c >= 1:
                            pe.wait_ge(g_out, c)
                    for k in range(2 * i, 2 * i + 2):
                        last = mm(ps[7][:, :], ring[j % 2][:, k, c % 4 * P:(c % 4 + 1) * P], hT[:, k, :],
                                  start=k == 0, stop=k == KD - 1)
                    if i == NT - 1:
                        last.then_inc(g_done, 1)
                if u >= 2:
                    q = u - 2
                    i, c = q % NT, q // NT
                    for h in range(2):
                        pe.wait_ge(p_ready, 2 * q + h + 1)
                        pe.wait_ge(pt_out[h], q)
                        for b in range(i + 1):
                            last = nc.tensor.transpose(ps[4 + h][:, b * P:(b + 1) * P],
                                                       Pr[:, q % 3, h, b * P:(b + 1) * P], ident[:, :])
                        last.then_inc(pt_tr, 1)
                    if i == NT - 1:
                        pe.wait_ge(pt_out[0], q + 1)
                        pe.wait_ge(pt_out[1], q + 1)
                        if c >= 1:
                            pe.wait_ge(o_gated, c)
                        for b in range(NT):
                            for h in range(2):
                                last = mm(ps[6][h * DH:(h + 1) * DH, b * P:T],
                                          V[:, b, (2 * c + h) * DH:(2 * c + h + 1) * DH], PT[:, h, b, b * P:T],
                                          start=b == 0, stop=b == NT - 1)
                        last.then_inc(o_done, 1)
            pe.wait_ge(o_gated, PAIRS)
            for n in range(2):
                i = T_WO + n
                pe.wait_ge(tile_loaded[i % 2], 16 * (i // 2 + 1))
                for t in range(NT):
                    g = G_WO + 4 * n + t
                    if 4 * n + t >= 2:
                        pe.wait_ge(x_attn, 4 * n + t - 1)
                    for c in range(PAIRS):
                        last = mm(ps[g % 2][:, :], GT[:, c, t * P:(t + 1) * P], ring[i % 2][:, c, :],
                                  start=c == 0, stop=c == PAIRS - 1)
                    last.then_inc(acc_ready, 1)
            moe_pe(1)


_INS = ["x", "a_norm", "a_w_in", "a_b_in", "a_v_norm", "a_w_s", "a_b_s", "a_w_out", "kv_norm", "kv_w", "kv_b_f",
        "k_norm", "b_norm", "b_w_qg", "q_norm", "b_w_out", "m_norm", "m_w_group", "m_b_group", "m_w_expert",
        "m_b_expert", "m_w1", "m_w3", "m_w2"]


def kernel(**inputs):
    import numpy as np
    import concourse.bacc as bacc
    from concourse.bass_utils import run_bass_kernel_spmd

    nc = bacc.Bacc("TRN2", target_bir_lowering=False, num_devices=1)
    arrays, args = {}, []
    for name in _INS:
        a = np.ascontiguousarray(inputs[name])
        arrays[f"in_{name}"] = a
        args.append(nc.dram_tensor(f"in_{name}", a.shape, mybir.dt.from_np(a.dtype), kind="ExternalInput").ap())
    args.append(nc.dram_tensor("out_x", (1, T, D), F32, kind="ExternalOutput").ap())
    trunk(nc, *args)
    r = run_bass_kernel_spmd(nc, [arrays], core_ids=[0])
    return r.results[0]["out_x"]
```

```python
from contextlib import ExitStack

import concourse.bass as bass
from concourse import mybir

F32 = mybir.dt.float32
I32 = mybir.dt.int32
BF16 = mybir.dt.bfloat16
F32R = mybir.dt.float32r
ALU = mybir.AluOpType
ACT = mybir.ActivationFunctionType
AX = mybir.AxisListType.X

P = 128
D = 1024
T = 512
NT = T // P
KD = D // P
EPS = 1e-6
WIDTH = 2 * D
NC = WIDTH // P
SG = 8
HEADS = 16
PAIRS = HEADS // 2
DH = D // HEADS
NG = 4
EPG = 8
NE = NG * EPG
DE = D // 2
KE = DE // P
NR = NG + NE
CAP = 64
SLOTS = 2 * T
MAX_ITEMS = SLOTS // CAP + NE
NBASE = MAX_ITEMS + 2
NBUF = 3
COL = 512
BIG = 1e30


def trunk(nc, x_in, a_norm, a_w_in, a_b_in, a_v_norm, a_w_s, a_b_s, a_w_out, kv_norm, kv_w, kv_b_f, k_norm,
          b_norm, b_w_qg, q_norm, b_w_out, m_norm, m_w_group, m_b_group, m_w_expert, m_b_expert,
          m_w1, m_w3, m_w2, out):
    with ExitStack() as ctx:
        def sb(name, shape, dt=F32):
            return ctx.enter_context(nc.sbuf_tensor(name, shape, dt))

        def sem(name):
            return ctx.enter_context(nc.semaphore(name))

        def sems(name, n):
            return [sem(f"{name}{i}") for i in range(n)]

        y_rows = [nc.dram_tensor(f"y_rows{l}", (SLOTS + CAP, D), F32, kind="Internal").ap() for l in range(2)]
        ncum_rows = nc.dram_tensor("ncum_rows", (HEADS, T), F32, kind="Internal").ap()

        def sb_split(name, shape):
            place = -(-nc.sbuf_base // 32) * 32
            full = sb(name, shape)
            return full, nc.alloc_sbuf_tensor_at(name + "_r", shape, F32R, offset=place)

        X = sb("X", [P, NT, D])
        H, H_r = sb_split("H", [P, NT * D])
        EB, EB_r = zip(*[sb_split(f"EB{s}", [P, 3 * KD * COL]) for s in range(NBUF)])
        SCR = sb("SCR", [P, 5 * D])
        gain = sb("gain", [P, D])

        h_tok = H[:, :].rearrange("p (t k q) -> p t k q", t=NT, k=KD)
        hT = H[:, :].rearrange("p (k n) -> p k n", k=KD)
        TILE = KD * COL
        w1_sb = [EB[s][:, 0:TILE].rearrange("p (k n) -> p k n", k=KD) for s in range(NBUF)]
        w3_sb = [EB[s][:, TILE:2 * TILE].rearrange("p (k n) -> p k n", k=KD) for s in range(NBUF)]
        w2_sb = [EB[s][:, 2 * TILE:3 * TILE].rearrange("p (k n) -> p k n", k=KE) for s in range(NBUF)]
        ring = [EB[1][:, s * TILE:(s + 1) * TILE].rearrange("p (k n) -> p k n", k=KD) for s in range(2)]
        ring_lo = [EB_r[1][:, s * TILE:(s + 1) * TILE].rearrange("p (k n) -> p k n", k=KD) for s in range(2)]
        ring_hi = [EB_r[0][:, s * TILE:(s + 1) * TILE].rearrange("p (k n) -> p k n", k=KD) for s in range(2)]
        hT_hi = H_r[:, :].rearrange("p (k n) -> p k n", k=KD)
        hT_lo = EB_r[0][:, 2 * TILE:3 * TILE].rearrange("p (k n) -> p k n", k=KD)
        spare = EB[1][:, 2 * TILE:3 * TILE]
        ws_raw = spare[:, 0:D].rearrange("p (g s) -> p g s", g=SG)
        wsT = spare[:, D:2 * D].rearrange("p (g s) -> p g s", g=SG)
        bs_bc = spare[:, 2 * D:3 * D].rearrange("p (g s) -> p g s", g=SG)
        vg = EB[2][:, 0:2 * TILE].rearrange("p (t n) -> p t n", t=NT)
        wsTs = EB[2][:, 2 * TILE:3 * TILE].rearrange("p (t g s) -> p t g s", t=NT, g=SG)
        vg_hi = EB_r[2][:, 0:2 * TILE].rearrange("p (t n) -> p t n", t=NT)
        vg_lo = [EB_r[b][:, 2 * TILE:3 * TILE].rearrange("p (t n) -> p t n", t=NT) for b in (2, 1)]
        KT = EB[2][:, 0:TILE].rearrange("p (c n) -> p c n", c=PAIRS)
        QT = EB[2][:, TILE:2 * TILE].rearrange("p (c n) -> p c n", c=PAIRS)
        V = EB[2][:, 2 * TILE:3 * TILE].rearrange("p (t n) -> p t n", t=NT)
        GT = spare.rearrange("p (c n) -> p c n", c=PAIRS)
        GT_hi = EB_r[1][:, 2 * TILE:3 * TILE].rearrange("p (c n) -> p c n", c=PAIRS)
        GT_lo = EB_r[2][:, TILE:2 * TILE].rearrange("p (c n) -> p c n", c=PAIRS)
        y_got = EB[2][:, 0:2 * TILE].rearrange("p (i n) -> p i n", i=2 * NT)

        PT = EB[0][:, 2 * TILE:3 * TILE].rearrange("p (h b n) -> p h b n", h=2, b=NT)

        def scr(a, b):
            return SCR[:, a:b]

        hrow = [scr(s * D, (s + 1) * D).rearrange("p (k q) -> p k q", k=KD) for s in range(2)]
        junk = scr(4 * D, 5 * D)
        b_v = [scr(2 * D + s * COL, 2 * D + (s + 1) * COL) for s in range(2)]
        u_tmp = [scr(3 * D + s * COL, 3 * D + (s + 1) * COL) for s in range(2)]
        kn = [scr(2 * D + s * COL, 2 * D + (s + 1) * COL) for s in range(2)]
        sq = [scr(3 * D + s * COL, 3 * D + (s + 1) * COL) for s in range(2)]
        Pr = scr(0, 6 * COL).rearrange("p (b h n) -> p b h n", b=3, h=2)
        nck = scr(6 * COL, 10 * COL).rearrange("p (b h n) -> p b h n", b=2, h=2)
        hTc = [scr(s * D, (s + 1) * D).rearrange("p (k q) -> p k q", k=KD) for s in range(2)]
        xg = scr(0, COL)
        xT = scr(COL, 2 * COL).rearrange("p (k c) -> p k c", k=KD)
        hid = scr(2 * COL, 3 * COL)
        silu = scr(3 * COL, 4 * COL)
        ysb = scr(4 * COL, 5 * COL)
        eqs = scr(5 * COL, 6 * COL).rearrange("p (k c j) -> p k c j", k=2, c=NT)
        hidT = scr(6 * COL, 6 * COL + 256).rearrange("p (k c) -> p k c", k=KE)
        S = scr(6 * COL + 256, 7 * COL).rearrange("p (c j) -> p c j", c=NT)
        at = [7 * COL]

        def route(n):
            at[0] += n
            assert at[0] <= 5 * D
            return scr(at[0] - n, at[0])

        lg = route(NT * NR).rearrange("p (t n) -> p t n", t=NT)
        el = route(NT * NE).rearrange("p (t n) -> p t n", t=NT)
        oh = [route(NT * NE).rearrange("p (t n) -> p t n", t=NT) for _ in range(2)]
        cand = route(NT * NE).rearrange("p (t n) -> p t n", t=NT)
        msum = route(NT * NE).rearrange("p (t n) -> p t n", t=NT)
        ohg = route(NT * NG).rearrange("p (t n) -> p t n", t=NT)
        pen = route(NT * NG).rearrange("p (t n) -> p t n", t=NT)
        cntb = route(P)
        item_tmp = route(3 * NBASE).rearrange("p (a n) -> p a n", a=3)
        cmp7 = route(8)

        col = sb("col", [P, 64])
        gmax, gmin, gsum, m1, m2, mmin, dexp = (col[:, 4 * i:4 * i + 4] for i in range(7))
        cn = col[:, 28:30]
        s0n0 = col[:, 30:32]
        pb = col[:, 32:40]
        gw = col[:, 40:44]
        w12 = sb("w12", [P, 8])
        pos = sb("pos", [P, 8])
        pos_i = sb("pos_i", [P, 8], I32)
        base_f = sb("base_f", [P, NBASE])
        base_i = sb("base_i", [1, NBASE + 2], I32)
        n0_i = sb("n0_i", [1, NE + 2], I32)
        ss = sb("ss", [P, NT])
        rms = sb("rms", [P, NT])
        rinv = sb("rinv", [P, NT])
        vss = sb("vss", [P, NT, 4])
        hss = sb("hss", [P, 2, 8])
        hr = sb("hr", [P, 2, 8])
        nmx = sb("nmx", [P, 3, 2])
        rsum = sb("rsum", [P, 3, 2])
        rrec = sb("rrec", [P, 3, 2])
        eps = sb("eps", [P, 1])
        cols_raw = sb("cols_raw", [2 * NC + 2, P])
        cols = sb("cols", [P, 2 * NC + 2])
        b_u, v_gain, kq_gain = cols[:, 0:NC], cols[:, NC:2 * NC], cols[:, 2 * NC:2 * NC + 2]
        wf = sb("wf", [P, KD, HEADS])
        bf_bc = sb("bf_bc", [P, HEADS])
        lf = sb("lf", [P, 3, NT * HEADS])
        wr = sb("wr", [P, KD, NR])
        br = sb("br", [P, NR])
        ident = sb("ident", [P, P])
        tri = sb("tri", [P, P])
        tri_in = sb("tri_in", [P, P])
        ones = sb("ones", [P, P])
        ident_b = sb("ident_b", [P, P], BF16)
        mask_b = sb("mask_b", [P, P], BF16)
        iota_m = sb("iota_m", [P, NE])
        iota_c = sb("iota_c", [P, CAP])
        thr7 = sb("thr7", [P, 8])

        ps = [ctx.enter_context(nc.psum_tensor(f"ps{i}", [P, COL], F32)) for i in range(8)]

        const_made = sem("const_made")
        const_ready = sem("const_ready")
        x_loaded = sems("x_loaded", NT)
        small_loaded = sem("small_loaded")
        col_loaded = sem("col_loaded")
        bv_loaded = sems("bv_loaded", 2)
        tile_loaded = sems("tile_loaded", 2)
        w_hi = sem("w_hi")
        w_lo = sem("w_lo")
        h_lo = sem("h_lo")
        acc_ready = sem("acc_ready")
        dve_step = sem("dve_step")
        act_step = sem("act_step")
        norm = {}
        for n in ("a", "m0", "kv", "b", "m1"):
            norm[n] = {k: sem(f"{n}_{k}") for k in ("gain", "rms", "hrow", "tr", "ht")}
        z_ready = sem("z_ready")
        v_ready = sem("v_ready")
        vr_ready = sem("vr_ready")
        wst_done = sem("wst_done")
        wst_ready = sem("wst_ready")
        wsts_ready = sem("wsts_ready")
        mix_done = sems("mix_done", 2)
        mix_free = sems("mix_free", 2)
        u_ready = sem("u_ready")
        gated = sem("gated")
        out_done = sem("out_done")
        x_mixed = sem("x_mixed")
        route_exp_in = sem("route_exp_in")
        route_exp = sem("route_exp")
        moe = []
        for l in range(2):
            moe.append({k: sem(f"moe{l}_{k}") for k in (
                "router_loaded", "logits", "lists_in", "lists_out", "tables", "sel", "up", "silu", "hid", "gath", "xg", "hidT_tr", "hidT",
                "xT_tr", "xT", "down", "y_out", "y_stored", "y_complete", "combined", "step")})
            moe[l]["w13"] = sems(f"moe{l}_w13_", NBUF)
            moe[l]["w2"] = sems(f"moe{l}_w2_", NBUF)
            moe[l]["y_got"] = sems(f"moe{l}_y_got", NT)
        v_out = sem("v_out")
        g_done = sem("g_done")
        g_out = sem("g_out")
        sq_ready = sem("sq_ready")
        hss_ready = sem("hss_ready")
        hrms_ready = sem("hrms_ready")
        kn_ready = sem("kn_ready")
        kn_tr = sem("kn_tr")
        kn_out = sem("kn_out")
        f_done = sem("f_done")
        f_ready = sem("f_ready")
        f_ln = sem("f_ln")
        lf_ready = sem("lf_ready")
        cum_done = sem("cum_done")
        cum_ready = sem("cum_ready")
        cumT_done = sem("cumT_done")
        ncum_ready = sem("ncum_ready")
        ncum_stored = sem("ncum_stored")
        nck_loaded = sems("nck_loaded", 2)
        s_done = sem("s_done")
        s_max = sem("s_max")
        p_exp = sem("p_exp")
        p_ready = sem("p_ready")
        pt_tr = sem("pt_tr")
        pt_out = sems("pt_out", 2)
        o_done = sem("o_done")
        o_gated = sem("o_gated")
        x_attn = sem("x_attn")
        stored = sem("stored")

        def rows_pk(w, c0):
            return w.rearrange("(p k) n -> p k n", k=KD)[:, :, c0:c0 + COL]

        def rows_cp(w, c, c0):
            return w[c * KD * P:(c + 1) * KD * P, c0:c0 + COL].rearrange("(k p) n -> p k n", p=P)

        tiles = [rows_pk(a_w_in[0], WIDTH + COL * i) for i in range(4)]
        tiles += [rows_pk(a_w_in[0], COL * i) for i in range(4)]
        tiles += [rows_cp(a_w_out[0], c, COL * n) for n in range(2) for c in range(2)]
        tiles += [rows_pk(kv_w, COL * i) for i in range(4)]
        tiles += [rows_pk(b_w_qg[0], COL * i) for i in range(4)]
        tiles += [rows_cp(b_w_out[0], 0, COL * n) for n in range(2)]
        T_V, T_U, T_O, T_K, T_VV, T_Q, T_G, T_WO = 0, 4, 8, 12, 14, 16, 18, 20
        G_V, G_U, G_K, G_VV, G_Q, G_WO = 0, 16, 32, 40, 48, 56

        def split_no(i):
            return i if i < T_G else i - (T_WO - T_G)

        H_LO = {"a": 0, "kv": 2 * NT, "b": 4 * NT}
        H_BACK = 6 * NT
        TURN = {"a": 3, "kv": 3, "b": 2}

        def turn_bank(n, t, h):
            return ps[2 + 2 * (t % TURN[n]) + h]

        def slot(e):
            return (e + 1) % NBUF

        block = ctx.enter_context(nc.Block())

        @block.sync
        def _(sp):
            def load_tile(i):
                if i >= 2:
                    j = i - 2
                    if T_O <= j < T_K:
                        sp.wait_ge(out_done, 4 * (j - T_O + 1))
                    elif j >= T_G:
                        sp.wait_ge(g_done, 4 * (j - T_G + 1))
                    else:
                        groups = 4 * (j + 1 if j < T_O else j + 1 - (T_K - T_O))
                        sp.wait_ge(acc_ready, groups)
                sp.dma_start(ring[i % 2], tiles[i]).then_inc(tile_loaded[i % 2], 16)

            def load_expert(l, e, w1=True, rest=True):
                m, s = moe[l], slot(e)
                if w1:
                    sp.dma_start(w1_sb[s], m_w1[l, e].rearrange("(p k) n -> p k n", k=KD)).then_inc(m["w13"][s], 16)
                if rest:
                    sp.dma_start(w3_sb[s], m_w3[l, e].rearrange("(p k) n -> p k n", k=KD)).then_inc(m["w13"][s], 16)
                    sp.dma_start(w2_sb[s], m_w2[l, e].rearrange("(p k) n -> p k n", k=KE)).then_inc(m["w2"][s], 16)

            def load_later_expert(l, e, s):
                m = moe[l]
                ended = sp.value_load(n0_i[0:1, bass.ds(e - (NBUF - 1), 1)], min_val=1, max_val=MAX_ITEMS)
                sp.wait_ge(m["up"], ended)
                w1e = m_w1[l][bass.ds(e, 1), :, :].rearrange("a (p k) n -> p (a k) n", k=KD)
                w3e = m_w3[l][bass.ds(e, 1), :, :].rearrange("a (p k) n -> p (a k) n", k=KD)
                w2e = m_w2[l][bass.ds(e, 1), :, :].rearrange("a (p k) n -> p (a k) n", k=KE)
                sp.dma_start(w1_sb[s], w1e).then_inc(m["w13"][s], 16)
                sp.dma_start(w3_sb[s], w3e).then_inc(m["w13"][s], 16)
                sp.wait_ge(m["down"], ended)
                sp.dma_start(w2_sb[s], w2e).then_inc(m["w2"][s], 16)

            def moe_loads(l):
                m = moe[l]
                load_expert(l, 0, w1=False)
                load_expert(l, 1)
                load_expert(l, 2)
                sp.wait_ge(m["tables"], 2)
                with sp.Fori(1, NE // NBUF) as r:
                    for s in range(NBUF):
                        load_later_expert(l, r * NBUF + s, slot(s))
                for e in range(NE // NBUF * NBUF, NE):
                    load_later_expert(l, e, slot(e))

            for t in range(NT):
                sp.dma_start(X[:, t, :], x_in[0, t * P:(t + 1) * P, :]).then_inc(x_loaded[t], 16)
            load_tile(0)
            load_tile(1)
            for i in range(2, T_K):
                load_tile(i)
            sp.wait_ge(out_done, 12)
            load_expert(0, 0, rest=False)
            sp.wait_ge(out_done, 16)
            moe_loads(0)
            ended = sp.value_load(n0_i[0:1, NE - 1:NE], min_val=1, max_val=MAX_ITEMS)
            sp.wait_ge(moe[0]["up"], ended)
            for i in range(T_K, T_K + 2):
                sp.dma_start(ring[i % 2], tiles[i]).then_inc(tile_loaded[i % 2], 16)
            for i in range(T_K + 2, len(tiles)):
                load_tile(i)
            sp.wait_ge(acc_ready, G_WO + 4)
            load_expert(1, 0, rest=False)
            sp.wait_ge(acc_ready, G_WO + 8)
            moe_loads(1)
            for t in range(NT):
                sp.wait_ge(moe[1]["combined"], 2 * t + 2)
                sp.dma_start(out[0, t * P:(t + 1) * P, :], X[:, t, :]).then_inc(stored, 16)
            sp.wait_ge(stored, 16 * NT)

        @block.gpsimd
        def _(pool):
            g = nc.gpsimd
            made = [0]

            def make(ins):
                made[0] += 1
                ins.then_inc(const_made, 1)

            make(g.memset(ident[:, :], 0.0))
            make(g.memset(tri[:, :], 1.0))
            make(g.memset(tri_in[:, :], 1.0))
            make(g.memset(ones[:, :], 1.0))
            make(g.memset(ident_b[:, :], 0.0))
            make(g.memset(mask_b[:, :], 0.0))
            make(g.memset(eps[:, :], EPS))
            make(g.iota(iota_m[:, :], pattern=[[1, NE]], base=-64, channel_multiplier=0,
                        allow_small_or_imprecise_dtypes=True))
            make(g.iota(iota_c[:, :], pattern=[[1, CAP]], base=0, channel_multiplier=0,
                        allow_small_or_imprecise_dtypes=True))
            make(g.iota(thr7[:, :], pattern=[[CAP, 8]], base=CAP, channel_multiplier=0,
                        allow_small_or_imprecise_dtypes=True))
            pool.wait_ge(const_made, made[0])
            for m in (ident, ident_b):
                g.affine_select(out=m[:, :], in_=m[:, :], compare_op=ALU.not_equal, fill=1.0, base=0,
                                pattern=[[-1, P]], channel_multiplier=1).then_inc(const_ready, 1)
            g.affine_select(out=tri[:, :], in_=tri[:, :], compare_op=ALU.is_ge, fill=0.0, base=-1,
                            pattern=[[1, P]], channel_multiplier=-1).then_inc(const_ready, 1)
            g.affine_select(out=tri_in[:, :], in_=tri_in[:, :], compare_op=ALU.is_ge, fill=0.0, base=0,
                            pattern=[[1, P]], channel_multiplier=-1).then_inc(const_ready, 1)
            g.affine_select(out=mask_b[:, :], in_=mask_b[:, :], compare_op=ALU.is_ge, fill=-BIG, base=0,
                            pattern=[[-1, P]], channel_multiplier=1).then_inc(const_ready, 1)

            def load_gain(n, src):
                pool.dma_start(gain[:, :], src.partition_broadcast(P)).then_inc(norm[n]["gain"], 16)

            def load_router(l):
                m = moe[l]
                pool.dma_start(wr[:, :, 0:NG], m_w_group[l].rearrange("(p k) n -> p k n", k=KD))\
                    .then_inc(m["router_loaded"], 16)
                pool.dma_start(wr[:, :, NG:NR], m_w_expert[l].rearrange("(p k) n -> p k n", k=KD))\
                    .then_inc(m["router_loaded"], 16)
                pool.dma_start(br[:, 0:NG], m_b_group[l].partition_broadcast(P)).then_inc(m["router_loaded"], 16)
                pool.dma_start(br[:, NG:NR], m_b_expert[l].partition_broadcast(P)).then_inc(m["router_loaded"], 16)

            def gather_outputs(l):
                m = moe[l]
                pool.wait_ge(m["y_complete"], 1)
                for t in range(NT):
                    for k in range(2):
                        g.indirect_dma_start(
                            out=y_got[:, 2 * t + k, :], out_offset=None, in_=y_rows[l][0:SLOTS, :],
                            in_offset=bass.IndirectOffsetOnAxis(ap=pos_i[:, 4 * k + t:4 * k + t + 1], axis=0),
                        ).then_inc(m["y_got"][t], 16)

            pool.dma_start(ws_raw, a_w_s[0].rearrange("g t s -> t g s")).then_inc(small_loaded, 16)
            pool.dma_start(spare[:, 2 * D:3 * D], a_b_s[0].rearrange("g t -> (g t)").partition_broadcast(P))\
                .then_inc(small_loaded, 16)
            for c, src in enumerate((a_b_in[0, 0:WIDTH], a_v_norm[0])):
                pool.dma_start(cols_raw[c * NC:(c + 1) * NC, :], src.rearrange("(c p) -> c p", p=P))\
                    .then_inc(col_loaded, 16)
            for i, src in enumerate((k_norm, q_norm[0])):
                for h in range(2):
                    pool.dma_start(cols_raw[2 * NC + i:2 * NC + i + 1, h * DH:(h + 1) * DH],
                                   src.rearrange("(a p) -> a p", a=1)).then_inc(col_loaded, 16)
            pool.dma_start(wf[:, :, :], kv_w.rearrange("(p k) n -> p k n", k=KD)[:, :, 2 * D:2 * D + HEADS])\
                .then_inc(col_loaded, 16)
            pool.dma_start(bf_bc[:, :], kv_b_f.partition_broadcast(P)).then_inc(col_loaded, 16)
            for i in range(4):
                if i >= 2:
                    pool.wait_ge(z_ready, 4 * (i - 1) + 1)
                pool.dma_start(b_v[i % 2], a_b_in[0, WIDTH + COL * i:WIDTH + COL * (i + 1)].partition_broadcast(P))\
                    .then_inc(bv_loaded[i % 2], 16)
            load_router(0)
            pool.wait_ge(norm["a"]["hrow"], NT)
            load_gain("m0", m_norm[0])
            pool.wait_ge(norm["m0"]["hrow"], NT)
            load_gain("kv", kv_norm)
            pool.wait_ge(moe[0]["lists_in"], 1)
            load_router(1)
            gather_outputs(0)
            pool.wait_ge(norm["kv"]["hrow"], NT)
            load_gain("b", b_norm[0])
            pool.wait_ge(norm["b"]["hrow"], NT)
            load_gain("m1", m_norm[1])

            gather_outputs(1)

        @block.scalar
        def _(act):
            a = nc.scalar
            done = [0]

            def then(ins):
                done[0] += 1
                ins.then_inc(act_step, 1)
                act.wait_ge(act_step, done[0])

            def stats(n, ready):
                for t in range(NT):
                    act.wait_ge(*ready(t))
                    then(a.activation(junk, X[:, t, :], ACT.Square, accum_out=ss[:, t:t + 1]))
                    a.activation(rms[:, t:t + 1], ss[:, t:t + 1], ACT.Sqrt, bias=eps[:, :], scale=1.0 / D)\
                        .then_inc(norm[n]["rms"], 1)

            def transposed_rows(n, after_first=None):
                for t in range(NT):
                    if t == 1 and after_first is not None:
                        after_first()
                    for h in range(2):
                        act.wait_ge(norm[n]["tr"], 2 * t + h + 1)
                        a.activation(hT_hi[:, 4 * h:4 * h + 4, t * P:(t + 1) * P],
                                     turn_bank(n, t, h)[:, :].rearrange("p (k n) -> p k n", k=4), ACT.Copy)\
                            .then_inc(norm[n]["ht"], 1)

            def split_hi(j, loads, q0=0, q1=4):
                act.wait_ge(tile_loaded[j], 16 * loads)
                for q in range(q0, q1):
                    a.activation(ring_hi[j][:, 2 * q:2 * q + 2, :], ring[j][:, 2 * q:2 * q + 2, :], ACT.Copy)\
                        .then_inc(w_hi, 1)

            def split_tile(i, q0=0, q1=4):
                split_hi(i % 2, i // 2 + 1, q0, q1)

            def moe_act(l, ready):
                m = moe[l]
                stats(f"m{l}", ready)
                for t in range(NT):
                    if t >= 2:
                        act.wait_ge(m["logits"], t - 1)
                    for h in range(2):
                        act.wait_ge(norm[f"m{l}"]["tr"], 2 * t + h + 1)
                        a.activation(hTc[t % 2][:, 4 * h:4 * h + 4, :],
                                     ps[2 + h][:, :].rearrange("p (k n) -> p k n", k=4), ACT.Copy)\
                            .then_inc(norm[f"m{l}"]["ht"], 1)
                act.wait_ge(route_exp_in, 2 * l + 1)
                a.activation(ohg, ohg, ACT.Exp).then_inc(route_exp, 1)
                act.wait_ge(route_exp_in, 2 * l + 2)
                a.activation(dexp, dexp, ACT.Exp).then_inc(route_exp, 1)
                act.wait_ge(m["tables"], 3)
                total = act.value_load(n0_i[0:1, NE:NE + 1], min_val=1, max_val=MAX_ITEMS)
                a.activation(junk[:, 0:1], eps[:, :], ACT.Copy).then_inc(m["y_out"], 1)
                a.activation(junk[:, 1:2], eps[:, :], ACT.Copy).then_inc(m["y_stored"], 1)
                with act.Fori(0, total) as n:
                    act.wait_ge(m["up"], n + 1)
                    a.activation(silu[CAP:P, :], ps[0][0:CAP, :], ACT.Silu).then_inc(m["silu"], 1)
                    base = act.value_load(base_i[0:1, bass.ds(n, 1)], min_val=0, max_val=SLOTS)
                    act.wait_ge(m["down"], n + 1)
                    act.wait_ge(m["y_stored"], 32 * n + 1)
                    a.activation(ysb, ps[4][:, :], ACT.Copy).then_inc(m["y_out"], 1)
                    act.wait_ge(m["y_out"], n + 2)
                    for h in range(2):
                        act.dma_start(y_rows[l][bass.ds(base, CAP), h * COL:(h + 1) * COL],
                                      ysb[h * CAP:(h + 1) * CAP, :]).then_inc(m["y_stored"], 16)
                act.wait_ge(m["y_stored"], 32 * total + 1)
                a.activation(junk[:, 0:1], eps[:, :], ACT.Copy).then_inc(m["y_complete"], 1)

            act.dma_start(gain[:, :], a_norm[0].partition_broadcast(P)).then_inc(norm["a"]["gain"], 16)
            act.wait_ge(const_ready, 5)
            stats("a", lambda t: (x_loaded[t], 16))
            transposed_rows("a", lambda: split_tile(0))
            with act.Fori(0, 2) as r:
                for j in range(2):
                    for t in range(NT):
                        act.wait_ge(z_ready, 8 * r + 4 * j + t + 2)
                        v_t = vg[:, t, bass.ds(r * 2 * COL + j * COL, COL)]
                        a.activation(v_t, v_t, ACT.Gelu_apprx_tanh).then_inc(v_ready, 1)
                        act.wait_ge(v_ready, 8 * r + 4 * j + t + 1)
                        a.activation(junk[:, 0:COL], v_t, ACT.Square,
                                     accum_out=vss[:, t, bass.ds(r * 2 + j, 1)]).then_inc(vr_ready, 1)
                        if t == 0:
                            split_hi(1 - j, r + 1 + j)
            act.wait_ge(wsts_ready, 1)
            then(a.activation(rms[:, :], ss[:, :], ACT.Sqrt, bias=eps[:, :], scale=1.0 / WIDTH))
            a.activation(junk[:, 0:1], rms[:, 0:1], ACT.Copy).then_inc(vr_ready, 1)
            act.wait_ge(wst_ready, 2)
            for c in range(NC):
                g = G_U + c
                act.wait_ge(acc_ready, g + 1)
                if c >= 2:
                    act.wait_ge(gated, c - 1)
                a.activation(u_tmp[c % 2], ps[g % 2][:, :], ACT.Gelu_apprx_tanh, bias=b_u[:, c:c + 1])\
                    .then_inc(u_ready, 1)
                if c % 4 == 1:
                    split_tile(T_U + c // 4 + 1)
            for i in range(T_O + 1, T_K):
                split_tile(i)
            moe_act(0, lambda t: (x_mixed, 4 + t + 1))

            split_tile(T_K)
            stats("kv", lambda t: (moe[0]["combined"], 2 * t + 2))
            transposed_rows("kv")

            def head_norms(r, g0, gain_col, dst, splits):
                for j in range(8):
                    g, q = g0 + j, 8 * r + j
                    act.wait_ge(acc_ready, g + 1)
                    if q >= 2:
                        act.wait_ge(hss_ready, q - 1)
                    a.activation(sq[q % 2], ps[g % 2][:, :], ACT.Square).then_inc(sq_ready, 1)
                    act.wait_ge(hss_ready, q + 1)
                    a.activation(hr[:, q % 2, :], hss[:, q % 2, :], ACT.Sqrt, bias=eps[:, :], scale=1.0 / DH)\
                        .then_inc(hrms_ready, 1)
                    if j >= 1:
                        put_heads(r, j - 1, gain_col, dst)
                    if j in splits:
                        split_tile(splits[j])
                put_heads(r, 7, gain_col, dst)

            def put_heads(r, j, gain_col, dst):
                q = 8 * r + j
                t, c = j % NT, 4 * (j // NT)
                act.wait_ge(kn_tr, q + 1)
                a.activation(dst[:, c:c + 4, t * P:(t + 1) * P],
                             ps[4 + q % 2][:, :].rearrange("p (c n) -> p c n", c=4), ACT.Copy,
                             scale=kq_gain[:, gain_col:gain_col + 1]).then_inc(kn_out, 1)

            head_norms(0, G_K, 0, KT, {0: T_K + 1, 5: T_VV})
            split_tile(T_VV + 1)
            split_tile(T_Q)
            act.wait_ge(f_ready, 1)
            then(a.activation(lf[:, 1, :], lf[:, 0, :], ACT.Abs))
            then(a.activation(lf[:, 1, :], lf[:, 1, :], ACT.Exp, scale=-1.0))
            a.activation(lf[:, 1, :], lf[:, 1, :], ACT.Ln, bias=1.0).then_inc(f_ln, 1)
            transposed_rows("b")
            act.wait_ge(cumT_done, 1)
            a.activation(junk[0:HEADS, 0:T], ps[6][0:HEADS, :], ACT.Copy, scale=-1.0).then_inc(ncum_ready, 1)
            act.wait_ge(ncum_ready, 1)
            act.dma_start(ncum_rows, junk[0:HEADS, 0:T]).then_inc(ncum_stored, 16)
            head_norms(1, G_Q, 1, QT, {1: T_Q + 1})
            def load_nck(c):
                for h in range(2):
                    act.dma_start(nck[:, c % 2, h, :], ncum_rows[2 * c + h].partition_broadcast(P))\
                        .then_inc(nck_loaded[c % 2], 16)

            act.wait_ge(ncum_stored, 16)
            act.wait_ge(kn_out, 16)
            load_nck(0)
            load_nck(1)
            for u in range(PAIRS * NT + 2):
                if u >= NT and u % NT == 0:
                    c = u // NT - 1
                    act.wait_ge(g_done, c + 1)
                    a.activation(GT[:, c, :], ps[7][:, :], ACT.Tanh, scale=0.5).then_inc(g_out, 1)
                if u < PAIRS * NT:
                    w = (u % NT + 1) * P
                    for h in range(2):
                        act.wait_ge(s_max, 2 * u + h + 1)
                        a.activation(Pr[:, u % 3, h, 0:w], Pr[:, u % 3, h, 0:w], ACT.Exp, scale=-1.0,
                                     bias=nmx[:, u % 3, h:h + 1],
                                     accum_out=rsum[:, u % 3, h:h + 1]).then_inc(p_exp, 1)
                    if u % NT == NT - 1 and u // NT + 2 < PAIRS:
                        load_nck(u // NT + 2)
                q = u - (PAIRS // 2 * NT + 2)
                if 0 <= q < 4:
                    split_tile(T_WO, q, q + 1)
                if u >= 2:
                    v = u - 2
                    i = v % NT
                    act.wait_ge(pt_tr, 2 * v + 2)
                    a.activation(PT[:, 1, 0:i + 1, i * P:(i + 1) * P],
                                 ps[5][:, 0:(i + 1) * P].rearrange("p (b n) -> p b n", n=P), ACT.Copy)\
                        .then_inc(pt_out[1], 1)
            split_tile(T_WO + 1)
            moe_act(1, lambda t: (x_attn, 4 + t + 1))

        @block.vector
        def _(dve):
            v = nc.vector
            done = [0]

            def then(ins):
                done[0] += 1
                ins.then_inc(dve_step, 1)
                dve.wait_ge(dve_step, done[0])

            def scaled_rows(n, dst, stats=True, combine=None):
                m = norm[n]
                dve.wait_ge(m["gain"], 16)
                for t in range(NT):
                    if combine is not None:
                        combine(t)
                    if stats:
                        dve.wait_ge(m["rms"], t + 1)
                        then(v.reciprocal(rinv[:, t:t + 1], rms[:, t:t + 1]))
                    if dst is hrow and t >= 2:
                        dve.wait_ge(m["tr"], 2 * t - 2)
                    to = hrow[t % 2] if dst is hrow else h_tok[:, t]
                    v.scalar_tensor_tensor(to, X[:, t, :].rearrange("p (q k) -> p k q", k=KD), rinv[:, t:t + 1],
                                           gain[:, :].rearrange("p (q k) -> p k q", k=KD), ALU.mult, ALU.mult)\
                        .then_inc(m["hrow"], 1)

            def rows_lo(n, t):
                for h in range(2):
                    dve.wait_ge(norm[n]["ht"], 2 * t + h + 1)
                    v.tensor_tensor(hT_lo[:, 4 * h:4 * h + 4, t * P:(t + 1) * P],
                                    turn_bank(n, t, h)[:, :].rearrange("p (k n) -> p k n", k=4),
                                    hT_hi[:, 4 * h:4 * h + 4, t * P:(t + 1) * P].bitcast(F32), ALU.subtract).then_inc(h_lo, 1)

            def split_lo(j, number, q0=0, q1=4):
                for q in range(q0, q1):
                    dve.wait_ge(w_hi, 4 * number + q + 1)
                    v.tensor_tensor(ring_lo[j][:, 2 * q:2 * q + 2, :], ring[j][:, 2 * q:2 * q + 2, :],
                                    ring_hi[j][:, 2 * q:2 * q + 2, :].bitcast(F32), ALU.subtract).then_inc(w_lo, 1)

            def split_tile(i, q0=0, q1=4):
                split_lo(i % 2, split_no(i), q0, q1)

            def bc(ap, n):
                return ap.unsqueeze(2).to_broadcast([P, NT, n])

            def over_t(ap, n):
                return ap.unsqueeze(1).to_broadcast([P, NT, n])

            def first_of_max(vals, top, n, onehot):
                then(v.tensor_reduce(top, vals, AX, ALU.max))
                then(v.tensor_tensor(cand[:, :, 0:n], vals, bc(top, n), ALU.is_equal))
                then(v.tensor_tensor(cand[:, :, 0:n], cand[:, :, 0:n], over_t(iota_m[:, 0:n], n), ALU.mult))
                then(v.tensor_reduce(mmin, cand[:, :, 0:n], AX, ALU.min))
                then(v.tensor_tensor(onehot, over_t(iota_m[:, 0:n], n), bc(mmin, n), ALU.is_equal))

            def select(n, m, k, link):
                link(v.tensor_scalar(pb, pos[:, :], base_f[:, bass.ds(n, 1)], None, ALU.subtract), 1)
                link(v.tensor_tensor(eqs.rearrange("p k c j -> p (k c) j"),
                                     pb.unsqueeze(2).to_broadcast([P, 8, CAP]),
                                     iota_c[:, :].unsqueeze(1).to_broadcast([P, 8, CAP]), ALU.is_equal), 2)
                v.tensor_tensor(S, eqs[:, 0], eqs[:, 1], ALU.add).then_inc(m["sel"], 1)

            def moe_dve(l):
                m = moe[l]
                scaled_rows(f"m{l}", h_tok)
                dve.wait_ge(m["router_loaded"], 64)
                dve.wait_ge(m["logits"], NT)
                then(v.tensor_tensor(lg, ps[4][:, 0:NT * NR].rearrange("p (t n) -> p t n", t=NT),
                                     over_t(br[:, :], NR), ALU.add))
                glog = lg[:, :, 0:NG]
                first_of_max(glog, gmax, NG, pen)
                then(v.tensor_scalar(pen, pen, BIG, -BIG, ALU.mult, ALU.add))
                v.tensor_tensor(ohg, glog, bc(gmax, NG), ALU.subtract).then_inc(route_exp_in, 1)
                then(v.tensor_tensor(el.rearrange("p t (g e) -> p t g e", g=NG),
                                     lg[:, :, NG:NR].rearrange("p t (g e) -> p t g e", g=NG),
                                     pen.unsqueeze(3).to_broadcast([P, NT, NG, EPG]), ALU.add))
                first_of_max(el, m1, NE, oh[0])
                then(v.scalar_tensor_tensor(el, oh[0], -2.0 * BIG, el, ALU.mult, ALU.add))
                first_of_max(el, m2, NE, oh[1])
                v.tensor_tensor(dexp, m2, m1, ALU.subtract).then_inc(route_exp_in, 1)
                v.tensor_tensor(msum, oh[0], oh[1], ALU.add).then_inc(m["lists_in"], 1)
                dve.wait_ge(route_exp, 2 * l + 2)
                then(v.tensor_reduce(gsum, ohg, AX, ALU.add))
                then(v.tensor_scalar(m1, dexp, 1.0, None, ALU.add))
                then(v.tensor_tensor(m1, m1, gsum, ALU.mult))
                then(v.reciprocal(w12[:, 0:4], m1))
                v.tensor_tensor(w12[:, 4:8], w12[:, 0:4], dexp, ALU.mult).then_inc(m["step"], 1)
                dve.wait_ge(m["step"], 1)
                dve.wait_ge(m["lists_out"], 1)
                then(v.tensor_copy(cn[0:NE, 0:1], ps[6][0:NE, 0:1]))
                then(v.tensor_tensor(cmp7[0:NE, 0:7], thr7[0:NE, 0:7], cn[0:NE, 0:1].to_broadcast([NE, 7]), ALU.is_lt))
                then(v.tensor_reduce(cn[0:NE, 1:2], cmp7[0:NE, 0:7], AX, ALU.add))
                then(v.tensor_scalar(cn[0:NE, 1:2], cn[0:NE, 1:2], 1.0, None, ALU.add))
                v.tensor_scalar(cntb[0:NE, :], ones[0:NE, :], cn[0:NE, 0:1], None, ALU.mult).then_inc(m["lists_in"], 1)
                dve.wait_ge(m["lists_out"], 2)
                then(v.tensor_copy(s0n0[0:NE, :], ps[6][0:NE, 4:6]))
                it = item_tmp[0:NE]
                then(v.tensor_scalar(it[:, 0, :], iota_c[0:NE, 0:NBASE], s0n0[0:NE, 1:2], None, ALU.subtract))
                then(v.tensor_scalar(it[:, 1, :], it[:, 0, :], float(CAP), s0n0[0:NE, 0:1], ALU.mult, ALU.add))
                then(v.tensor_scalar(it[:, 2, :], it[:, 0, :], cn[0:NE, 1:2], None, ALU.is_lt))
                then(v.tensor_tensor(it[:, 1, :], it[:, 1, :], it[:, 2, :], ALU.mult))
                then(v.tensor_scalar(it[:, 2, :], it[:, 0, :], 0.0, None, ALU.is_ge))
                v.tensor_tensor(it[:, 1, :], it[:, 1, :], it[:, 2, :], ALU.mult).then_inc(m["lists_in"], 1)
                for k in range(2):
                    then(v.tensor_tensor(cand, oh[k], ps[5][:, 0:NT * NE].rearrange("p (t n) -> p t n", t=NT),
                                         ALU.mult))
                    then(v.tensor_reduce(pos[:, 4 * k:4 * k + 4], cand, AX, ALU.add))
                v.tensor_copy(pos_i[:, :], pos[:, :]).then_inc(m["tables"], 1)
                v.tensor_copy(n0_i[0:1, 0:NE + 1], ps[6][0:1, 8:8 + NE + 1]).then_inc(m["tables"], 1)
                dve.wait_ge(m["lists_out"], 3)
                then(v.tensor_copy(base_f[:, :], ps[7][:, 0:NBASE]))
                v.tensor_copy(base_i[0:1, 0:NBASE], base_f[0:1, :]).then_inc(m["tables"], 1)
                dve.wait_ge(m["tables"], 3)
                total = dve.value_load(n0_i[0:1, NE:NE + 1], min_val=1, max_val=MAX_ITEMS)
                v.memset(hid[CAP:P, :], 0.0)
                select(0, m, 0, lambda ins, k: then(ins))
                dve.wait_ge(m["gath"], 1)
                v.tensor_copy(xg, ps[1][:, :]).then_inc(m["xg"], 1)
                dve.wait_ge(m["xT_tr"], 1)
                v.tensor_copy(xT.rearrange("p (h j) c -> p j h c", h=2),
                              ps[3][:, :].rearrange("p (j h c) -> p j h c", j=4, h=2)).then_inc(m["xT"], 1)
                select(1, m, 0, lambda ins, k: then(ins))
                with dve.Fori(0, total) as n:
                    dve.wait_ge(m["silu"], n + 1)
                    v.tensor_tensor(hid[0:CAP, :], silu[CAP:P, :], ps[0][CAP:P, :], ALU.mult).then_inc(m["hid"], 1)
                    dve.wait_ge(m["gath"], n + 2)
                    v.tensor_copy(xg, ps[1][:, :]).then_inc(m["xg"], 1)
                    dve.wait_ge(m["hidT_tr"], n + 1)
                    v.tensor_copy(hidT, ps[2][:, :].rearrange("p (k c) -> p k c", k=KE)[:, :, 0:CAP])\
                        .then_inc(m["hidT"], 1)
                    dve.wait_ge(m["xT_tr"], n + 2)
                    v.tensor_copy(xT.rearrange("p (h j) c -> p j h c", h=2),
                                  ps[3][:, :].rearrange("p (j h c) -> p j h c", j=4, h=2)).then_inc(m["xT"], 1)

                    def link(ins, k):
                        ins.then_inc(m["step"], 1)
                        dve.wait_ge(m["step"], 2 * n + k + 1)

                    select(n + 2, m, 0, link)

            def combine(l, t):
                m = moe[l]
                dve.wait_ge(m["y_got"][t], 32)
                for k in range(2):
                    v.scalar_tensor_tensor(X[:, t, :], y_got[:, 2 * t + k, :], w12[:, 4 * k + t:4 * k + t + 1],
                                           X[:, t, :], ALU.mult, ALU.add).then_inc(m["combined"], 1)
                    dve.wait_ge(m["combined"], 2 * t + k + 1)

            dve.wait_ge(const_ready, 5)
            scaled_rows("a", hrow)
            rows_lo("a", 0)
            split_tile(0)
            for t in range(1, NT):
                rows_lo("a", t)
            v.memset(vss[:, :, :], 0.0).then_inc(z_ready, 1)
            with dve.Fori(0, 2) as r:
                for j in range(2):
                    dve.wait_ge(bv_loaded[j], 16 * (r + 1))
                    for t in range(NT):
                        b = t % 2
                        dve.wait_ge(acc_ready, 8 * r + 4 * j + t + 1)
                        v.tensor_tensor(vg[:, t, bass.ds(r * 2 * COL + j * COL, COL)], ps[b][:, :], b_v[j], ALU.add)\
                            .then_inc(z_ready, 1)
                        if t == 1:
                            split_lo(1 - j, 2 * r + j + 1)
            dve.wait_ge(wst_done, 3)
            for h in range(2):
                then(v.tensor_copy(wsT[:, 4 * h:4 * h + 4, :], ps[4 + h][:, :].rearrange("p (g s) -> p g s", g=4)))
            v.memset(wsT[P // 2:P, :, 0:P // 2], 0.0).then_inc(wst_ready, 1)
            v.tensor_copy(cols[:, :], ps[6][:, 0:2 * NC + 2]).then_inc(wst_ready, 1)
            dve.wait_ge(vr_ready, 16)
            v.tensor_reduce(ss[:, :], vss[:, :, :], AX, ALU.add).then_inc(wsts_ready, 1)
            dve.wait_ge(vr_ready, 17)
            then(v.reciprocal(rinv[:, :], rms[:, :]))
            dve.wait_ge(wst_ready, 2)
            for t in range(NT):
                v.tensor_scalar(wsTs[:, t], wsT, rinv[:, t:t + 1], None, ALU.mult).then_inc(wsts_ready, 1)
            split_tile(T_U + 1)
            dve.wait_ge(small_loaded, 32)
            for c in range(NC):
                dve.wait_ge(mix_done[c % 2], c // 2 + 1)
                v.scalar_tensor_tensor(vg[:, :, c * P:(c + 1) * P], ps[4 + c % 2][:, :].rearrange("p (t n) -> p t n", t=NT),
                                       v_gain[:, c:c + 1], over_t(bs_bc[:, c // 2, :], P), ALU.mult, ALU.add)\
                    .then_inc(mix_free[c % 2], 1)
            for c in range(NC):
                dve.wait_ge(u_ready, c + 1)
                dve.wait_ge(mix_free[c % 2], c // 2 + 1)
                u3 = u_tmp[c % 2].rearrange("p (t n) -> p t n", t=NT)
                vg_c = vg[:, :, c * P:(c + 1) * P]
                then(v.tensor_tensor(u3, vg_c, u3, ALU.mult))
                hi = vg_hi[:, :, c * P:(c + 1) * P]
                then(v.tensor_copy(hi, u3))
                v.tensor_tensor(vg_lo[c // 8][:, :, c % 8 * P:(c % 8 + 1) * P], u3, hi.bitcast(F32), ALU.subtract)\
                    .then_inc(gated, 1)
                if c % 4 == 1 and c >= 4:
                    split_tile(T_U + c // 4 + 1)
            split_tile(T_O + 1)
            split_tile(T_O + 2)
            for n in range(2):
                if n == 1:
                    split_tile(T_O + 3)
                for t in range(NT):
                    dve.wait_ge(out_done, 8 * n + 4 + t + 1)
                    v.tensor_tensor(X[:, t, n * COL:(n + 1) * COL], X[:, t, n * COL:(n + 1) * COL], ps[4 + t][:, :],
                                    ALU.add).then_inc(x_mixed, 1)
            moe_dve(0)

            split_tile(T_K)
            combine(0, 0)
            scaled_rows("kv", hrow, combine=lambda t: combine(0, t + 1) if t + 1 < NT else None)
            for t in range(NT):
                rows_lo("kv", t)

            def head_norms(r, g0, splits):
                for j in range(8):
                    g, q = g0 + j, 8 * r + j
                    dve.wait_ge(sq_ready, q + 1)
                    v.tensor_reduce(hss[:, q % 2, :], sq[q % 2].rearrange("p (h d) -> p h d", h=8), AX, ALU.add)\
                        .then_inc(hss_ready, 1)
                    dve.wait_ge(hrms_ready, q + 1)
                    then(v.reciprocal(hr[:, q % 2, :], hr[:, q % 2, :]))
                    if q >= 2:
                        dve.wait_ge(kn_tr, q - 1)
                    v.tensor_tensor(kn[q % 2].rearrange("p (h d) -> p h d", h=8),
                                    ps[g % 2][:, :].rearrange("p (h d) -> p h d", h=8),
                                    hr[:, q % 2, :].unsqueeze(2).to_broadcast([P, 8, DH]), ALU.mult)\
                        .then_inc(kn_ready, 1)
                    if j in splits:
                        split_tile(splits[j])

            head_norms(0, G_K, {0: T_K + 1, 5: T_VV})
            for j in range(8):
                g = G_VV + j
                dve.wait_ge(acc_ready, g + 1)
                v.tensor_copy(V[:, j % NT, (j // NT) * COL:(j // NT + 1) * COL], ps[g % 2][:, :])\
                    .then_inc(v_out, 1)
                if j % 4 == 1:
                    split_tile(T_VV + j // 4 + 1)
            dve.wait_ge(f_done, 1)
            f3 = lf[:, 0, :].rearrange("p (t n) -> p t n", t=NT)
            v.tensor_tensor(f3, ps[6][:, 0:NT * HEADS].rearrange("p (t n) -> p t n", t=NT),
                            over_t(bf_bc[:, :], HEADS), ALU.add).then_inc(f_ready, 1)
            dve.wait_ge(f_ready, 1)
            then(v.tensor_scalar(lf[:, 2, :], lf[:, 0, :], 0.0, None, ALU.min))
            scaled_rows("b", hrow, stats=False, combine=lambda t: rows_lo("b", 0) if t == NT - 1 else None)
            for t in range(1, NT):
                rows_lo("b", t)
            dve.wait_ge(f_ln, 1)
            v.tensor_tensor(lf[:, 0, :], lf[:, 2, :], lf[:, 1, :], ALU.subtract).then_inc(lf_ready, 1)
            dve.wait_ge(cum_done, 1)
            v.tensor_copy(lf[:, 1, :], ps[7][:, 0:NT * HEADS]).then_inc(cum_ready, 1)
            then(v.tensor_scalar(kq_gain[:, 1:2], kq_gain[:, 1:2], DH ** -0.5, None, ALU.mult))
            head_norms(1, G_Q, {1: T_Q + 1})
            n_units = PAIRS * NT
            for u in range(n_units + 3):
                if u < n_units:
                    i, c = u % NT, u // NT
                    w = (i + 1) * P
                    if c == 0:
                        dve.wait_ge(acc_ready, G_Q + 8)
                        v.tensor_tensor(hT[:, 2 * i:2 * i + 2, :], hT_hi[:, 2 * i:2 * i + 2, :].bitcast(F32),
                                        hT_lo[:, 2 * i:2 * i + 2, :].bitcast(F32), ALU.add).then_inc(h_lo, 1)
                    if i == 0:
                        dve.wait_ge(nck_loaded[c % 2], 32 * (c // 2 + 1))
                    for h in range(2):
                        dve.wait_ge(s_done, 2 * u + h + 1)
                        if u >= 3:
                            dve.wait_ge(pt_tr, 2 * (u - 3) + h + 1)
                        v.tensor_tensor_reduce(out=Pr[:, u % 3, h, 0:w], in0=ps[2 * (u % 2) + h][:, 0:w],
                                               in1=nck[:, c % 2, h, 0:w], scale=-1.0, scalar=BIG, op0=ALU.add,
                                               op1=ALU.min, accum_out=nmx[:, u % 3, h:h + 1]).then_inc(s_max, 1)
                q = u - (PAIRS // 2 * NT + 3)
                if 0 <= q < 4:
                    split_tile(T_WO, q, q + 1)
                if 1 <= u <= n_units:
                    q = u - 1
                    dve.wait_ge(p_exp, 2 * q + 2)
                    then(v.reciprocal(rrec[:, q % 3, :], rsum[:, q % 3, :]))
                    w = (q % NT + 1) * P
                    for h in range(2):
                        v.tensor_scalar(Pr[:, q % 3, h, 0:w], Pr[:, q % 3, h, 0:w], rrec[:, q % 3, h:h + 1], 0.5,
                                        ALU.mult, ALU.mult).then_inc(p_ready, 1)
                if 2 <= u <= n_units + 1:
                    q = u - 2
                    i = q % NT
                    dve.wait_ge(pt_tr, 2 * q + 1)
                    v.tensor_copy(PT[:, 0, 0:i + 1, i * P:(i + 1) * P],
                                  ps[4][:, 0:(i + 1) * P].rearrange("p (b n) -> p b n", n=P)).then_inc(pt_out[0], 1)
                if u >= 3 and (u - 3) % NT == NT - 1:
                    c = (u - 3) // NT
                    dve.wait_ge(o_done, c + 1)
                    dve.wait_ge(g_out, c + 1)
                    then(v.scalar_tensor_tensor(QT[:, c, :], GT[:, c, :], 1.0, ps[6][:, :], ALU.add, ALU.mult))
                    then(v.tensor_copy(GT_hi[:, c, :], QT[:, c, :]))
                    v.tensor_tensor(GT_lo[:, c, :], QT[:, c, :], GT_hi[:, c, :].bitcast(F32), ALU.subtract).then_inc(o_gated, 1)
            for j in range(8):
                g, t, n = G_WO + j, j % NT, j // NT
                dve.wait_ge(acc_ready, g + 1)
                v.tensor_tensor(X[:, t, n * COL:(n + 1) * COL], X[:, t, n * COL:(n + 1) * COL], ps[g % 2][:, :],
                                ALU.add).then_inc(x_attn, 1)
                if j == 0:
                    split_tile(T_WO + 1)
            moe_dve(1)
            for t in range(NT):
                combine(1, t)

        @block.tensor
        def _(pe):
            mm = nc.tensor.matmul

            def split_product(o, left, right, start, stop):
                mm(o, left[0], right[0], start=start, stop=False)
                mm(o, left[0], right[1], start=False, stop=False)
                return mm(o, left[1], right[0], start=False, stop=stop)

            def h_part(k, t=None):
                at_t = slice(0, T) if t is None else slice(t * P, (t + 1) * P)
                return hT_hi[:, k, at_t], hT_lo[:, k, at_t]

            def w_part(j, k, a=0, b=COL):
                return ring_hi[j][:, k, a:b], ring_lo[j][:, k, a:b]

            def wait_split(i):
                pe.wait_ge(w_lo, 4 * split_no(i) + 4)

            def transpose_dense_rows(n, t):
                pe.wait_ge(norm[n]["hrow"], t + 1)
                for h in range(2):
                    if t >= TURN[n]:
                        pe.wait_ge(h_lo, H_LO[n] + 2 * (t - TURN[n]) + h + 1)
                    for j in range(4):
                        last = nc.tensor.transpose(turn_bank(n, t, h)[:, j * P:(j + 1) * P],
                                                   hrow[t % 2][:, 4 * h + j, :], ident[:, :])
                    last.then_inc(norm[n]["tr"], 1)

            def transpose_rows(n, t, rows):
                m = norm[n]
                pe.wait_ge(m["hrow"], t + 1)
                for h in range(2):
                    if t >= 1:
                        pe.wait_ge(m["ht"], 2 * (t - 1) + h + 1)
                    for j in range(4):
                        last = nc.tensor.transpose(ps[2 + h][:, j * P:(j + 1) * P], rows[:, 4 * h + j, :], ident[:, :])
                    last.then_inc(m["tr"], 1)

            def project(i, g0, bank_free):
                wait_split(i)
                for t in range(NT):
                    g = g0 + t
                    bank_free(g)
                    for k in range(KD):
                        last = split_product(ps[g % 2][:, :], h_part(k, t), w_part(i % 2, k), k == 0, k == KD - 1)
                    last.then_inc(acc_ready, 1)

            def project_transposed(i, g0, bank_free):
                wait_split(i)
                for j in range(4):
                    g = g0 + j
                    bank_free(g)
                    for k in range(KD):
                        last = split_product(ps[g % 2][:, :], w_part(i % 2, k, j * P, (j + 1) * P), h_part(k),
                                             k == 0, k == KD - 1)
                    last.then_inc(acc_ready, 1)

            def moe_pe(l):
                m = moe[l]

                def logits(t):
                    pe.wait_ge(norm[f"m{l}"]["ht"], 2 * t + 2)
                    for k in range(KD):
                        last = mm(ps[4][:, t * NR:(t + 1) * NR], hTc[t % 2][:, k, :], wr[:, k, :],
                                  start=k == 0, stop=k == KD - 1)
                    last.then_inc(m["logits"], 1)

                pe.wait_ge(m["router_loaded"], 64)
                for t in range(NT):
                    transpose_rows(f"m{l}", t, h_tok[:, t])
                    if t >= 1:
                        logits(t - 1)
                logits(NT - 1)
                pe.wait_ge(m["lists_in"], 1)
                for c in range(NT):
                    last = mm(ps[6][0:NE, 0:1], msum[:, c, :], ones[:, 0:1], start=c == 0, stop=c == NT - 1)
                last.then_inc(m["lists_out"], 1)
                pe.wait_ge(m["lists_in"], 2)
                mm(ps[6][0:NE, 4:6], tri[0:NE, 0:NE], cn[0:NE, :], start=True, stop=True)
                mm(ps[6][0:1, 8:8 + NE + 1], cn[0:NE, 1:2], tri[0:NE, 0:NE + 1], start=True, stop=True)
                for c in range(NT):
                    rk = ps[5][:, c * NE:(c + 1) * NE]
                    mm(rk, tri[:, :], msum[:, c, :], start=True, stop=False)
                    for b in range(c):
                        mm(rk, ones[:, :], msum[:, b, :], start=False, stop=False)
                    last = mm(rk, cntb[0:NE, :], tri[0:NE, 0:NE], start=False, stop=True)
                last.then_inc(m["lists_out"], 1)
                pe.wait_ge(m["lists_in"], 3)
                mm(ps[7][:, 0:NBASE], ones[0:NE, :], item_tmp[0:NE, 1, :], start=True, stop=True)\
                    .then_inc(m["lists_out"], 1)

                def gather(n):
                    pe.wait_ge(m["sel"], n + 1)
                    for c in range(NT):
                        for h in range(2):
                            last = mm(ps[1][h * CAP:(h + 1) * CAP, :], S[:, c, :],
                                      H[:, c * D + h * COL:c * D + (h + 1) * COL], start=c == 0, stop=c == NT - 1)
                    last.then_inc(m["gath"], 1)

                def transpose_item(n):
                    pe.wait_ge(m["xg"], n + 1)
                    for j in range(4):
                        last = nc.tensor.transpose(ps[3][:, j * P:(j + 1) * P], xg[:, j * P:(j + 1) * P], ident[:, :])
                    last.then_inc(m["xT_tr"], 1)

                def expert(s, loads, r0, r1):
                    with pe.Fori(r0, r1) as n:
                        pe.wait_ge(m["w13"][s], 32 * loads)
                        pe.wait_ge(m["xT"], n + 1)
                        for k in range(KD):
                            for h, w in enumerate((w1_sb[s], w3_sb[s])):
                                last = mm(ps[0][h * CAP:(h + 1) * CAP, :], xT[:, k, :], w[:, k, :],
                                          start=k == 0, stop=k == KD - 1)
                        last.then_inc(m["up"], 1)
                        gather(n + 1)
                        pe.wait_ge(m["hid"], n + 1)
                        for k in range(KE):
                            last = nc.tensor.transpose(ps[2][:, k * P:(k + 1) * P], hid[:, k:DE:KE], ident[:, :])
                        last.then_inc(m["hidT_tr"], 1)
                        transpose_item(n + 1)
                        pe.wait_ge(m["hidT"], n + 1)
                        pe.wait_ge(m["w2"][s], 16 * loads)
                        pe.wait_ge(m["y_out"], n + 1)
                        for k in range(KE):
                            for h in range(2):
                                last = mm(ps[4][h * CAP:(h + 1) * CAP, :], hidT[:, k, :],
                                          w2_sb[s][:, k, h * COL:(h + 1) * COL], start=k == 0, stop=k == KE - 1)
                        last.then_inc(m["down"], 1)

                def items_of(e):
                    return (pe.value_load(n0_i[0:1, bass.ds(e, 1)], min_val=0, max_val=MAX_ITEMS - 1),
                            pe.value_load(n0_i[0:1, bass.ds(e + 1, 1)], min_val=1, max_val=MAX_ITEMS))

                pe.wait_ge(m["tables"], 3)
                gather(0)
                transpose_item(0)
                with pe.Fori(0, NE // NBUF) as r:
                    for s in range(NBUF):
                        expert(slot(s), r + 1, *items_of(r * NBUF + s))
                for e in range(NE // NBUF * NBUF, NE):
                    expert(slot(e), e // NBUF + 1, *items_of(e))

            pe.wait_ge(const_ready, 5)
            for t in range(NT):
                transpose_dense_rows("a", t)
            with pe.Fori(0, 2) as r:
                for j in range(2):
                    pe.wait_ge(w_lo, 8 * r + 4 * j + 4)
                    for t in range(NT):
                        b = t % 2
                        pe.wait_ge(h_lo, 2 * t + 2)
                        pe.wait_ge(z_ready, 8 * r + max(4 * j + t - 1, 0) + 1)
                        for k in range(KD):
                            last = split_product(ps[b][:, :], h_part(k, t), w_part(j, k), k == 0, k == KD - 1)
                        last.then_inc(acc_ready, 1)
            pe.wait_ge(small_loaded, 32)
            for h in range(2):
                for j in range(4):
                    last = nc.tensor.transpose(ps[4 + h][:, j * P:(j + 1) * P], ws_raw[:, 4 * h + j, :], ident[:, :])
                last.then_inc(wst_done, 1)
            pe.wait_ge(col_loaded, 16 * 8)
            nc.tensor.transpose(ps[6][:, 0:2 * NC + 2], cols_raw[:, :], ident[0:2 * NC + 2, 0:2 * NC + 2])\
                .then_inc(wst_done, 1)
            def free_u(g):
                c = g - G_U
                pe.wait_ge(*((z_ready, 16 + c) if c < 2 else (u_ready, c - 1)))

            for i in range(4):
                project_transposed(T_U + i, G_U + 4 * i, free_u)
                if i == 0:
                    pe.wait_ge(wsts_ready, 5)
                    for c in range(NC):
                        pe.wait_ge(mix_free[c % 2], c // 2)
                        for t in range(NT):
                            last = mm(ps[4 + c % 2][:, t * P:(t + 1) * P], vg[:, t, c * P:(c + 1) * P],
                                      wsTs[:, t, c // 2, :], start=True, stop=True)
                        last.then_inc(mix_done[c % 2], 1)
            for n in range(2):
                for c in range(2):
                    i = T_O + 2 * n + c
                    wait_split(i)
                    pe.wait_ge(gated, 8 * (c + 1))
                    for t in range(NT):
                        if n == 1 and c == 0:
                            pe.wait_ge(x_mixed, t + 1)
                        for k in range(KD):
                            kc = 8 * c + k
                            last = split_product(ps[4 + t][:, :], (vg_hi[:, t, kc * P:(kc + 1) * P],
                                                                   vg_lo[c][:, t, k * P:(k + 1) * P]),
                                                 w_part(i % 2, k), c == 0 and k == 0, c == 1 and k == KD - 1)
                        last.then_inc(out_done, 1)
            moe_pe(0)

            for t in range(NT):
                transpose_dense_rows("kv", t)

            def turn_heads(q):
                pe.wait_ge(kn_ready, q + 1)
                if q >= 2:
                    pe.wait_ge(kn_out, q - 1)
                for c in range(4):
                    last = nc.tensor.transpose(ps[4 + q % 2][:, c * P:(c + 1) * P], kn[q % 2][:, c * P:(c + 1) * P],
                                               ident[:, :])
                last.then_inc(kn_tr, 1)

            def project_heads(n, i0, g0, r, bank_free):
                for i in range(2):
                    wait_split(i0 + i)
                    for t in range(NT):
                        g = g0 + 4 * i + t
                        bank_free(g)
                        if i == 0:
                            pe.wait_ge(h_lo, H_LO[n] + 2 * t + 2)
                        for k in range(KD):
                            last = split_product(ps[g % 2][:, :], h_part(k, t), w_part((i0 + i) % 2, k),
                                                 k == 0, k == KD - 1)
                        last.then_inc(acc_ready, 1)
                        if 4 * i + t >= 1:
                            turn_heads(8 * r + 4 * i + t - 1)

            def free_k(g):
                if g - G_K >= 2:
                    pe.wait_ge(kn_ready, g - G_K - 1)

            def free_vv(g):
                j = g - G_VV
                pe.wait_ge(*((kn_ready, 7 + j) if j < 2 else (v_out, j - 1)))

            def free_q(g):
                j = g - G_Q
                pe.wait_ge(*((v_out, 7 + j) if j < 2 else (kn_ready, 8 + j - 1)))

            project_heads("kv", T_K, G_K, 0, free_k)
            for t in range(NT):
                for k in range(KD):
                    for part, h in enumerate(h_part(k, t)):
                        last = mm(ps[6][:, t * HEADS:(t + 1) * HEADS], h.bitcast(F32), wf[:, k, :],
                                  start=k == 0 and part == 0, stop=k == KD - 1 and part == 1)
            last.then_inc(f_done, 1)
            turn_heads(7)
            project(T_VV, G_VV, free_vv)
            project(T_VV + 1, G_VV + 4, free_vv)
            pe.wait_ge(kn_out, 8)
            for t in range(NT):
                transpose_dense_rows("b", t)
            pe.wait_ge(lf_ready, 1)
            for c in range(NT):
                o = ps[7][:, c * HEADS:(c + 1) * HEADS]
                for b in range(c):
                    mm(o, ones[:, :], lf[:, 0, b * HEADS:(b + 1) * HEADS], start=b == 0, stop=False)
                last = mm(o, tri_in[:, :], lf[:, 0, c * HEADS:(c + 1) * HEADS], start=c == 0, stop=True)
            last.then_inc(cum_done, 1)
            pe.wait_ge(cum_ready, 1)
            for c in range(NT):
                last = nc.tensor.transpose(ps[6][0:HEADS, c * P:(c + 1) * P], lf[:, 1, c * HEADS:(c + 1) * HEADS],
                                           ident[:, :])
            last.then_inc(cumT_done, 1)
            project_heads("b", T_Q, G_Q, 1, free_q)
            turn_heads(15)

            pe.wait_ge(kn_out, 16)
            n_units = PAIRS * NT
            for u in range(n_units + 2):
                if u < n_units:
                    i, c = u % NT, u // NT
                    w = (i + 1) * P
                    if u >= 2:
                        pe.wait_ge(s_max, 2 * (u - 2) + 2)
                    for h in range(2):
                        mm(ps[2 * (u % 2) + h][:, 0:w], QT[h * DH:(h + 1) * DH, c, i * P:(i + 1) * P],
                           KT[h * DH:(h + 1) * DH, c, 0:w], start=True, stop=False)
                    for h in range(2):
                        mm(ps[2 * (u % 2) + h][:, i * P:w], ident_b[:, :], mask_b[:, :], start=False, stop=True)\
                            .then_inc(s_done, 1)
                    j = T_G + c // 4
                    if i == 0:
                        pe.wait_ge(tile_loaded[j % 2], 16 * (j // 2 + 1))
                        if c >= 1:
                            pe.wait_ge(g_out, c)
                    if c == 0:
                        pe.wait_ge(h_lo, H_BACK + i + 1)
                    for k in range(2 * i, 2 * i + 2):
                        last = mm(ps[7][:, :], ring[j % 2][:, k, c % 4 * P:(c % 4 + 1) * P], hT[:, k, :],
                                  start=k == 0, stop=k == KD - 1)
                    if i == NT - 1:
                        last.then_inc(g_done, 1)
                if u >= 2:
                    q = u - 2
                    i, c = q % NT, q // NT
                    for h in range(2):
                        pe.wait_ge(p_ready, 2 * q + h + 1)
                        pe.wait_ge(pt_out[h], q)
                        for b in range(i + 1):
                            last = nc.tensor.transpose(ps[4 + h][:, b * P:(b + 1) * P],
                                                       Pr[:, q % 3, h, b * P:(b + 1) * P], ident[:, :])
                        last.then_inc(pt_tr, 1)
                    if i == NT - 1:
                        pe.wait_ge(pt_out[0], q + 1)
                        pe.wait_ge(pt_out[1], q + 1)
                        if c >= 1:
                            pe.wait_ge(o_gated, c)
                        for b in range(NT):
                            for h in range(2):
                                last = mm(ps[6][h * DH:(h + 1) * DH, b * P:T],
                                          V[:, b, (2 * c + h) * DH:(2 * c + h + 1) * DH], PT[:, h, b, b * P:T],
                                          start=b == 0, stop=b == NT - 1)
                        last.then_inc(o_done, 1)
            pe.wait_ge(o_gated, PAIRS)
            for n in range(2):
                i = T_WO + n
                wait_split(i)
                for t in range(NT):
                    g = G_WO + 4 * n + t
                    if 4 * n + t >= 2:
                        pe.wait_ge(x_attn, 4 * n + t - 1)
                    for c in range(PAIRS):
                        last = split_product(ps[g % 2][:, :], (GT_hi[:, c, t * P:(t + 1) * P],
                                                               GT_lo[:, c, t * P:(t + 1) * P]),
                                             w_part(i % 2, c), c == 0, c == PAIRS - 1)
                    last.then_inc(acc_ready, 1)
            moe_pe(1)


_INS = ["x", "a_norm", "a_w_in", "a_b_in", "a_v_norm", "a_w_s", "a_b_s", "a_w_out", "kv_norm", "kv_w", "kv_b_f",
        "k_norm", "b_norm", "b_w_qg", "q_norm", "b_w_out", "m_norm", "m_w_group", "m_b_group", "m_w_expert",
        "m_b_expert", "m_w1", "m_w3", "m_w2"]


def kernel(**inputs):
    import numpy as np
    import concourse.bacc as bacc
    from concourse.bass_utils import run_bass_kernel_spmd

    nc = bacc.Bacc("TRN2", target_bir_lowering=False, num_devices=1)
    arrays, args = {}, []
    for name in _INS:
        a = np.ascontiguousarray(inputs[name])
        arrays[f"in_{name}"] = a
        args.append(nc.dram_tensor(f"in_{name}", a.shape, mybir.dt.from_np(a.dtype), kind="ExternalInput").ap())
    args.append(nc.dram_tensor("out_x", (1, T, D), F32, kind="ExternalOutput").ap())
    trunk(nc, *args)
    r = run_bass_kernel_spmd(nc, [arrays], core_ids=[0])
    return r.results[0]["out_x"]
```

```python
from contextlib import ExitStack

import concourse.bass as bass
from concourse import mybir

F32 = mybir.dt.float32
I32 = mybir.dt.int32
BF16 = mybir.dt.bfloat16
F32R = mybir.dt.float32r
ALU = mybir.AluOpType
ACT = mybir.ActivationFunctionType
AX = mybir.AxisListType.X

P = 128
D = 1024
T = 512
NT = T // P
KD = D // P
EPS = 1e-6
WIDTH = 2 * D
NC = WIDTH // P
SG = 8
HEADS = 16
PAIRS = HEADS // 2
DH = D // HEADS
NG = 4
EPG = 8
NE = NG * EPG
DE = D // 2
KE = DE // P
NR = NG + NE
CAP = 64
SLOTS = 2 * T
MAX_ITEMS = SLOTS // CAP + NE
N_BASE = MAX_ITEMS + 2
Y_ROWS = MAX_ITEMS * CAP
NBUF = 3
COL = 512
HALF = P // 2
BIG = 1e30


def trunk(nc, x_in, a_norm, a_w_in, a_b_in, a_v_norm, a_w_s, a_b_s, a_w_out, kv_norm, kv_w, kv_b_f, k_norm,
          b_norm, b_w_qg, q_norm, b_w_out, m_norm, m_w_group, m_b_group, m_w_expert, m_b_expert,
          m_w1, m_w3, m_w2, out):
    with ExitStack() as ctx:
        def sb(name, shape, dt=F32):
            return ctx.enter_context(nc.sbuf_tensor(name, shape, dt))

        def sem(name):
            return ctx.enter_context(nc.semaphore(name))

        def sems(name, n):
            return [sem(f"{name}{i}") for i in range(n)]

        y_rows = nc.dram_tensor("y_rows", (Y_ROWS, D), F32, kind="Internal").ap()
        ncum_rows = nc.dram_tensor("ncum_rows", (HEADS, T), F32, kind="Internal").ap()

        def sb_split(name, shape):
            place = -(-nc.sbuf_base // 32) * 32
            full = sb(name, shape)
            return full, nc.alloc_sbuf_tensor_at(name + "_r", shape, F32R, offset=place)

        X = sb("X", [P, NT, D])
        H, H_r = sb_split("H", [P, NT * D])
        EB, EB_r = zip(*[sb_split(f"EB{s}", [P, 3 * KD * COL]) for s in range(NBUF)])
        SCR = sb("SCR", [P, 5 * D])
        gain = sb("gain", [P, D])

        h_tok = H[:, :].rearrange("p (t k q) -> p t k q", t=NT, k=KD)
        hT = H[:, :].rearrange("p (k n) -> p k n", k=KD)
        TILE = KD * COL
        w1_sb = [EB[s][:, 0:TILE].rearrange("p (k n) -> p k n", k=KD) for s in range(NBUF)]
        w3_sb = [EB[s][:, TILE:2 * TILE].rearrange("p (k n) -> p k n", k=KD) for s in range(NBUF)]
        w2_sb = [EB[s][:, 2 * TILE:3 * TILE].rearrange("p (k n) -> p k n", k=KE) for s in range(NBUF)]
        ring = [EB[1][:, s * TILE:(s + 1) * TILE].rearrange("p (k n) -> p k n", k=KD) for s in range(2)]
        ring_lo = [EB_r[1][:, s * TILE:(s + 1) * TILE].rearrange("p (k n) -> p k n", k=KD) for s in range(2)]
        ring_hi = [EB_r[0][:, s * TILE:(s + 1) * TILE].rearrange("p (k n) -> p k n", k=KD) for s in range(2)]
        hT_hi = H_r[:, :].rearrange("p (k n) -> p k n", k=KD)
        hT_lo = EB_r[0][:, 2 * TILE:3 * TILE].rearrange("p (k n) -> p k n", k=KD)
        spare = EB[1][:, 2 * TILE:3 * TILE]
        ws_raw = spare[:, 0:D].rearrange("p (g s) -> p g s", g=SG)
        wsT = spare[:, D:2 * D].rearrange("p (g s) -> p g s", g=SG)
        bs_bc = spare[:, 2 * D:3 * D].rearrange("p (g s) -> p g s", g=SG)
        vg = EB[2][:, 0:2 * TILE].rearrange("p (t n) -> p t n", t=NT)
        wsTs = EB[2][:, 2 * TILE:3 * TILE].rearrange("p (t g s) -> p t g s", t=NT, g=SG)
        vg_hi = EB_r[2][:, 0:2 * TILE].rearrange("p (t n) -> p t n", t=NT)
        vg_lo = [EB_r[b][:, 2 * TILE:3 * TILE].rearrange("p (t n) -> p t n", t=NT) for b in (2, 1)]
        KT = EB[2][:, 0:TILE].rearrange("p (c n) -> p c n", c=PAIRS)
        QT = EB[2][:, TILE:2 * TILE].rearrange("p (c n) -> p c n", c=PAIRS)
        V = EB[2][:, 2 * TILE:3 * TILE].rearrange("p (t n) -> p t n", t=NT)
        GT = spare.rearrange("p (c n) -> p c n", c=PAIRS)
        GT_hi = EB_r[1][:, 2 * TILE:3 * TILE].rearrange("p (c n) -> p c n", c=PAIRS)
        GT_lo = EB_r[2][:, TILE:2 * TILE].rearrange("p (c n) -> p c n", c=PAIRS)
        y_got = EB[2][:, 0:2 * TILE].rearrange("p (i n) -> p i n", i=2 * NT)

        PT = EB[0][:, 2 * TILE:3 * TILE].rearrange("p (h b n) -> p h b n", h=2, b=NT)

        def scr(a, b):
            return SCR[:, a:b]

        hrow = [scr(s * D, (s + 1) * D).rearrange("p (k q) -> p k q", k=KD) for s in range(2)]
        junk = scr(4 * D, 5 * D)
        b_v = [scr(2 * D + s * COL, 2 * D + (s + 1) * COL) for s in range(2)]
        u_tmp = [scr(s * COL, (s + 1) * COL) for s in range(4)]
        kn = [scr(2 * D + s * COL, 2 * D + (s + 1) * COL) for s in range(2)]
        sq = [scr(3 * D + s * COL, 3 * D + (s + 1) * COL) for s in range(2)]
        Pr = scr(0, 6 * COL).rearrange("p (b h n) -> p b h n", b=3, h=2)
        nck = scr(6 * COL, 10 * COL).rearrange("p (b h n) -> p b h n", b=2, h=2)
        hTc = [scr(s * D, (s + 1) * D).rearrange("p (k q) -> p k q", k=KD) for s in range(2)]
        xg = scr(0, COL)
        xT = scr(COL, 2 * COL).rearrange("p (k c) -> p k c", k=KD)
        hid = scr(2 * COL, 3 * COL)
        silu = scr(3 * COL, 4 * COL)
        eqs = scr(4 * COL, 5 * COL).rearrange("p (k c j) -> p k c j", k=2, c=NT)
        hidT = scr(5 * COL, 5 * COL + 256).rearrange("p (k c) -> p k c", k=KE)
        S = scr(5 * COL + 256, 6 * COL).rearrange("p (c j) -> p c j", c=NT)
        ysb = scr(6 * COL, 10 * COL)
        at = [6 * COL]

        def route(n):
            at[0] += n
            assert at[0] <= 5 * D
            return scr(at[0] - n, at[0])

        lg = route(NT * NR).rearrange("p (t n) -> p t n", t=NT)
        el = route(NT * NE).rearrange("p (t n) -> p t n", t=NT)
        both = route(2 * NT * NE).rearrange("p (k t n) -> p k t n", k=2, t=NT)
        oh = [both[:, k] for k in range(2)]
        cand = route(NT * NE).rearrange("p (t n) -> p t n", t=NT)
        msum = route(NT * NE).rearrange("p (t n) -> p t n", t=NT)
        ohg = route(NT * NG).rearrange("p (t n) -> p t n", t=NT)
        pen = route(NT * NG).rearrange("p (t n) -> p t n", t=NT)
        cntb = route(P)
        cmp7 = route(8)

        col = sb("col", [P, 64])
        gmax, gmin, gsum, m1, m2, mmin, dexp = (col[:, 4 * i:4 * i + 4] for i in range(7))
        cn = col[:, 28:30]
        pb = col[:, 32:40]
        gw = col[:, 40:44]
        w12 = sb("w12", [P, 8])
        pos = sb("pos", [P, 8])
        pos_i = sb("pos_i", [P, 8], I32)
        item_slot = sb("item_slot", [P, N_BASE])
        n0_i = sb("n0_i", [1, NE + 2], I32)
        ss = sb("ss", [P, NT])
        rms = sb("rms", [P, NT])
        rinv = sb("rinv", [P, NT])
        vss = sb("vss", [P, NT, 4])
        hss = sb("hss", [P, 2, 8])
        hr = sb("hr", [P, 2, 8])
        nmx = sb("nmx", [P, 3, 2])
        rsum = sb("rsum", [P, 3, 2])
        rrec = sb("rrec", [P, 3, 2])
        eps = sb("eps", [P, 1])
        cols_raw = sb("cols_raw", [2 * NC + 2, P])
        cols = sb("cols", [P, 2 * NC + 2])
        b_u, v_gain, kq_gain = cols[:, 0:NC], cols[:, NC:2 * NC], cols[:, 2 * NC:2 * NC + 2]
        wf = sb("wf", [P, KD, HEADS])
        bf_bc = sb("bf_bc", [P, HEADS])
        lf = sb("lf", [P, 3, NT * HEADS])
        wr = sb("wr", [P, KD, NR])
        br = sb("br", [P, NR])
        ident = sb("ident", [P, P])
        tri = sb("tri", [P, P])
        tri_in = sb("tri_in", [P, P])
        ones = sb("ones", [P, P])
        ident_b = sb("ident_b", [P, P], BF16)
        mask_b = sb("mask_b", [P, P], BF16)
        iota_m = sb("iota_m", [P, NE])
        iota_c = sb("iota_c", [P, CAP])
        thr7 = sb("thr7", [P, 8])

        ps = [ctx.enter_context(nc.psum_tensor(f"ps{i}", [P, COL], F32)) for i in range(8)]

        const_made = sem("const_made")
        const_ready = sem("const_ready")
        x_loaded = sems("x_loaded", NT)
        y_filled = sem("y_filled")
        small_loaded = sem("small_loaded")
        col_loaded = sem("col_loaded")
        bv_loaded = sems("bv_loaded", 2)
        tile_loaded = sems("tile_loaded", 2)
        w_hi = sem("w_hi")
        w_lo = sem("w_lo")
        h_lo = sem("h_lo")
        acc_ready = sem("acc_ready")
        dve_step = sem("dve_step")
        act_step = sem("act_step")
        norm = {}
        for n in ("a", "m0", "kv", "b", "m1"):
            norm[n] = {k: sem(f"{n}_{k}") for k in ("gain", "rms", "hrow", "tr", "ht")}
        z_ready = sem("z_ready")
        v_ready = sem("v_ready")
        vr_ready = sem("vr_ready")
        wst_done = sem("wst_done")
        wst_ready = sem("wst_ready")
        wsts_ready = sem("wsts_ready")
        mix_done = sems("mix_done", 2)
        mix_free = sems("mix_free", 2)
        u_ready = sem("u_ready")
        gated = sem("gated")
        out_done = sem("out_done")
        x_mixed = sem("x_mixed")
        route_exp_in = sem("route_exp_in")
        route_exp = sem("route_exp")
        moe = []
        for l in range(2):
            moe.append({k: sem(f"moe{l}_{k}") for k in (
                "router_loaded", "logits", "lists_in", "lists_out", "tables", "sel", "up", "silu", "hid", "gath", "xg", "hidT_tr", "hidT",
                "xT_tr", "xT", "down", "y_out", "y_stored", "y_complete", "combined", "step")})
            moe[l]["w13"] = sems(f"moe{l}_w13_", NBUF)
            moe[l]["w2"] = sems(f"moe{l}_w2_", NBUF)
            moe[l]["y_got"] = sems(f"moe{l}_y_got", NT)
        v_out = sem("v_out")
        g_done = sem("g_done")
        g_out = sem("g_out")
        sq_ready = sem("sq_ready")
        hss_ready = sem("hss_ready")
        hrms_ready = sem("hrms_ready")
        kn_ready = sem("kn_ready")
        kn_tr = sem("kn_tr")
        kn_out = sem("kn_out")
        f_done = sem("f_done")
        f_ready = sem("f_ready")
        f_ln = sem("f_ln")
        lf_ready = sem("lf_ready")
        cum_done = sem("cum_done")
        cum_ready = sem("cum_ready")
        cumT_done = sem("cumT_done")
        ncum_ready = sem("ncum_ready")
        ncum_stored = sem("ncum_stored")
        nck_loaded = sems("nck_loaded", 2)
        s_done = sem("s_done")
        s_max = sem("s_max")
        p_exp = sem("p_exp")
        p_ready = sem("p_ready")
        pt_tr = sem("pt_tr")
        pt_out = sems("pt_out", 2)
        o_done = sem("o_done")
        o_gated = sem("o_gated")
        x_attn = sem("x_attn")
        stored = sem("stored")

        def rows_pk(w, c0):
            return w.rearrange("(p k) n -> p k n", k=KD)[:, :, c0:c0 + COL]

        def rows_cp(w, c, c0):
            return w[c * KD * P:(c + 1) * KD * P, c0:c0 + COL].rearrange("(k p) n -> p k n", p=P)

        tiles = [rows_pk(a_w_in[0], WIDTH + COL * i) for i in range(4)]
        tiles += [rows_pk(a_w_in[0], COL * i) for i in range(4)]
        tiles += [rows_cp(a_w_out[0], c, COL * n) for n in range(2) for c in range(2)]
        tiles += [rows_pk(kv_w, COL * i) for i in range(4)]
        tiles += [rows_pk(b_w_qg[0], COL * i) for i in range(4)]
        tiles += [rows_cp(b_w_out[0], 0, COL * n) for n in range(2)]
        T_V, T_U, T_O, T_K, T_VV, T_Q, T_G, T_WO = 0, 4, 8, 12, 14, 16, 18, 20
        G_V, G_U, G_K, G_VV, G_Q, G_WO = 0, 16, 32, 40, 48, 56

        def split_no(i):
            return i if i < T_G else i - (T_WO - T_G)

        H_LO = {"a": 0, "kv": 2 * NT, "b": 4 * NT}
        H_BACK = 6 * NT
        TURN = {"a": 3, "kv": 3, "b": 2}

        def turn_bank(n, t, h):
            return ps[2 + 2 * (t % TURN[n]) + h]

        logit_bank = [ps[0], ps[4]]

        def slot(e):
            return (e + 1) % NBUF

        block = ctx.enter_context(nc.Block())

        @block.sync
        def _(sp):
            def load_tile(i):
                if i >= 2:
                    j = i - 2
                    if T_O <= j < T_K:
                        sp.wait_ge(out_done, 4 * (j - T_O + 1))
                    elif j >= T_G:
                        sp.wait_ge(g_done, 4 * (j - T_G + 1))
                    else:
                        groups = 4 * (j + 1 if j < T_O else j + 1 - (T_K - T_O))
                        sp.wait_ge(acc_ready, groups)
                sp.dma_start(ring[i % 2], tiles[i]).then_inc(tile_loaded[i % 2], 16)

            def load_expert(l, e, parts=(1, 3, 2)):
                m, s = moe[l], slot(e)
                for part in parts:
                    w, to = {1: (m_w1, w1_sb), 3: (m_w3, w3_sb), 2: (m_w2, w2_sb)}[part]
                    loaded = m["w2"][s] if part == 2 else m["w13"][s]
                    sp.dma_start(to[s], w[l, e].rearrange("(p k) n -> p k n", k=to[s].shape[1])).then_inc(loaded, 16)

            def load_later_expert(l, e, s, before, loads_before):
                m = moe[l]
                sp.wait_ge(m["w13"][before], 32 * loads_before)
                ended = sp.value_load(n0_i[0:1, bass.ds(e - (NBUF - 1), 1)], min_val=1, max_val=MAX_ITEMS)
                sp.wait_ge(m["up"], ended)
                w1e = m_w1[l][bass.ds(e, 1), :, :].rearrange("a (p k) n -> p (a k) n", k=KD)
                w3e = m_w3[l][bass.ds(e, 1), :, :].rearrange("a (p k) n -> p (a k) n", k=KD)
                w2e = m_w2[l][bass.ds(e, 1), :, :].rearrange("a (p k) n -> p (a k) n", k=KE)
                sp.dma_start(w1_sb[s], w1e).then_inc(m["w13"][s], 16)
                sp.wait_ge(m["w2"][before], 16 * loads_before)
                sp.dma_start(w3_sb[s], w3e).then_inc(m["w13"][s], 16)
                sp.wait_ge(m["down"], ended)
                sp.dma_start(w2_sb[s], w2e).then_inc(m["w2"][s], 16)

            def moe_loads(l):
                m = moe[l]
                load_expert(l, 0, (3, 2))
                load_expert(l, 1, (1, 3) if l == 0 else (3,))
                load_expert(l, 2, (3,))
                sp.wait_ge(m["tables"], 2)
                with sp.Fori(1, NE // NBUF) as r:
                    for s in range(NBUF):
                        load_later_expert(l, r * NBUF + s, slot(s), slot(s - 1), r + (1 if s else 0))
                for e in range(NE // NBUF * NBUF, NE):
                    load_later_expert(l, e, slot(e), slot(e - 1), (e - 1) // NBUF + 1)

            for t in range(NT):
                sp.dma_start(X[:, t, :], x_in[0, t * P:(t + 1) * P, :]).then_inc(x_loaded[t], 16)
            load_tile(0)
            load_tile(1)
            for i in range(2, T_K):
                load_tile(i)
                r = SLOTS + (i - 2) * T
                if r < Y_ROWS:
                    sp.dma_start(y_rows[r:r + T, :].rearrange("(p t) n -> p t n", t=NT), X[:, :, :])\
                        .then_inc(y_filled, 16)
            sp.wait_ge(out_done, 12)
            load_expert(0, 0, (1,))
            load_expert(0, 2, (1, 2))
            load_expert(0, 1, (2,))
            sp.wait_ge(out_done, 16)
            moe_loads(0)
            ended = sp.value_load(n0_i[0:1, NE - 1:NE], min_val=1, max_val=MAX_ITEMS)
            sp.wait_ge(moe[0]["up"], ended)
            for i in range(T_K, T_K + 2):
                sp.dma_start(ring[i % 2], tiles[i]).then_inc(tile_loaded[i % 2], 16)
            for i in range(T_K + 2, len(tiles)):
                load_tile(i)
            sp.wait_ge(o_done, PAIRS)
            load_expert(1, 1, (1, 2))
            load_expert(1, 2, (2,))
            sp.wait_ge(acc_ready, G_WO + 4)
            load_expert(1, 0, (1,))
            load_expert(1, 2, (1,))
            sp.wait_ge(acc_ready, G_WO + 8)
            moe_loads(1)
            for t in range(NT):
                sp.wait_ge(moe[1]["combined"], 2 * t + 2)
                sp.dma_start(out[0, t * P:(t + 1) * P, :], X[:, t, :]).then_inc(stored, 16)
            sp.wait_ge(stored, 16 * NT)

        @block.gpsimd
        def _(pool):
            g = nc.gpsimd
            made = [0]

            def make(ins):
                made[0] += 1
                ins.then_inc(const_made, 1)

            make(g.memset(ident[:, :], 0.0))
            make(g.memset(tri[:, :], 1.0))
            make(g.memset(tri_in[:, :], 1.0))
            make(g.memset(ones[:, :], 1.0))
            make(g.memset(ident_b[:, :], 0.0))
            make(g.memset(mask_b[:, :], 0.0))
            make(g.memset(eps[:, :], EPS))
            make(g.iota(iota_m[:, :], pattern=[[1, NE]], base=-64, channel_multiplier=0,
                        allow_small_or_imprecise_dtypes=True))
            make(g.iota(iota_c[:, :], pattern=[[1, CAP]], base=0, channel_multiplier=0,
                        allow_small_or_imprecise_dtypes=True))
            make(g.iota(item_slot[:, :], pattern=[[CAP, N_BASE]], base=0, channel_multiplier=0,
                        allow_small_or_imprecise_dtypes=True))
            make(g.iota(thr7[:, :], pattern=[[CAP, 8]], base=CAP, channel_multiplier=0,
                        allow_small_or_imprecise_dtypes=True))
            pool.wait_ge(const_made, made[0])
            for m in (ident, ident_b):
                g.affine_select(out=m[:, :], in_=m[:, :], compare_op=ALU.not_equal, fill=1.0, base=0,
                                pattern=[[-1, P]], channel_multiplier=1).then_inc(const_ready, 1)
            g.affine_select(out=tri[:, :], in_=tri[:, :], compare_op=ALU.is_ge, fill=0.0, base=-1,
                            pattern=[[1, P]], channel_multiplier=-1).then_inc(const_ready, 1)
            g.affine_select(out=tri_in[:, :], in_=tri_in[:, :], compare_op=ALU.is_ge, fill=0.0, base=0,
                            pattern=[[1, P]], channel_multiplier=-1).then_inc(const_ready, 1)
            g.affine_select(out=mask_b[:, :], in_=mask_b[:, :], compare_op=ALU.is_ge, fill=-BIG, base=0,
                            pattern=[[-1, P]], channel_multiplier=1).then_inc(const_ready, 1)

            def load_gain(n, src):
                pool.dma_start(gain[:, :], src.partition_broadcast(P)).then_inc(norm[n]["gain"], 16)

            def load_router(l):
                m = moe[l]
                pool.dma_start(wr[:, :, 0:NG], m_w_group[l].rearrange("(p k) n -> p k n", k=KD))\
                    .then_inc(m["router_loaded"], 16)
                pool.dma_start(wr[:, :, NG:NR], m_w_expert[l].rearrange("(p k) n -> p k n", k=KD))\
                    .then_inc(m["router_loaded"], 16)
                pool.dma_start(br[:, 0:NG], m_b_group[l].partition_broadcast(P)).then_inc(m["router_loaded"], 16)
                pool.dma_start(br[:, NG:NR], m_b_expert[l].partition_broadcast(P)).then_inc(m["router_loaded"], 16)

            def gather_outputs(l):
                m = moe[l]
                pool.wait_ge(m["y_complete"], 1)
                for t in range(NT):
                    for k in range(2):
                        g.indirect_dma_start(
                            out=y_got[:, 2 * t + k, :], out_offset=None, in_=y_rows[:, :],
                            in_offset=bass.IndirectOffsetOnAxis(ap=pos_i[:, 4 * k + t:4 * k + t + 1], axis=0),
                        ).then_inc(m["y_got"][t], 16)

            pool.dma_start(ws_raw, a_w_s[0].rearrange("g t s -> t g s")).then_inc(small_loaded, 16)
            pool.dma_start(spare[:, 2 * D:3 * D], a_b_s[0].rearrange("g t -> (g t)").partition_broadcast(P))\
                .then_inc(small_loaded, 16)
            for c, src in enumerate((a_b_in[0, 0:WIDTH], a_v_norm[0])):
                pool.dma_start(cols_raw[c * NC:(c + 1) * NC, :], src.rearrange("(c p) -> c p", p=P))\
                    .then_inc(col_loaded, 16)
            for i, src in enumerate((k_norm, q_norm[0])):
                for h in range(2):
                    pool.dma_start(cols_raw[2 * NC + i:2 * NC + i + 1, h * DH:(h + 1) * DH],
                                   src.rearrange("(a p) -> a p", a=1)).then_inc(col_loaded, 16)
            pool.dma_start(wf[:, :, :], kv_w.rearrange("(p k) n -> p k n", k=KD)[:, :, 2 * D:2 * D + HEADS])\
                .then_inc(col_loaded, 16)
            pool.dma_start(bf_bc[:, :], kv_b_f.partition_broadcast(P)).then_inc(col_loaded, 16)
            for i in range(4):
                if i >= 2:
                    pool.wait_ge(z_ready, 4 * (i - 1) + 1)
                pool.dma_start(b_v[i % 2], a_b_in[0, WIDTH + COL * i:WIDTH + COL * (i + 1)].partition_broadcast(P))\
                    .then_inc(bv_loaded[i % 2], 16)
            load_router(0)
            pool.wait_ge(norm["a"]["hrow"], NT)
            load_gain("m0", m_norm[0])
            pool.wait_ge(norm["m0"]["hrow"], NT)
            load_gain("kv", kv_norm)
            pool.wait_ge(moe[0]["lists_in"], 1)
            load_router(1)
            gather_outputs(0)
            pool.wait_ge(norm["kv"]["hrow"], NT)
            load_gain("b", b_norm[0])
            pool.wait_ge(norm["b"]["hrow"], NT)
            load_gain("m1", m_norm[1])

            gather_outputs(1)

        @block.scalar
        def _(act):
            a = nc.scalar
            done = [0]

            def then(ins):
                done[0] += 1
                ins.then_inc(act_step, 1)
                act.wait_ge(act_step, done[0])

            def block_stats(n, t, ready):
                act.wait_ge(*ready(t))
                then(a.activation(junk, X[:, t, :], ACT.Square, accum_out=ss[:, t:t + 1]))
                a.activation(rms[:, t:t + 1], ss[:, t:t + 1], ACT.Sqrt, bias=eps[:, :], scale=1.0 / D)\
                    .then_inc(norm[n]["rms"], 1)


            def transposed_rows(n, ready=None, before_last=None):
                if ready is not None:
                    block_stats(n, 0, ready)
                for t in range(NT):
                    if ready is not None and t + 1 < NT:
                        block_stats(n, t + 1, ready)
                    if before_last is not None and t == NT - 1:
                        before_last()
                    for h in range(2):
                        act.wait_ge(norm[n]["tr"], 2 * t + h + 1)
                        a.activation(hT_hi[:, 4 * h:4 * h + 4, t * P:(t + 1) * P],
                                     turn_bank(n, t, h)[:, :].rearrange("p (k n) -> p k n", k=4), ACT.Copy)\
                            .then_inc(norm[n]["ht"], 1)

            def split_hi(j, loads, q0=0, q1=4):
                act.wait_ge(tile_loaded[j], 16 * loads)
                for q in range(q0, q1):
                    a.activation(ring_hi[j][:, 2 * q:2 * q + 2, :], ring[j][:, 2 * q:2 * q + 2, :], ACT.Copy)\
                        .then_inc(w_hi, 1)

            def split_tile(i, q0=0, q1=4):
                split_hi(i % 2, i // 2 + 1, q0, q1)

            def moe_act(l, ready, before_end=None):
                m = moe[l]

                def router_rows(t):
                    if t >= 2:
                        act.wait_ge(m["logits"], t - 1)
                    for h in range(2):
                        act.wait_ge(norm[f"m{l}"]["tr"], 2 * t + h + 1)
                        a.activation(hTc[t % 2][:, 4 * h:4 * h + 4, :],
                                     ps[2 + h][:, :].rearrange("p (k n) -> p k n", k=4), ACT.Copy)\
                            .then_inc(norm[f"m{l}"]["ht"], 1)

                for t in range(NT):
                    block_stats(f"m{l}", t, ready)
                    if t >= 2:
                        router_rows(t - 2)
                router_rows(NT - 2)
                router_rows(NT - 1)
                act.wait_ge(route_exp_in, 2 * l + 1)
                a.activation(ohg, ohg, ACT.Exp).then_inc(route_exp, 1)
                act.wait_ge(route_exp_in, 2 * l + 2)
                a.activation(dexp, dexp, ACT.Exp).then_inc(route_exp, 1)
                act.wait_ge(m["tables"], 2)
                total = act.value_load(n0_i[0:1, NE:NE + 1], min_val=1, max_val=MAX_ITEMS)
                a.activation(junk[:, 0:1], eps[:, :], ACT.Copy).then_inc(m["y_out"], 1)
                a.activation(junk[:, 1:2], eps[:, :], ACT.Copy).then_inc(m["y_stored"], 17)

                def item_silu(n):
                    act.wait_ge(m["up"], n + 1)
                    a.activation(silu[CAP:P, :], ps[0][0:CAP, :], ACT.Silu).then_inc(m["silu"], 1)

                def item_output(n):
                    act.wait_ge(m["down"], n + 1)
                    for h in range(2):
                        a.activation(ysb[0:CAP, bass.ds((n & 1) * D + h * COL, COL)], ps[4][h * CAP:(h + 1) * CAP, :],
                                     ACT.Copy).then_inc(m["y_out"], 1)

                def store_before(n):
                    act.wait_ge(m["y_stored"], 16 * n + 1)
                    act.wait_ge(m["y_out"], 2 * n + 1)
                    act.dma_start(y_rows[bass.ds(n * CAP - CAP, CAP), :], ysb[0:CAP, bass.ds(((n + 1) & 1) * D, D)])\
                        .then_inc(m["y_stored"], 16)

                act.wait_ge(y_filled, 16 * ((Y_ROWS - SLOTS) // T))
                item_silu(0)
                item_output(0)
                with act.Fori(1, total) as n:
                    item_silu(n)
                    store_before(n)
                    item_output(n)
                store_before(total)
                if before_end is not None:
                    before_end()
                act.wait_ge(m["y_stored"], 16 * total + 17)
                a.activation(junk[:, 0:1], eps[:, :], ACT.Copy).then_inc(m["y_complete"], 1)

            act.dma_start(gain[:, :], a_norm[0].partition_broadcast(P)).then_inc(norm["a"]["gain"], 16)
            act.wait_ge(const_ready, 5)
            transposed_rows("a", lambda t: (x_loaded[t], 16), lambda: split_tile(0))
            with act.Fori(0, 2) as r:
                for j in range(2):
                    for t in range(NT):
                        act.wait_ge(z_ready, 8 * r + 4 * j + t + 2)
                        v_t = vg[:, t, bass.ds(r * 2 * COL + j * COL, COL)]
                        a.activation(v_t, v_t, ACT.Gelu_apprx_tanh).then_inc(v_ready, 1)
                        act.wait_ge(v_ready, 8 * r + 4 * j + t + 1)
                        a.activation(junk[:, 0:COL], v_t, ACT.Square,
                                     accum_out=vss[:, t, bass.ds(r * 2 + j, 1)]).then_inc(vr_ready, 1)
                        if t == 0:
                            split_hi(1 - j, r + 1 + j)
            act.wait_ge(wsts_ready, 1)
            then(a.activation(rms[:, :], ss[:, :], ACT.Sqrt, bias=eps[:, :], scale=1.0 / WIDTH))
            a.activation(junk[:, 0:1], rms[:, 0:1], ACT.Copy).then_inc(vr_ready, 1)
            act.wait_ge(wst_ready, 2)
            for c in range(NC):
                g = G_U + c
                act.wait_ge(acc_ready, g + 1)
                if c >= 4:
                    act.wait_ge(gated, c - 3)
                a.activation(u_tmp[c % 4], ps[g % 2][:, :], ACT.Gelu_apprx_tanh, bias=b_u[:, c:c + 1])\
                    .then_inc(u_ready, 1)
                if c % 4 == 1:
                    split_tile(T_U + c // 4 + 1)
            for i in range(T_O + 1, T_K):
                split_tile(i)
            moe_act(0, lambda t: (x_mixed, 4 + t + 1), before_end=lambda: split_tile(T_K))

            transposed_rows("kv", lambda t: (moe[0]["combined"], 2 * t + 2))

            def head_norms(r, g0, gain_col, dst, splits):
                for j in range(8):
                    g, q = g0 + j, 8 * r + j
                    act.wait_ge(acc_ready, g + 1)
                    if q >= 2:
                        act.wait_ge(hss_ready, q - 1)
                    a.activation(sq[q % 2], ps[g % 2][:, :], ACT.Square).then_inc(sq_ready, 1)
                    act.wait_ge(hss_ready, q + 1)
                    a.activation(hr[:, q % 2, :], hss[:, q % 2, :], ACT.Sqrt, bias=eps[:, :], scale=1.0 / DH)\
                        .then_inc(hrms_ready, 1)
                    if j >= 1:
                        put_heads(r, j - 1, gain_col, dst)
                    if j in splits:
                        split_tile(splits[j])
                put_heads(r, 7, gain_col, dst)

            def put_heads(r, j, gain_col, dst):
                q = 8 * r + j
                t, c = j % NT, 4 * (j // NT)
                act.wait_ge(kn_tr, q + 1)
                a.activation(dst[:, c:c + 4, t * P:(t + 1) * P],
                             ps[4 + q % 2][:, :].rearrange("p (c n) -> p c n", c=4), ACT.Copy,
                             scale=kq_gain[:, gain_col:gain_col + 1]).then_inc(kn_out, 1)

            head_norms(0, G_K, 0, KT, {0: T_K + 1, 5: T_VV})
            act.wait_ge(f_ready, 1)
            then(a.activation(lf[:, 1, :], lf[:, 0, :], ACT.Abs))
            then(a.activation(lf[:, 1, :], lf[:, 1, :], ACT.Exp, scale=-1.0))
            a.activation(lf[:, 1, :], lf[:, 1, :], ACT.Ln, bias=1.0).then_inc(f_ln, 1)
            split_tile(T_VV + 1)
            split_tile(T_Q)
            transposed_rows("b")
            act.wait_ge(cumT_done, 1)
            a.activation(junk[0:HEADS, 0:T], ps[6][0:HEADS, :], ACT.Copy, scale=-1.0).then_inc(ncum_ready, 1)
            act.wait_ge(ncum_ready, 1)
            act.dma_start(ncum_rows, junk[0:HEADS, 0:T]).then_inc(ncum_stored, 16)
            head_norms(1, G_Q, 1, QT, {1: T_Q + 1})
            def load_nck(c):
                for h in range(2):
                    act.dma_start(nck[:, c % 2, h, :], ncum_rows[2 * c + h].partition_broadcast(P))\
                        .then_inc(nck_loaded[c % 2], 16)

            act.wait_ge(ncum_stored, 16)
            act.wait_ge(kn_out, 16)
            load_nck(0)
            load_nck(1)
            for u in range(PAIRS * NT + 2):
                if u < PAIRS * NT:
                    w = (u % NT + 1) * P
                    for h in range(2):
                        act.wait_ge(s_max, 2 * u + h + 1)
                        a.activation(Pr[:, u % 3, h, 0:w], Pr[:, u % 3, h, 0:w], ACT.Exp, scale=-1.0,
                                     bias=nmx[:, u % 3, h:h + 1],
                                     accum_out=rsum[:, u % 3, h:h + 1]).then_inc(p_exp, 1)
                    if u % NT == NT - 1 and u // NT + 2 < PAIRS:
                        load_nck(u // NT + 2)
                if u < PAIRS * NT and u % NT == NT - 1:
                    c = u // NT
                    act.wait_ge(g_done, c + 1)
                    a.activation(GT[:, c, :], ps[7][:, :], ACT.Tanh, scale=0.5).then_inc(g_out, 1)
                q = u - (PAIRS // 2 * NT + 2)
                if 0 <= q < 4:
                    split_tile(T_WO, q, q + 1)
                if u >= 2:
                    v = u - 2
                    i = v % NT
                    act.wait_ge(pt_tr, 2 * v + 2)
                    a.activation(PT[:, 1, 0:i + 1, i * P:(i + 1) * P],
                                 ps[5][:, 0:(i + 1) * P].rearrange("p (b n) -> p b n", n=P), ACT.Copy)\
                        .then_inc(pt_out[1], 1)
            split_tile(T_WO + 1)
            moe_act(1, lambda t: (x_attn, 4 + t + 1))

        @block.vector
        def _(dve):
            v = nc.vector
            done = [0]

            def then(ins):
                done[0] += 1
                ins.then_inc(dve_step, 1)
                dve.wait_ge(dve_step, done[0])

            def scaled_rows(n, dst, stats=True, combine=None, after=None, blocks=range(NT)):
                m = norm[n]
                dve.wait_ge(m["gain"], 16)
                for t in blocks:
                    if combine is not None:
                        combine(t)
                    if stats:
                        dve.wait_ge(m["rms"], t + 1)
                        then(v.reciprocal(rinv[:, t:t + 1], rms[:, t:t + 1]))
                    if dst is hrow and t >= 2:
                        dve.wait_ge(m["tr"], 2 * t - 2)
                    to = hrow[t % 2] if dst is hrow else h_tok[:, t]
                    v.scalar_tensor_tensor(to, X[:, t, :].rearrange("p (q k) -> p k q", k=KD), rinv[:, t:t + 1],
                                           gain[:, :].rearrange("p (q k) -> p k q", k=KD), ALU.mult, ALU.mult)\
                        .then_inc(m["hrow"], 1)
                    if after is not None and t >= 1:
                        after(t - 1)

            def rows_lo(n, t):
                for h in range(2):
                    dve.wait_ge(norm[n]["ht"], 2 * t + h + 1)
                    v.tensor_tensor(hT_lo[:, 4 * h:4 * h + 4, t * P:(t + 1) * P],
                                    turn_bank(n, t, h)[:, :].rearrange("p (k n) -> p k n", k=4),
                                    hT_hi[:, 4 * h:4 * h + 4, t * P:(t + 1) * P].bitcast(F32), ALU.subtract).then_inc(h_lo, 1)

            def split_lo(j, number, q0=0, q1=4):
                for q in range(q0, q1):
                    dve.wait_ge(w_hi, 4 * number + q + 1)
                    v.tensor_tensor(ring_lo[j][:, 2 * q:2 * q + 2, :], ring[j][:, 2 * q:2 * q + 2, :],
                                    ring_hi[j][:, 2 * q:2 * q + 2, :].bitcast(F32), ALU.subtract).then_inc(w_lo, 1)

            def split_tile(i, q0=0, q1=4):
                split_lo(i % 2, split_no(i), q0, q1)

            def bc(ap, n):
                return ap.unsqueeze(2).to_broadcast([P, NT, n])

            def over_t(ap, n):
                return ap.unsqueeze(1).to_broadcast([P, NT, n])

            def first_of_max(vals, top, n, onehot):
                then(v.tensor_reduce(top, vals, AX, ALU.max))
                then(v.tensor_tensor(cand[:, :, 0:n], vals, bc(top, n), ALU.is_equal))
                then(v.tensor_tensor(cand[:, :, 0:n], cand[:, :, 0:n], over_t(iota_m[:, 0:n], n), ALU.mult))
                then(v.tensor_reduce(mmin, cand[:, :, 0:n], AX, ALU.min))
                then(v.tensor_tensor(onehot, over_t(iota_m[:, 0:n], n), bc(mmin, n), ALU.is_equal))

            def select(n, m, k, link):
                link(v.tensor_scalar(pb, pos[:, :], item_slot[:, bass.ds(n, 1)], None, ALU.subtract), 1)
                link(v.tensor_tensor(eqs.rearrange("p k c j -> p (k c) j"),
                                     pb.unsqueeze(2).to_broadcast([P, 8, CAP]),
                                     iota_c[:, :].unsqueeze(1).to_broadcast([P, 8, CAP]), ALU.is_equal), 2)
                v.tensor_tensor(S, eqs[:, 0], eqs[:, 1], ALU.add).then_inc(m["sel"], 1)

            def moe_dve(l):
                m = moe[l]
                dve.wait_ge(m["router_loaded"], 64)
                dve.wait_ge(m["logits"], NT)
                then(v.tensor_tensor(lg, logit_bank[l][:, 0:NT * NR].rearrange("p (t n) -> p t n", t=NT),
                                     over_t(br[:, :], NR), ALU.add))
                glog = lg[:, :, 0:NG]
                first_of_max(glog, gmax, NG, pen)
                then(v.tensor_scalar(pen, pen, BIG, -BIG, ALU.mult, ALU.add))
                v.tensor_tensor(ohg, glog, bc(gmax, NG), ALU.subtract).then_inc(route_exp_in, 1)
                then(v.tensor_tensor(el.rearrange("p t (g e) -> p t g e", g=NG),
                                     lg[:, :, NG:NR].rearrange("p t (g e) -> p t g e", g=NG),
                                     pen.unsqueeze(3).to_broadcast([P, NT, NG, EPG]), ALU.add))
                first_of_max(el, m1, NE, oh[0])
                then(v.scalar_tensor_tensor(el, oh[0], -2.0 * BIG, el, ALU.mult, ALU.add))
                first_of_max(el, m2, NE, oh[1])
                v.tensor_tensor(msum, oh[0], oh[1], ALU.add).then_inc(m["lists_in"], 1)
                v.tensor_tensor(dexp, m2, m1, ALU.subtract).then_inc(route_exp_in, 1)
                v.memset(hid[CAP:P, :], 0.0)
                dve.wait_ge(m["lists_out"], 1)
                then(v.tensor_copy(cn[0:NE, 0:1], ps[6][0:NE, 0:1]))
                then(v.tensor_tensor(cmp7[0:NE, 0:7], thr7[0:NE, 0:7], cn[0:NE, 0:1].to_broadcast([NE, 7]), ALU.is_lt))
                then(v.tensor_reduce(cn[0:NE, 1:2], cmp7[0:NE, 0:7], AX, ALU.add))
                then(v.tensor_scalar(cn[0:NE, 1:2], cn[0:NE, 1:2], 1.0, None, ALU.add))
                v.tensor_scalar(cntb[0:NE, :], ones[0:NE, :], cn[0:NE, 1:2], float(CAP), ALU.mult, ALU.mult)\
                    .then_inc(m["lists_in"], 1)
                dve.wait_ge(m["lists_out"], 2)
                v.tensor_copy(n0_i[0:1, 0:NE + 1], ps[6][0:1, 8:8 + NE + 1]).then_inc(m["tables"], 1)
                slots_at = ps[5][:, 0:NT * NE].unsqueeze(1).to_broadcast([P, 2, NT * NE])
                then(v.tensor_tensor(both.rearrange("p k t n -> p k (t n)"), both.rearrange("p k t n -> p k (t n)"),
                                     slots_at, ALU.mult))
                then(v.tensor_reduce(pos[:, :], both.rearrange("p k t n -> p (k t) n"), AX, ALU.add))
                v.tensor_copy(pos_i[:, :], pos[:, :]).then_inc(m["tables"], 1)
                dve.wait_ge(m["tables"], 2)
                total = dve.value_load(n0_i[0:1, NE:NE + 1], min_val=1, max_val=MAX_ITEMS)
                select(0, m, 0, lambda ins, k: then(ins))
                dve.wait_ge(m["gath"], 1)
                v.tensor_copy(xg, ps[1][:, :]).then_inc(m["xg"], 1)
                dve.wait_ge(m["xT_tr"], 1)
                v.tensor_copy(xT.rearrange("p (h j) c -> p j h c", h=2),
                              ps[3][:, :].rearrange("p (j h c) -> p j h c", j=4, h=2)).then_inc(m["xT"], 1)
                select(1, m, 0, lambda ins, k: then(ins))
                dve.wait_ge(route_exp, 2 * l + 2)
                then(v.tensor_reduce(gsum, ohg, AX, ALU.add))
                then(v.tensor_scalar(m1, dexp, 1.0, None, ALU.add))
                then(v.tensor_tensor(m1, m1, gsum, ALU.mult))
                then(v.reciprocal(w12[:, 0:4], m1))
                v.tensor_tensor(w12[:, 4:8], w12[:, 0:4], dexp, ALU.mult).then_inc(m["step"], 1)
                dve.wait_ge(m["step"], 1)
                with dve.Fori(0, total) as n:
                    dve.wait_ge(m["silu"], n + 1)
                    v.tensor_tensor(hid[0:CAP, :], silu[CAP:P, :], ps[0][CAP:P, :], ALU.mult).then_inc(m["hid"], 1)
                    dve.wait_ge(m["gath"], n + 2)
                    v.tensor_copy(xg, ps[1][:, :]).then_inc(m["xg"], 1)
                    dve.wait_ge(m["hidT_tr"], n + 1)
                    v.tensor_copy(hidT, ps[2][:, :].rearrange("p (k c) -> p k c", k=KE)[:, :, 0:CAP])\
                        .then_inc(m["hidT"], 1)
                    dve.wait_ge(m["xT_tr"], n + 2)
                    v.tensor_copy(xT.rearrange("p (h j) c -> p j h c", h=2),
                                  ps[3][:, :].rearrange("p (j h c) -> p j h c", j=4, h=2)).then_inc(m["xT"], 1)

                    def link(ins, k):
                        ins.then_inc(m["step"], 1)
                        dve.wait_ge(m["step"], 2 * n + k + 1)

                    select(n + 2, m, 0, link)

            def combine(l, t):
                m = moe[l]
                dve.wait_ge(m["y_got"][t], 32)
                for k in range(2):
                    v.scalar_tensor_tensor(X[:, t, :], y_got[:, 2 * t + k, :], w12[:, 4 * k + t:4 * k + t + 1],
                                           X[:, t, :], ALU.mult, ALU.add).then_inc(m["combined"], 1)
                    dve.wait_ge(m["combined"], 2 * t + k + 1)

            dve.wait_ge(const_ready, 5)
            v.memset(vss[:, :, :], 0.0).then_inc(z_ready, 1)
            scaled_rows("a", hrow, after=lambda t: rows_lo("a", t))
            split_tile(0)
            rows_lo("a", NT - 1)
            with dve.Fori(0, 2) as r:
                for j in range(2):
                    dve.wait_ge(bv_loaded[j], 16 * (r + 1))
                    for t in range(NT):
                        b = t % 2
                        dve.wait_ge(acc_ready, 8 * r + 4 * j + t + 1)
                        v.tensor_tensor(vg[:, t, bass.ds(r * 2 * COL + j * COL, COL)], ps[b][:, :], b_v[j], ALU.add)\
                            .then_inc(z_ready, 1)
                        if t == 1:
                            split_lo(1 - j, 2 * r + j + 1)
            dve.wait_ge(wst_done, 3)
            for h in range(2):
                then(v.tensor_copy(wsT[:, 4 * h:4 * h + 4, :], ps[4 + h][:, :].rearrange("p (g s) -> p g s", g=4)))
            v.memset(wsT[P // 2:P, :, 0:P // 2], 0.0).then_inc(wst_ready, 1)
            v.tensor_copy(cols[:, :], ps[6][:, 0:2 * NC + 2]).then_inc(wst_ready, 1)
            dve.wait_ge(vr_ready, 16)
            v.tensor_reduce(ss[:, :], vss[:, :, :], AX, ALU.add).then_inc(wsts_ready, 1)
            dve.wait_ge(vr_ready, 17)
            then(v.reciprocal(rinv[:, :], rms[:, :]))
            dve.wait_ge(wst_ready, 2)
            for t in range(NT):
                v.tensor_scalar(wsTs[:, t], wsT, rinv[:, t:t + 1], None, ALU.mult).then_inc(wsts_ready, 1)
            split_tile(T_U + 1)
            dve.wait_ge(small_loaded, 32)
            for c in range(NC):
                dve.wait_ge(mix_done[c % 2], c // 2 + 1)
                v.scalar_tensor_tensor(vg[:, :, c * P:(c + 1) * P], ps[4 + c % 2][:, :].rearrange("p (t n) -> p t n", t=NT),
                                       v_gain[:, c:c + 1], over_t(bs_bc[:, c // 2, :], P), ALU.mult, ALU.add)\
                    .then_inc(mix_free[c % 2], 1)
            for c in range(NC):
                dve.wait_ge(u_ready, c + 1)
                dve.wait_ge(mix_free[c % 2], c // 2 + 1)
                u3 = u_tmp[c % 4].rearrange("p (t n) -> p t n", t=NT)
                vg_c = vg[:, :, c * P:(c + 1) * P]
                then(v.tensor_tensor(u3, vg_c, u3, ALU.mult))
                hi = vg_hi[:, :, c * P:(c + 1) * P]
                then(v.tensor_copy(hi, u3))
                v.tensor_tensor(vg_lo[c // 8][:, :, c % 8 * P:(c % 8 + 1) * P], u3, hi.bitcast(F32), ALU.subtract)\
                    .then_inc(gated, 1)
                if c % 4 == 1 and c >= 4:
                    split_tile(T_U + c // 4 + 1)
            split_tile(T_O + 1)
            split_tile(T_O + 2)

            def add_mixed(n, t):
                if t < NT:
                    dve.wait_ge(out_done, 8 * n + 4 + t + 1)
                    v.tensor_tensor(X[:, t, n * COL:(n + 1) * COL], X[:, t, n * COL:(n + 1) * COL], ps[4 + t][:, :],
                                    ALU.add).then_inc(x_mixed, 1)

            dve.wait_ge(y_filled, 16 * ((Y_ROWS - SLOTS) // T))
            for t in range(NT):
                add_mixed(0, t)
            split_tile(T_O + 3)
            add_mixed(1, 0)
            scaled_rows("m0", h_tok, combine=lambda t: add_mixed(1, t + 1))
            moe_dve(0)

            split_tile(T_K)
            combine(0, 0)
            scaled_rows("kv", hrow, combine=lambda t: combine(0, t + 1) if t + 1 < NT else None,
                        after=lambda t: rows_lo("kv", t))
            rows_lo("kv", NT - 1)

            def head_norms(r, g0, splits):
                for j in range(8):
                    g, q = g0 + j, 8 * r + j
                    dve.wait_ge(sq_ready, q + 1)
                    v.tensor_reduce(hss[:, q % 2, :], sq[q % 2].rearrange("p (h d) -> p h d", h=8), AX, ALU.add)\
                        .then_inc(hss_ready, 1)
                    dve.wait_ge(hrms_ready, q + 1)
                    then(v.reciprocal(hr[:, q % 2, :], hr[:, q % 2, :]))
                    if q >= 2:
                        dve.wait_ge(kn_tr, q - 1)
                    v.tensor_tensor(kn[q % 2].rearrange("p (h d) -> p h d", h=8),
                                    ps[g % 2][:, :].rearrange("p (h d) -> p h d", h=8),
                                    hr[:, q % 2, :].unsqueeze(2).to_broadcast([P, 8, DH]), ALU.mult)\
                        .then_inc(kn_ready, 1)
                    if j in splits:
                        split_tile(splits[j])

            head_norms(0, G_K, {0: T_K + 1, 5: T_VV})
            dve.wait_ge(f_done, 1)
            f3 = lf[:, 0, :].rearrange("p (t n) -> p t n", t=NT)
            v.tensor_tensor(f3, ps[6][:, 0:NT * HEADS].rearrange("p (t n) -> p t n", t=NT),
                            over_t(bf_bc[:, :], HEADS), ALU.add).then_inc(f_ready, 1)
            dve.wait_ge(f_ready, 1)
            then(v.tensor_scalar(lf[:, 2, :], lf[:, 0, :], 0.0, None, ALU.min))
            for j in range(8):
                g = G_VV + j
                dve.wait_ge(acc_ready, g + 1)
                v.tensor_copy(V[:, j % NT, (j // NT) * COL:(j // NT + 1) * COL], ps[g % 2][:, :])\
                    .then_inc(v_out, 1)
                if j % 4 == 1:
                    split_tile(T_VV + j // 4 + 1)
                if j == 3:
                    dve.wait_ge(f_ln, 1)
                    v.tensor_tensor(lf[:, 0, :], lf[:, 2, :], lf[:, 1, :], ALU.subtract).then_inc(lf_ready, 1)
                if j == 6:
                    scaled_rows("b", hrow, stats=False, blocks=(0, 1))
            scaled_rows("b", hrow, stats=False, combine=lambda t: rows_lo("b", 0) if t == NT - 1 else None,
                        blocks=(2, 3))
            for t in range(1, NT):
                rows_lo("b", t)
            dve.wait_ge(cum_done, 1)
            v.tensor_copy(lf[:, 1, :], ps[7][:, 0:NT * HEADS]).then_inc(cum_ready, 1)
            then(v.tensor_scalar(kq_gain[:, 1:2], kq_gain[:, 1:2], DH ** -0.5, None, ALU.mult))
            head_norms(1, G_Q, {1: T_Q + 1})
            n_units = PAIRS * NT
            for u in range(n_units + 4):
                if u < n_units:
                    i, c = u % NT, u // NT
                    w = (i + 1) * P
                    if c == 0:
                        dve.wait_ge(acc_ready, G_Q + 8)
                        v.tensor_tensor(hT[:, 2 * i:2 * i + 2, :], hT_hi[:, 2 * i:2 * i + 2, :].bitcast(F32),
                                        hT_lo[:, 2 * i:2 * i + 2, :].bitcast(F32), ALU.add).then_inc(h_lo, 1)
                    if i == 0:
                        dve.wait_ge(nck_loaded[c % 2], 32 * (c // 2 + 1))
                    for h in range(2):
                        dve.wait_ge(s_done, 2 * u + h + 1)
                        if u >= 3:
                            dve.wait_ge(pt_tr, 2 * (u - 3) + h + 1)
                        v.tensor_tensor_reduce(out=Pr[:, u % 3, h, 0:w], in0=ps[2 * (u % 2) + h][:, 0:w],
                                               in1=nck[:, c % 2, h, 0:w], scale=-1.0, scalar=BIG, op0=ALU.add,
                                               op1=ALU.min, accum_out=nmx[:, u % 3, h:h + 1]).then_inc(s_max, 1)
                q = u - (PAIRS // 2 * NT + 3)
                if 0 <= q < 4:
                    split_tile(T_WO, q, q + 1)
                if 1 <= u <= n_units:
                    q = u - 1
                    dve.wait_ge(p_exp, 2 * q + 2)
                    then(v.reciprocal(rrec[:, q % 3, :], rsum[:, q % 3, :]))
                    w = (q % NT + 1) * P
                    for h in range(2):
                        v.tensor_scalar(Pr[:, q % 3, h, 0:w], Pr[:, q % 3, h, 0:w], rrec[:, q % 3, h:h + 1], 0.5,
                                        ALU.mult, ALU.mult).then_inc(p_ready, 1)
                if 2 <= u <= n_units + 1:
                    q = u - 2
                    i = q % NT
                    dve.wait_ge(pt_tr, 2 * q + 1)
                    v.tensor_copy(PT[:, 0, 0:i + 1, i * P:(i + 1) * P],
                                  ps[4][:, 0:(i + 1) * P].rearrange("p (b n) -> p b n", n=P)).then_inc(pt_out[0], 1)
                if u >= 4 and (u - 4) % NT == NT - 1:
                    c = (u - 4) // NT
                    dve.wait_ge(o_done, c + 1)
                    dve.wait_ge(g_out, c + 1)
                    then(v.scalar_tensor_tensor(QT[:, c, :], GT[:, c, :], 1.0, ps[6][:, :], ALU.add, ALU.mult))
                    then(v.tensor_copy(GT_hi[:, c, :], QT[:, c, :]))
                    v.tensor_tensor(GT_lo[:, c, :], QT[:, c, :], GT_hi[:, c, :].bitcast(F32), ALU.subtract).then_inc(o_gated, 1)

            def add_attended(n, t):
                if t < NT:
                    g = G_WO + 4 * n + t
                    dve.wait_ge(acc_ready, g + 1)
                    v.tensor_tensor(X[:, t, n * COL:(n + 1) * COL], X[:, t, n * COL:(n + 1) * COL], ps[g % 2][:, :],
                                    ALU.add).then_inc(x_attn, 1)

            add_attended(0, 0)
            split_tile(T_WO + 1)
            for t in range(1, NT):
                add_attended(0, t)
            add_attended(1, 0)
            scaled_rows("m1", h_tok, combine=lambda t: add_attended(1, t + 1))
            moe_dve(1)
            for t in range(NT):
                combine(1, t)

        @block.tensor
        def _(pe):
            mm = nc.tensor.matmul

            def split_product(o, left, right, start, stop):
                mm(o, left[0], right[0], start=start, stop=False)
                mm(o, left[0], right[1], start=False, stop=False)
                return mm(o, left[1], right[0], start=False, stop=stop)

            def h_part(k, t=None):
                at_t = slice(0, T) if t is None else slice(t * P, (t + 1) * P)
                return hT_hi[:, k, at_t], hT_lo[:, k, at_t]

            def w_part(j, k, a=0, b=COL):
                return ring_hi[j][:, k, a:b], ring_lo[j][:, k, a:b]

            def wait_split(i, k, first_group):
                if first_group and k % 2 == 0:
                    pe.wait_ge(w_lo, 4 * split_no(i) + k // 2 + 1)

            def transpose_dense_rows(n, t):
                pe.wait_ge(norm[n]["hrow"], t + 1)
                for h in range(2):
                    if t >= TURN[n]:
                        pe.wait_ge(h_lo, H_LO[n] + 2 * (t - TURN[n]) + h + 1)
                    for j in range(4):
                        last = nc.tensor.transpose(turn_bank(n, t, h)[:, j * P:(j + 1) * P],
                                                   hrow[t % 2][:, 4 * h + j, :], ident[:, :])
                    last.then_inc(norm[n]["tr"], 1)

            def transpose_rows(n, t, rows):
                m = norm[n]
                pe.wait_ge(m["hrow"], t + 1)
                for h in range(2):
                    if t >= 1:
                        pe.wait_ge(m["ht"], 2 * (t - 1) + h + 1)
                    for j in range(4):
                        last = nc.tensor.transpose(ps[2 + h][:, j * P:(j + 1) * P], rows[:, 4 * h + j, :], ident[:, :])
                    last.then_inc(m["tr"], 1)

            def project(i, g0, bank_free):
                for t in range(NT):
                    g = g0 + t
                    bank_free(g)
                    for k in range(KD):
                        wait_split(i, k, t == 0)
                        last = split_product(ps[g % 2][:, :], h_part(k, t), w_part(i % 2, k), k == 0, k == KD - 1)
                    last.then_inc(acc_ready, 1)

            def project_transposed(i, g0, bank_free):
                for j in range(4):
                    g = g0 + j
                    bank_free(g)
                    for k in range(KD):
                        wait_split(i, k, j == 0)
                        last = split_product(ps[g % 2][:, :], w_part(i % 2, k, j * P, (j + 1) * P), h_part(k),
                                             k == 0, k == KD - 1)
                    last.then_inc(acc_ready, 1)

            def router_step(l, t):
                m = moe[l]

                def logits(t):
                    pe.wait_ge(norm[f"m{l}"]["ht"], 2 * t + 2)
                    for k in range(KD):
                        for h in range(2):
                            last = mm(logit_bank[l][h * HALF:(h + 1) * HALF, t * NR:(t + 1) * NR],
                                      hTc[t % 2][:, k, h * HALF:(h + 1) * HALF], wr[:, k, :],
                                      start=k == 0, stop=k == KD - 1)
                    last.then_inc(m["logits"], 1)

                if t >= 2:
                    if t == 2:
                        pe.wait_ge(m["router_loaded"], 64)
                    else:
                        logits(t - 3)
                    transpose_rows(f"m{l}", t - 2, h_tok[:, t - 2])
                if t == NT - 1:
                    for b in range(t - 1, NT):
                        logits(b - 1)
                        transpose_rows(f"m{l}", b, h_tok[:, b])
                    logits(t)

            def moe_pe(l):
                m = moe[l]
                pe.wait_ge(m["lists_in"], 1)
                for c in range(NT):
                    last = mm(ps[6][0:NE, 0:1], msum[:, c, :], ones[:, 0:1], start=c == 0, stop=c == NT - 1)
                last.then_inc(m["lists_out"], 1)
                ranks = ps[5][:, 0:NT * NE].rearrange("p (t n) -> p t n", t=NT)
                mm(ranks, tri[:, :], msum, start=True, stop=False)
                for b in range(NT - 1):
                    later = NT - 1 - b
                    mm(ranks[:, b + 1:NT, :], ones[:, :], msum[:, b, :].unsqueeze(1).to_broadcast([P, later, NE]),
                       start=False, stop=False)
                pe.wait_ge(m["lists_in"], 2)
                mm(ps[6][0:1, 8:8 + NE + 1], cn[0:NE, 1:2], tri[0:NE, 0:NE + 1], start=True, stop=True)
                mm(ranks, cntb[0:NE, :], tri[0:NE, 0:NE].unsqueeze(1).to_broadcast([NE, NT, NE]),
                   start=False, stop=True).then_inc(m["lists_out"], 1)

                def gather(n):
                    pe.wait_ge(m["sel"], n + 1)
                    for c in range(NT):
                        for h in range(2):
                            last = mm(ps[1][h * CAP:(h + 1) * CAP, :], S[:, c, :],
                                      H[:, c * D + h * COL:c * D + (h + 1) * COL], start=c == 0, stop=c == NT - 1)
                    last.then_inc(m["gath"], 1)

                def transpose_item(n):
                    pe.wait_ge(m["xg"], n + 1)
                    for j in range(4):
                        last = nc.tensor.transpose(ps[3][:, j * P:(j + 1) * P], xg[:, j * P:(j + 1) * P], ident[:, :])
                    last.then_inc(m["xT_tr"], 1)

                def expert(s, loads, r0, r1):
                    with pe.Fori(r0, r1) as n:
                        pe.wait_ge(m["w13"][s], 32 * loads)
                        pe.wait_ge(m["xT"], n + 1)
                        for k in range(KD):
                            for h, w in enumerate((w1_sb[s], w3_sb[s])):
                                last = mm(ps[0][h * CAP:(h + 1) * CAP, :], xT[:, k, :], w[:, k, :],
                                          start=k == 0, stop=k == KD - 1)
                        last.then_inc(m["up"], 1)
                        gather(n + 1)
                        pe.wait_ge(m["hid"], n + 1)
                        for k in range(KE):
                            last = nc.tensor.transpose(ps[2][:, k * P:(k + 1) * P], hid[:, k:DE:KE], ident[:, :])
                        last.then_inc(m["hidT_tr"], 1)
                        transpose_item(n + 1)
                        pe.wait_ge(m["hidT"], n + 1)
                        pe.wait_ge(m["w2"][s], 16 * loads)
                        pe.wait_ge(m["y_out"], 2 * n + 1)
                        for k in range(KE):
                            for h in range(2):
                                last = mm(ps[4][h * CAP:(h + 1) * CAP, :], hidT[:, k, :],
                                          w2_sb[s][:, k, h * COL:(h + 1) * COL], start=k == 0, stop=k == KE - 1)
                        last.then_inc(m["down"], 1)

                def items_of(e):
                    return (pe.value_load(n0_i[0:1, bass.ds(e, 1)], min_val=0, max_val=MAX_ITEMS - 1),
                            pe.value_load(n0_i[0:1, bass.ds(e + 1, 1)], min_val=1, max_val=MAX_ITEMS))

                pe.wait_ge(m["tables"], 2)
                gather(0)
                transpose_item(0)
                with pe.Fori(0, NE // NBUF) as r:
                    for s in range(NBUF):
                        expert(slot(s), r + 1, *items_of(r * NBUF + s))
                for e in range(NE // NBUF * NBUF, NE):
                    expert(slot(e), e // NBUF + 1, *items_of(e))

            pe.wait_ge(const_ready, 5)
            for t in range(NT):
                transpose_dense_rows("a", t)
            with pe.Fori(0, 2) as r:
                for j in range(2):
                    for t in range(NT):
                        b = t % 2
                        pe.wait_ge(h_lo, 2 * t + 2)
                        pe.wait_ge(z_ready, 8 * r + max(4 * j + t - 1, 0) + 1)
                        for k in range(KD):
                            if t == 0 and k % 2 == 0:
                                pe.wait_ge(w_lo, 8 * r + 4 * j + k // 2 + 1)
                            last = split_product(ps[b][:, :], h_part(k, t), w_part(j, k), k == 0, k == KD - 1)
                        last.then_inc(acc_ready, 1)
            pe.wait_ge(small_loaded, 32)
            for h in range(2):
                for j in range(4):
                    last = nc.tensor.transpose(ps[4 + h][:, j * P:(j + 1) * P], ws_raw[:, 4 * h + j, :], ident[:, :])
                last.then_inc(wst_done, 1)
            pe.wait_ge(col_loaded, 16 * 8)
            nc.tensor.transpose(ps[6][:, 0:2 * NC + 2], cols_raw[:, :], ident[0:2 * NC + 2, 0:2 * NC + 2])\
                .then_inc(wst_done, 1)
            def free_u(g):
                c = g - G_U
                pe.wait_ge(*((z_ready, 16 + c) if c < 2 else (u_ready, c - 1)))

            for i in range(4):
                project_transposed(T_U + i, G_U + 4 * i, free_u)
                if i == 0:
                    pe.wait_ge(wsts_ready, 5)
                    for c in range(NC):
                        pe.wait_ge(mix_free[c % 2], c // 2)
                        for t in range(NT):
                            last = mm(ps[4 + c % 2][:, t * P:(t + 1) * P], vg[:, t, c * P:(c + 1) * P],
                                      wsTs[:, t, c // 2, :], start=True, stop=True)
                        last.then_inc(mix_done[c % 2], 1)
            for n in range(2):
                for c in range(2):
                    i = T_O + 2 * n + c
                    pe.wait_ge(gated, 8 * (c + 1))
                    for t in range(NT):
                        if n == 1 and c == 0:
                            pe.wait_ge(x_mixed, t + 1)
                        for k in range(KD):
                            wait_split(i, k, t == 0)
                            kc = 8 * c + k
                            last = split_product(ps[4 + t][:, :], (vg_hi[:, t, kc * P:(kc + 1) * P],
                                                                   vg_lo[c][:, t, k * P:(k + 1) * P]),
                                                 w_part(i % 2, k), c == 0 and k == 0, c == 1 and k == KD - 1)
                        last.then_inc(out_done, 1)
                        if n == 1 and c == 1:
                            router_step(0, t)
            moe_pe(0)

            for t in range(NT - 1):
                transpose_dense_rows("kv", t)

            def turn_heads(q):
                pe.wait_ge(kn_ready, q + 1)
                if q >= 2:
                    pe.wait_ge(kn_out, q - 1)
                for c in range(4):
                    last = nc.tensor.transpose(ps[4 + q % 2][:, c * P:(c + 1) * P], kn[q % 2][:, c * P:(c + 1) * P],
                                               ident[:, :])
                last.then_inc(kn_tr, 1)

            def project_heads(n, i0, g0, r, bank_free):
                for i in range(2):
                    for t in range(NT):
                        g = g0 + 4 * i + t
                        bank_free(g)
                        if i == 0:
                            pe.wait_ge(h_lo, H_LO[n] + 2 * t + 2)
                        for k in range(KD):
                            wait_split(i0 + i, k, t == 0)
                            last = split_product(ps[g % 2][:, :], h_part(k, t), w_part((i0 + i) % 2, k),
                                                 k == 0, k == KD - 1)
                        last.then_inc(acc_ready, 1)
                        if n == "kv" and g == g0:
                            transpose_dense_rows(n, NT - 1)
                        if 4 * i + t >= 1:
                            turn_heads(8 * r + 4 * i + t - 1)

            def free_k(g):
                if g - G_K >= 2:
                    pe.wait_ge(kn_ready, g - G_K - 1)

            def free_vv(g):
                j = g - G_VV
                pe.wait_ge(*((kn_ready, 7 + j) if j < 2 else (v_out, j - 1)))

            def free_q(g):
                j = g - G_Q
                pe.wait_ge(*((v_out, 7 + j) if j < 2 else (kn_ready, 8 + j - 1)))

            project_heads("kv", T_K, G_K, 0, free_k)
            for t in range(NT):
                for k in range(KD):
                    for part, h in enumerate(h_part(k, t)):
                        for c in range(2):
                            last = mm(ps[6][c * HALF:(c + 1) * HALF, t * HEADS:(t + 1) * HEADS],
                                      h.bitcast(F32)[:, c * HALF:(c + 1) * HALF], wf[:, k, :],
                                      start=k == 0 and part == 0, stop=k == KD - 1 and part == 1)
            last.then_inc(f_done, 1)
            turn_heads(7)
            project(T_VV, G_VV, free_vv)
            project(T_VV + 1, G_VV + 4, free_vv)
            pe.wait_ge(kn_out, 8)
            for t in range(NT):
                transpose_dense_rows("b", t)
            pe.wait_ge(lf_ready, 1)
            for c in range(NT):
                o = ps[7][:, c * HEADS:(c + 1) * HEADS]
                for b in range(c):
                    mm(o, ones[:, :], lf[:, 0, b * HEADS:(b + 1) * HEADS], start=b == 0, stop=False)
                last = mm(o, tri_in[:, :], lf[:, 0, c * HEADS:(c + 1) * HEADS], start=c == 0, stop=True)
            last.then_inc(cum_done, 1)
            pe.wait_ge(cum_ready, 1)
            for c in range(NT):
                last = nc.tensor.transpose(ps[6][0:HEADS, c * P:(c + 1) * P], lf[:, 1, c * HEADS:(c + 1) * HEADS],
                                           ident[:, :])
            last.then_inc(cumT_done, 1)
            project_heads("b", T_Q, G_Q, 1, free_q)
            turn_heads(15)

            pe.wait_ge(kn_out, 16)
            n_units = PAIRS * NT
            for u in range(n_units + 3):
                if u < n_units:
                    i, c = u % NT, u // NT
                    w = (i + 1) * P
                    if u >= 2:
                        pe.wait_ge(s_max, 2 * (u - 2) + 2)
                    for h in range(2):
                        mm(ps[2 * (u % 2) + h][:, 0:w], QT[h * DH:(h + 1) * DH, c, i * P:(i + 1) * P],
                           KT[h * DH:(h + 1) * DH, c, 0:w], start=True, stop=False)
                    for h in range(2):
                        mm(ps[2 * (u % 2) + h][:, i * P:w], ident_b[:, :], mask_b[:, :], start=False, stop=True)\
                            .then_inc(s_done, 1)
                    j = T_G + c // 4
                    if i == 0:
                        pe.wait_ge(tile_loaded[j % 2], 16 * (j // 2 + 1))
                        if c >= 1:
                            pe.wait_ge(g_out, c)
                    if c == 0:
                        pe.wait_ge(h_lo, H_BACK + i + 1)
                    for k in range(2 * i, 2 * i + 2):
                        last = mm(ps[7][:, :], ring[j % 2][:, k, c % 4 * P:(c % 4 + 1) * P], hT[:, k, :],
                                  start=k == 0, stop=k == KD - 1)
                    if i == NT - 1:
                        last.then_inc(g_done, 1)
                if u >= 3 and (u - 3) % NT == NT - 1:
                    q, c = u - 3, (u - 3) // NT
                    pe.wait_ge(pt_out[0], q + 1)
                    pe.wait_ge(pt_out[1], q + 1)
                    if c >= 1:
                        pe.wait_ge(o_gated, c)
                    for b in range(NT):
                        for h in range(2):
                            last = mm(ps[6][h * DH:(h + 1) * DH, b * P:T],
                                      V[:, b, (2 * c + h) * DH:(2 * c + h + 1) * DH], PT[:, h, b, b * P:T],
                                      start=b == 0, stop=b == NT - 1)
                    last.then_inc(o_done, 1)
                if 2 <= u < n_units + 2:
                    q = u - 2
                    i, c = q % NT, q // NT
                    for h in range(2):
                        pe.wait_ge(p_ready, 2 * q + h + 1)
                        pe.wait_ge(pt_out[h], q)
                        for b in range(i + 1):
                            last = nc.tensor.transpose(ps[4 + h][:, b * P:(b + 1) * P],
                                                       Pr[:, q % 3, h, b * P:(b + 1) * P], ident[:, :])
                        last.then_inc(pt_tr, 1)
            pe.wait_ge(o_gated, PAIRS)
            for n in range(2):
                i = T_WO + n
                for t in range(NT):
                    g = G_WO + 4 * n + t
                    if 4 * n + t >= 2:
                        pe.wait_ge(x_attn, 4 * n + t - 1)
                    for c in range(PAIRS):
                        wait_split(i, c, t == 0)
                        last = split_product(ps[g % 2][:, :], (GT_hi[:, c, t * P:(t + 1) * P],
                                                               GT_lo[:, c, t * P:(t + 1) * P]),
                                             w_part(i % 2, c), c == 0, c == PAIRS - 1)
                    last.then_inc(acc_ready, 1)
                    if n == 1:
                        router_step(1, t)
            moe_pe(1)


_INS = ["x", "a_norm", "a_w_in", "a_b_in", "a_v_norm", "a_w_s", "a_b_s", "a_w_out", "kv_norm", "kv_w", "kv_b_f",
        "k_norm", "b_norm", "b_w_qg", "q_norm", "b_w_out", "m_norm", "m_w_group", "m_b_group", "m_w_expert",
        "m_b_expert", "m_w1", "m_w3", "m_w2"]


def kernel(**inputs):
    import numpy as np
    import concourse.bacc as bacc
    from concourse.bass_utils import run_bass_kernel_spmd

    nc = bacc.Bacc("TRN2", target_bir_lowering=False, num_devices=1)
    arrays, args = {}, []
    for name in _INS:
        a = np.ascontiguousarray(inputs[name])
        arrays[f"in_{name}"] = a
        args.append(nc.dram_tensor(f"in_{name}", a.shape, mybir.dt.from_np(a.dtype), kind="ExternalInput").ap())
    args.append(nc.dram_tensor("out_x", (1, T, D), F32, kind="ExternalOutput").ap())
    trunk(nc, *args)
    r = run_bass_kernel_spmd(nc, [arrays], core_ids=[0])
    return r.results[0]["out_x"]
```
